# Optimizing a Trainium2 kernel written in Bass

```python
import jax, jax.numpy as jnp
from jax import lax
import numpy as np

D_MODEL = 1024
BATCH = 1
SEQ = 2048
DEPTH = 1
DEC_BATCH = 1
DEC_SEQ = 32
PAST_LEN = 128

CHUNK = 64
POOL_WIDTH = D_MODEL // 2
POOL_GROUPS = 4
POOL_GROUP_DIM = POOL_WIDTH // POOL_GROUPS
POOL_WINDOWS = (2, 4, 8, 16)
POOL_HIST = max(POOL_WINDOWS) - 1
GMLP_WIDTH = D_MODEL // 2
GMLP_HEADS = 4
GMLP_HEAD_DIM = GMLP_WIDTH // GMLP_HEADS
GMLP_CHUNK = 128
N_BRANCH = 2
IN_COLS = POOL_WIDTH + 2 * GMLP_WIDTH + N_BRANCH * D_MODEL
N_GROUPS = 4
EXPERTS_PER_GROUP = 4
N_EXPERTS = N_GROUPS * EXPERTS_PER_GROUP
TOP_K = 2
D_EXPERT = D_MODEL // 2
DISPATCH_BLOCK = 256
EPS = 1e-6

kernel_name = "hybrid_pool_gmlp_hmoe_stream_step"

def rmsnorm(x, g):
    xf = x.astype(jnp.float32)
    y = xf * lax.rsqrt(jnp.mean(xf * xf, axis=-1, keepdims=True) + EPS) * g.astype(jnp.float32)
    return y.astype(x.dtype)

def pool_mixer(a, hist, pos0, w_pool, pool_scale):
    B, L, _ = a.shape
    ext = jnp.concatenate([hist, a], axis=1)
    cs = jnp.cumsum(ext.astype(jnp.float32), axis=1)
    cs = jnp.pad(cs, ((0, 0), (1, 0), (0, 0)))
    pos = pos0 + jnp.arange(L, dtype=jnp.int32)
    outs = []
    for k, w in enumerate(POOL_WINDOWS):
        sl = slice(k * POOL_GROUP_DIM, (k + 1) * POOL_GROUP_DIM)
        s = cs[:, POOL_HIST + 1:POOL_HIST + 1 + L, sl] - cs[:, POOL_HIST + 1 - w:POOL_HIST + 1 - w + L, sl]
        cnt = jnp.minimum(pos + 1, w).astype(jnp.float32)
        outs.append(s / cnt[None, :, None])
    pooled = jnp.concatenate(outs, axis=-1)
    d = (pooled - a.astype(jnp.float32)).astype(a.dtype).reshape(B, L, POOL_GROUPS, POOL_GROUP_DIM)
    m = jnp.einsum('blgc,gcd->blgd', d, w_pool).reshape(B, L, POOL_WIDTH) * pool_scale
    return m, ext[:, -POOL_HIST:]

def gmlp_mixer(u, v, g_v, w_spatial, b_spatial):
    B, L, _ = v.shape
    vn = rmsnorm(v, g_v)
    Lp = -(-L // GMLP_CHUNK) * GMLP_CHUNK
    vp = jnp.pad(vn, ((0, 0), (0, Lp - L), (0, 0)))
    vp = vp.reshape(B, Lp // GMLP_CHUNK, GMLP_CHUNK, GMLP_HEADS, GMLP_HEAD_DIM)
    mask = jnp.tril(jnp.ones((GMLP_CHUNK, GMLP_CHUNK), w_spatial.dtype))
    ws = w_spatial * mask
    s = jnp.einsum('hij,bcjhd->bcihd', ws, vp) + b_spatial.T[None, None, :, :, None]
    s = s.reshape(B, Lp, GMLP_WIDTH)[:, :L]
    return u * s, vn

def hier_moe(x2d, w_group, b_group, w_router, b_router, w_gate, w_up, w_down):
    T, D = x2d.shape
    xf = x2d.astype(jnp.float32)
    gl = xf @ w_group.astype(jnp.float32) + b_group.astype(jnp.float32)
    gp = jax.nn.softmax(gl, axis=-1)
    g = jnp.argmax(gl, axis=-1).astype(jnp.int32)
    p_g = jnp.take_along_axis(gp, g[:, None], axis=1)[:, 0]
    el = (xf @ w_router.astype(jnp.float32) + b_router.astype(jnp.float32)).reshape(T, N_GROUPS, EXPERTS_PER_GROUP)
    el_g = jnp.take_along_axis(el, g[:, None, None], axis=1)[:, 0]
    top_v, top_i = lax.top_k(el_g, TOP_K)
    gate = jax.nn.softmax(top_v, axis=-1) * p_g[:, None]
    eid = (g[:, None] * EXPERTS_PER_GROUP + top_i).reshape(-1).astype(jnp.int32)
    tok = jnp.repeat(jnp.arange(T, dtype=jnp.int32), TOP_K)
    wts = gate.reshape(-1)
    A = T * TOP_K
    order = jnp.argsort(eid)
    e_s, t_s, w_s = eid[order], tok[order], wts[order]
    counts = jnp.bincount(eid, length=N_EXPERTS).astype(jnp.int32)
    starts = jnp.cumsum(counts) - counts
    padded = (counts + DISPATCH_BLOCK - 1) // DISPATCH_BLOCK * DISPATCH_BLOCK
    pends = jnp.cumsum(padded)
    pstarts = pends - padded
    dest = pstarts[e_s] + jnp.arange(A, dtype=jnp.int32) - starts[e_s]
    NB = -(-A // DISPATCH_BLOCK) + N_EXPERTS
    slot_tok = jnp.zeros((NB * DISPATCH_BLOCK,), jnp.int32).at[dest].set(t_s)
    blk_e = jnp.minimum(jnp.searchsorted(pends, jnp.arange(NB, dtype=jnp.int32) * DISPATCH_BLOCK, side='right'),
                        N_EXPERTS - 1).astype(jnp.int32)
    xb = x2d[slot_tok].reshape(NB, DISPATCH_BLOCK, D)

    def expert_block(args):
        xb_i, e = args
        h = jax.nn.silu(xb_i @ w_gate[e]) * (xb_i @ w_up[e])
        return h @ w_down[e]

    yb = lax.map(expert_block, (xb, blk_e)).reshape(NB * DISPATCH_BLOCK, D)
    return jnp.zeros_like(x2d).at[t_s].add(yb[dest] * w_s[:, None].astype(x2d.dtype))

def trunk_layer(x, hist, pos0, g_mix, w_in, w_pool, pool_scale, g_v, w_spatial, b_spatial,
                w_up_pool, w_up_gmlp, w_out, g_ffn, w_group, b_group, w_router, b_router,
                w_gate, w_up, w_down):
    B, L, D = x.shape
    xn = rmsnorm(x, g_mix)
    z = xn @ w_in
    a, u, v, ga, gb = jnp.split(z, [POOL_WIDTH, POOL_WIDTH + GMLP_WIDTH, POOL_WIDTH + 2 * GMLP_WIDTH,
                                    POOL_WIDTH + 2 * GMLP_WIDTH + D_MODEL], axis=-1)
    pa, new_hist = pool_mixer(a, hist, pos0, w_pool, pool_scale)
    pb, vn = gmlp_mixer(u, v, g_v, w_spatial, b_spatial)
    merged = jax.nn.sigmoid(ga) * (pa @ w_up_pool) + jax.nn.sigmoid(gb) * (pb @ w_up_gmlp)
    h = x + merged @ w_out
    hn = rmsnorm(h, g_ffn).reshape(B * L, D)
    y = h + hier_moe(hn, w_group, b_group, w_router, b_router, w_gate, w_up, w_down).reshape(B, L, D)
    return y, new_hist, vn

def setup_inputs(seed: int = 0) -> dict:
    key = jax.random.key(seed)
    ks = jax.random.split(key, 24)
    f32 = jnp.float32
    nrm = lambda k, s, sc: jax.random.normal(k, s, f32) * sc
    return {
        "x_prompt": nrm(ks[0], (BATCH, SEQ, D_MODEL), 1.0),
        "x_sample": nrm(ks[1], (DEC_BATCH, DEC_SEQ, D_MODEL), 1.0),
        "state_pool": nrm(ks[2], (DEPTH, DEC_BATCH, POOL_HIST, POOL_WIDTH), 0.5),
        "g_mix": 1.0 + nrm(ks[3], (DEPTH, D_MODEL), 0.02),
        "w_in": nrm(ks[4], (DEPTH, D_MODEL, IN_COLS), D_MODEL ** -0.5),
        "w_pool": nrm(ks[5], (DEPTH, POOL_GROUPS, POOL_GROUP_DIM, POOL_GROUP_DIM), POOL_GROUP_DIM ** -0.5),
        "pool_scale": 1.0 + nrm(ks[6], (DEPTH, POOL_WIDTH), 0.1),
        "g_v": 1.0 + nrm(ks[7], (DEPTH, GMLP_WIDTH), 0.02),
        "w_spatial": nrm(ks[8], (DEPTH, GMLP_HEADS, GMLP_CHUNK, GMLP_CHUNK), GMLP_CHUNK ** -0.5),
        "b_spatial": 1.0 + nrm(ks[9], (DEPTH, GMLP_HEADS, GMLP_CHUNK), 0.1),
        "w_up_pool": nrm(ks[10], (DEPTH, POOL_WIDTH, D_MODEL), POOL_WIDTH ** -0.5),
        "w_up_gmlp": nrm(ks[11], (DEPTH, GMLP_WIDTH, D_MODEL), GMLP_WIDTH ** -0.5),
        "w_out": nrm(ks[12], (DEPTH, D_MODEL, D_MODEL), D_MODEL ** -0.5),
        "g_ffn": 1.0 + nrm(ks[13], (DEPTH, D_MODEL), 0.02),
        "w_group": nrm(ks[14], (DEPTH, D_MODEL, N_GROUPS), D_MODEL ** -0.5),
        "b_group": nrm(ks[15], (DEPTH, N_GROUPS), 0.01),
        "w_router": nrm(ks[16], (DEPTH, D_MODEL, N_EXPERTS), D_MODEL ** -0.5),
        "b_router": nrm(ks[17], (DEPTH, N_EXPERTS), 0.01),
        "w_gate": nrm(ks[18], (DEPTH, N_EXPERTS, D_MODEL, D_EXPERT), D_MODEL ** -0.5),
        "w_up": nrm(ks[19], (DEPTH, N_EXPERTS, D_MODEL, D_EXPERT), D_MODEL ** -0.5),
        "w_down": nrm(ks[20], (DEPTH, N_EXPERTS, D_EXPERT, D_MODEL), D_EXPERT ** -0.5),
        "g_final": 1.0 + nrm(ks[21], (D_MODEL,), 0.02),
    }

def reference(x_prompt, x_sample, state_pool, g_mix, w_in, w_pool, pool_scale, g_v, w_spatial,
              b_spatial, w_up_pool, w_up_gmlp, w_out, g_ffn, w_group, b_group, w_router, b_router,
              w_gate, w_up, w_down, g_final):
    hp, hs = x_prompt, x_sample
    pool_p, pool_s, gv_s = [], [], []
    for l in range(DEPTH):
        lw = (g_mix[l], w_in[l], w_pool[l], pool_scale[l], g_v[l], w_spatial[l], b_spatial[l],
              w_up_pool[l], w_up_gmlp[l], w_out[l], g_ffn[l], w_group[l], b_group[l],
              w_router[l], b_router[l], w_gate[l], w_up[l], w_down[l])
        zero_hist = jnp.zeros((hp.shape[0], POOL_HIST, POOL_WIDTH), hp.dtype)
        hp, hist_p, _ = trunk_layer(hp, zero_hist, 0, *lw)
        hs, hist_s, vn_s = trunk_layer(hs, state_pool[l], PAST_LEN, *lw)
        pool_p.append(hist_p)
        pool_s.append(hist_s)
        gv_s.append(vn_s)
    y_prompt = rmsnorm(hp, g_final)
    y_sample = rmsnorm(hs, g_final)
    new_pool_prompt = jnp.stack(pool_p, axis=0)
    new_pool_sample = jnp.stack(pool_s, axis=0)
    new_gmlp_v_sample = jnp.stack(gv_s, axis=0)
    return (y_prompt, y_sample, new_pool_prompt, new_pool_sample, new_gmlp_v_sample)


_drawn_inputs = setup_inputs


def setup_inputs(seed=0):
    import zlib

    import numpy as np

    out = dict(_drawn_inputs(seed))
    spreads = {}
    factors = {'g_v': 2.829, 'g_ffn': 2.739, 'b_group': 8.0, 'b_router': 6.377, 'g_final': 2.745}
    for name, (base, spread) in spreads.items():
        noise = np.random.default_rng([zlib.crc32(name.encode()), seed]).standard_normal(out[name].shape)
        drawn = base * np.exp(spread * noise) if base else spread * noise
        out[name] = __import__('jax').numpy.asarray(drawn.astype(out[name].dtype))
    for name, factor in factors.items():
        out[name] = (out[name] * factor).astype(out[name].dtype)
    return out
```

```python
from contextlib import ExitStack

import concourse.bass as bass
from concourse import mybir

F32 = mybir.dt.float32
F32R = mybir.dt.float32r
BF16 = mybir.dt.bfloat16
I32 = mybir.dt.int32
U32 = mybir.dt.uint32
ALU = mybir.AluOpType
ACT = mybir.ActivationFunctionType
AX = mybir.AxisListType.X

P = 128
D = 1024
KD = D // P
SEQ = 2048
SAMPLE = 32
HALF = 512
KH = HALF // P
IN_COLS = 3 * HALF + 2 * D
HIST = 15
GROUP = 512
TPG = GROUP // P
NPROMPT = SEQ // GROUP
NT = SEQ // P + 1
NG, EPG = 4, 4
NE = NG * EPG
BPE = (SEQ + SAMPLE + P - 1) // P
NSLOT = NE * BPE
MAXBLK = (2 * (SEQ + SAMPLE)) // P + NE + 1
EPS = 1e-6
NREC = 10
NEG = -3.0e38

NPAN = 22
PRE = 4
SPLITS = 20


def products(nc, out, pairs):
    n = len(pairs)
    last = None
    for i, ((lh, ll), (rh, rl)) in enumerate(pairs):
        nc.tensor.matmul(out, lh, rh, start=(i == 0), stop=False)
        nc.tensor.matmul(out, lh, rl, start=False, stop=False)
        last = nc.tensor.matmul(out, ll, rh, start=False, stop=(i == n - 1))
    return last


def bank_uses(nt, nt_next, first):
    seq = []
    if not first:
        seq += [("u", m) for m in range(4)]
        for i in range(4):
            seq += [("ga", 2 * i), ("ga", 2 * i + 1), ("gb", 2 * i), ("gb", 2 * i + 1)]
            seq += [("P", 2 * i), ("Q", 2 * i), ("P", 2 * i + 1), ("Q", 2 * i + 1)]
    seq += [("x", t, c) for t in range(nt_next) for c in range(2)]
    if not first:
        seq += [("hn", t, c) for t in range(nt) for c in range(2)]
    if nt_next:
        seq += [("a", 0), ("a", 1), ("a", 2), ("pm", 0), ("a", 3), ("pm", 1)]
        seq += [("sp", t) for t in range(nt_next)]
        seq += [("pm", 2), ("pm", 3)]
    return {key: i for i, key in enumerate(seq)}, len(seq)


PRO_USES, N_PRO = bank_uses(0, TPG, True)
MID_USES, N_MID = bank_uses(TPG, TPG, False)
LAST_P_USES, N_LAST_P = bank_uses(TPG, 1, False)
SAM_USES, N_SAM = bank_uses(1, 0, False)
assert N_PRO % 2 == N_MID % 2 == 0
N_USES = N_PRO + (NPROMPT - 1) * N_MID + N_LAST_P + N_SAM


def wait_apart(eng, s, value, passed):
    eng.wait_ge(s, value)
    eng.sem_inc(passed, 1)


class PhaseOne:

    def __init__(self, g):
        self.g = g
        static = isinstance(g, int)
        self.pro = static and g < 0
        self.nt = 0 if self.pro else (1 if static and g == NPROMPT else TPG)
        self.n = SAMPLE if static and g == NPROMPT else GROUP
        self.rows = SAMPLE if static and g == NPROMPT else P
        self.next = not (static and g == NPROMPT)
        self.nt2 = 0 if not self.next else (1 if static and g == NPROMPT - 1 else TPG)
        self.n2 = SAMPLE if static and g == NPROMPT - 1 else GROUP
        self.rows2 = SAMPLE if static and g == NPROMPT - 1 else P
        before_last = N_PRO + (NPROMPT - 1) * N_MID
        if self.pro:
            self.uses, self.start = PRO_USES, 0
        elif static and g == NPROMPT:
            self.uses, self.start = SAM_USES, before_last + N_LAST_P
        elif static and g == NPROMPT - 1:
            self.uses, self.start = LAST_P_USES, before_last
        else:
            self.uses, self.start = MID_USES, (N_PRO + g * N_MID if static else None)
        self.before = None if self.pro else (
            (LAST_P_USES, N_LAST_P) if static and g == NPROMPT else (MID_USES, N_MID))

    @property
    def prev(self):
        return None if isinstance(self.g, int) and self.g < 1 else PhaseOne(self.g - 1)

    def use(self, *key):
        return self._place(self.uses[key])

    def use_before(self, *key):
        table, n = self.before
        return self._place(table[key] - n)

    def _place(self, i):
        if self.start is None:
            return i % 2, self.g * (N_MID // 2) + (N_PRO + i) // 2
        return (self.start + i) % 2, (self.start + i) // 2

    def panel(self, i):
        if self.pro:
            return i % 2, i
        return i % 2, self.g * NPAN + PRE + i


def build(nc, x_prompt, x_sample, state_pool, g_mix, w_in, w_pool, pool_scale, g_v, w_spatial, b_spatial,
          w_up_pool, w_up_gmlp, w_out, g_ffn, w_group, b_group, w_router, b_router, w_gate, w_up, w_down,
          g_final, y_prompt, y_sample, new_pool_prompt, new_pool_sample, new_v):
    outer = ExitStack()

    def sem(name):
        return outer.enter_context(nc.semaphore(name))

    def tiles(stack):
        def sb(name, shape, dt=F32):
            return stack.enter_context(nc.sbuf_tensor(name, shape, dt))
        return sb

    h_dram = nc.dram_tensor("h_rows", [SEQ + SAMPLE, D], F32).ap()
    hn_dram = nc.dram_tensor("hn_rows", [SEQ + SAMPLE, D], F32).ap()
    slot_dram = nc.dram_tensor("slot_ids", [P * NSLOT, 1], I32).ap()
    y_dram = nc.dram_tensor("expert_rows", [(MAXBLK + 1) * P, D], F32).ap()

    with outer:
        keep = tiles(outer)
        ident = keep("ident", [P, P])
        records = keep("records", [P, NT, NREC])
        running = keep("running", [P, NE])
        iota16 = keep("iota16", [P, NE])
        blk_tab = keep("blk_tab", [P, 2 * NE], I32)
        gains = keep("gains", [P, 2, NT])
        rows_i = keep("rows_i", [P, 2, NT], I32)
        psum = [outer.enter_context(nc.psum_tensor(f"bank{b}", [P, 512], F32)) for b in range(8)]

        shared = dict(locals())
        phase_one(nc, shared)
        phase_three(nc, shared)
        phase_four(nc, shared)


def phase_one(nc, v):
    sem, psum, ident, records, running, iota16 = (v[k] for k in
                                                  ("sem", "psum", "ident", "records", "running", "iota16"))
    x_prompt, x_sample = v["x_prompt"], v["x_sample"]
    w_in, w_out = v["w_in"], v["w_out"]
    h_dram, hn_dram, slot_dram = v["h_dram"], v["hn_dram"], v["slot_dram"]
    bankA = [psum[5], psum[6]]
    bankR, bankC = psum[4], psum[7]
    bankV = psum[0:4]

    stack = ExitStack()
    with stack:
        sb = v["tiles"](stack)
        xT = [sb("xT_hi", [P, KD, GROUP], F32R), sb("xT_lo", [P, KD, GROUP], F32R)]
        mg = [sb("mg_hi", [P, KD, GROUP], F32R), sb("mg_lo", [P, KD, GROUP], F32R)]
        with ExitStack() as shared:
            s1 = v["tiles"](shared)
            pa = [s1("pa_hi", [P, KH, GROUP], F32R), s1("pa_lo", [P, KH, GROUP], F32R)]
            pb = [s1("pb_hi", [P, KH, GROUP], F32R), s1("pb_lo", [P, KH, GROUP], F32R)]
        h = sb("h", [P, TPG, D])
        hn = sb("hn", [P, 2, D])
        hnT = sb("hnT", [P, KD, P])
        sb("shared_tail", [P, 4 * KH * GROUP - TPG * D - 2 * D - KD * P])
        raw = [sb("raw0", [P, 8, 256]), sb("raw1", [P, 8, 256])]
        wh = [sb("wh0", [P, 8, 256], F32R), sb("wh1", [P, 8, 256], F32R)]
        wl = [sb("wl0", [P, 8, 256], F32R), sb("wl1", [P, 8, 256], F32R)]
        xb = sb("xb", [P, 2, D])
        S = sb("S", [P, 4, GROUP])
        vf = sb("vf", [P, HALF])
        vn = [m[:, 4:8, :] for m in mg]
        ext = sb("ext", [P, GROUP + 16])
        win = [sb("win0", [P, GROUP + 16]), sb("win1", [P, GROUP + 16])]
        dd = [m[:, 0:2, :] for m in mg]
        junk = sb("junk", [P, D], BF16)
        hist = [sb("hist_prompt", [P, 4, 16]), sb("hist_sample", [P, 4, 16])]
        state = vf[0:16, :]
        corr = sb("corr", [P, 4, 16])
        wp_raw = S[:, 0, :].rearrange("p (g d) -> p g d", g=4)
        wsp_raw = S[:, 1, :].rearrange("p (g d) -> p g d", g=4)
        wp = [sb("wp_hi", [P, 4, P], F32R), sb("wp_lo", [P, 4, P], F32R)]
        ws = [sb("ws_hi", [P, 4, P], F32R), sb("ws_lo", [P, 4, P], F32R)]
        bsp = sb("bsp", [P, 4, P])
        gv = sb("gv", [P, HALF])
        gmix = sb("gmix", [P, D])
        gffn = sb("gffn", [P, D])
        pscale = sb("pscale", [P, 4])
        wr = sb("wr", [P, KD, 20])
        br = sb("br", [P, 20])
        upper = sb("upper", [P, P])
        ones = sb("ones", [P, P])
        half_neg = sb("half_neg", [P, 1])
        ss = sb("ss", [P, 12])
        ms = sb("ms", [P, 12])
        rs = sb("rs", [P, 12])
        lg = sb("lg", [P, TPG, 24])
        best = sb("best", [P, TPG, 8])
        besti = sb("besti", [P, TPG, 8], U32)
        inside = sb("inside", [P, TPG, NG])
        el = sb("el", [P, TPG, NE])
        gidx = sb("gidx", [P, TPG])
        mask = sb("mask", [P, 2, TPG, NE])
        msum = sb("msum", [P, TPG, NE])
        rank = sb("rank", [P, TPG, NE])
        prod = sb("prod", [P, 2, TPG, NE])
        pen = sb("pen", [P, TPG, NG])
        rec = sb("rec", [P, TPG, NREC])
        ri = sb("ri", [P, 2, 2 * TPG], I32)
        dest_f = sb("dest_f", [P, 2, TPG])
        dest = sb("dest", [P, 2, TPG], I32)
        tok = sb("tok", [P, TPG], I32)
        tok_all = sb("tok_all", [P, NT], I32)
        zero_i = S[:, 2, 0:NSLOT].bitcast(I32)
        histT = xb[0:16, :, 0:HALF]
        low7 = sb("low7", [P, 2, TPG], I32)
        high7 = sb("high7", [P, 2, TPG], I32)

        const_in, const_tr, const_ok, setup, dve_setup = (sem(s) for s in (
            "const_in", "const_tr", "const_ok", "setup", "dve_setup"))
        passed_pool, passed_dve = sem("passed_pool"), sem("passed_dve")
        raw_in = [sem("raw_in0"), sem("raw_in1")]
        w_hi, w_lo, half_used = sem("w_hi"), sem("w_lo"), sem("half_used")
        a_full = [sem("a0_full"), sem("a1_full")]
        a_free = [sem("a0_free"), sem("a1_free")]
        x_in = [sem("x_in0"), sem("x_in1")]
        x_ss, x_ms, x_rs, x_scaled, xT_hi = (sem(s) for s in ("x_ss", "x_ms", "x_rs", "x_scaled", "xT_hi"))
        v_full, v_ss, v_ms, v_rs, vf_ok, vn_hi, vn_ok, v_out = (sem(s) for s in (
            "v_full", "v_ss", "v_ms", "v_rs", "vf_ok", "vn_hi", "vn_ok", "v_out"))
        d_ok, d_hi, d_lo, pa_hi = sem("d_ok"), sem("d_hi"), sem("d_lo"), sem("pa_hi")
        pb_hi, pb_ok = sem("pb_hi"), sem("pb_ok")
        mix_ok, mg_hi, mg_ok = sem("mix_ok"), sem("mg_hi"), sem("mg_ok")
        res_in, o_full, h_part, h_ss, h_ms, h_rs, hn_ok, h_out = (sem(s) for s in (
            "res_in", "o_full", "h_part", "h_ss", "h_ms", "h_rs", "hn_ok", "h_out"))
        hn_out = [sem("hn_out0"), sem("hn_out1")]
        lg_full, lg_ok, mask_ok, cum_full, dest_ok, scattered = (sem(s) for s in (
            "lg_full", "lg_ok", "mask_ok", "cum_full", "dest_ok", "scattered"))
        hist_full, hist_ok, hist_out = sem("hist_full"), sem("hist_ok"), sem("hist_out")

        def win_view(c0, k0, nk, width):
            return w_in[0, k0 * P:(k0 + nk) * P, c0:c0 + width].rearrange("(k p) n -> p k n", p=P)

        def panel_sources(i, pro):
            whole = lambda r: r[:, :, :]
            wide = lambda r: r[:, :, :].rearrange("p (k a) n -> p k (a n)", a=2)
            if pro:
                i += NPAN - PRE
            if i < 2:
                return [(whole, win_view(HALF + i * 256, 0, 8, 256))]
            if i < 14:
                j, kind = (i - 2) // 3, (i - 2) % 3
                if kind < 2:
                    return [(whole, win_view(3 * HALF + kind * D + j * 256, 0, 8, 256))]
                view = lambda w: w[0, :, j * 256:(j + 1) * 256].rearrange("(k p) n -> p k n", p=P)
                return [(lambda r: r[:, 0:4, :], view(v["w_up_pool"])),
                        (lambda r: r[:, 4:8, :], view(v["w_up_gmlp"]))]
            if i < 18:
                half, kh = (i - 14) // 2, (i - 14) % 2
                return [(wide, w_out[0, kh * 512:(kh + 1) * 512, half * 512:(half + 1) * 512]
                         .rearrange("(k p) n -> p k n", p=P))]
            if i < 20:
                return [(wide, win_view(2 * HALF, 4 * (i - 18), 4, 512))]
            return [(whole, win_view((i - 20) * 256, 0, 8, 256))]

        def part(w, q):
            return w[:, 2 * q:2 * q + 2, :]

        def x_rows(ph, t, nxt=True):
            g = ph.g + 1 if nxt else ph.g
            if isinstance(g, int) and g == NPROMPT:
                return x_sample[0, :, :]
            return x_prompt[0, bass.ds(g * GROUP + t * P, P), :]

        def passes(eng, body):
            body(PhaseOne(-1))
            body(PhaseOne(0))
            with eng.Fori(1, NPROMPT - 1) as g:
                body(PhaseOne(g))
            body(PhaseOne(NPROMPT - 1))
            body(PhaseOne(NPROMPT))

        def wait(eng, s, value):
            if not (isinstance(value, int) and value <= 0):
                eng.wait_ge(s, value)

        def full(eng, ph, *key):
            b, q = ph.use(*key)
            eng.wait_ge(a_full[b], q + 1)
            return b

        def freed(eng, ph, *key):
            b, q = ph.use(*key)
            eng.wait_ge(a_free[b], q + 1)

        def panel_done(eng, ph, i):
            if ph.pro:
                i += 18
            if i < 0:
                b, q = ph.use_before("a", 5 + 2 * i)
            elif i < 2:
                b, q = ph.use("u", 2 * i + 1)
            elif i < 14:
                b, q = ph.use(("ga", "gb", "Q")[(i - 2) % 3], 2 * ((i - 2) // 3) + 1)
            elif i in (14, 16, 18):
                eng.wait_ge(half_used, 3 * ph.g + 2 + (i - 14) // 2)
                return
            elif i in (15, 17):
                eng.wait_ge(o_full, ph.g * 2 * TPG + (1 if i == 15 else 2) * ph.nt)
                return
            elif i == 19:
                eng.wait_ge(v_full, (ph.g + 1) * TPG + ph.nt2)
                return
            else:
                b, q = ph.use("a", 2 * (i - 20) + 1)
            eng.wait_ge(a_full[b], q + 1)

        block_stack = ExitStack()
        block = block_stack.enter_context(nc.Block())

        @block.sync
        def _(sp):
            consts = [
                (wp_raw, v["w_pool"][0].rearrange("g c d -> c g d")),
                (wsp_raw, v["w_spatial"][0].rearrange("h i j -> i h j")),
                (bsp[:, :, :].rearrange("p h i -> p (h i)"),
                 v["b_spatial"].rearrange("a h i -> a (h i)").broadcast_to([P, HALF])),
                (gv[:, :], v["g_v"].broadcast_to([P, HALF])),
                (gmix[:, :], v["g_mix"].broadcast_to([P, D])),
                (gffn[:, :], v["g_ffn"].broadcast_to([P, D])),
                (pscale[:, :], v["pool_scale"][0].rearrange("(k p) -> p k", p=P)),
                (wr[:, :, 0:4], v["w_group"][0].rearrange("(k p) n -> p k n", p=P)),
                (wr[:, :, 4:20], v["w_router"][0].rearrange("(k p) n -> p k n", p=P)),
                (br[:, 0:4], v["b_group"].broadcast_to([P, NG])),
                (br[:, 4:20], v["b_router"].broadcast_to([P, NE])),
            ]
            assert len(consts) == 11
            sp.wait_ge(setup, 1)
            sp.dma_start(state[1:16, :], v["state_pool"][0, 0, :, :]).then_inc(const_in, 16)
            with nc.allow_non_contiguous_dma(reason="short columns of constants"):
                for dst, src in consts:
                    sp.dma_start(dst, src).then_inc(const_in, 16)

            def load_panel(ph, i):
                par, n = ph.panel(i)
                if not (ph.pro and i < 2):
                    sp.wait_ge(w_lo, n - 1)
                for view, src in panel_sources(i, ph.pro):
                    sp.dma_start(view(raw[par]), src).then_inc(raw_in[par], 16)

            def store_h(ph, tiles):
                for t in tiles:
                    sp.wait_ge(hn_ok, ph.g * TPG + t + 1)
                    rows = bass.ds(ph.g * GROUP + t * P, ph.rows)
                    sp.dma_start(h_dram[rows, :], h[0:ph.rows, t, :]).then_inc(h_out, 16)
                    sp.dma_start(hn_dram[rows, :], hn[0:ph.rows, t % 2, :]).then_inc(hn_out[t % 2], 16)

            def body(ph):
                count = PRE if ph.pro else (NPAN if ph.next else NPAN - PRE)
                for i in range(count):
                    load_panel(ph, i)
                    if not ph.pro and i == 15:
                        panel_done(sp, ph, 13)
                        for t in range(ph.nt):
                            sp.dma_start(h[0:ph.rows, t, :], x_rows(ph, t, False)).then_inc(res_in, 16)
                    if not ph.pro and i == 19:
                        store_h(ph, range(0, ph.nt - 2))
                    if not ph.pro and i == 20:
                        store_h(ph, range(ph.nt - 2, ph.nt))
                if not ph.next:
                    store_h(ph, range(ph.nt))
                if isinstance(ph.g, int) and ph.g == NPROMPT - 1:
                    sp.wait_ge(vf_ok, NT)
                    sp.dma_start(v["new_v"][0, 0, :, :], vf[0:SAMPLE, :]).then_inc(v_out, 16)
            passes(sp, body)
            sp.wait_ge(v_out, 16)
            sp.wait_ge(h_out, 16 * NT)
            sp.wait_ge(hn_out[0], 16 + 16 * (2 * NPROMPT + 1))
            sp.wait_ge(hn_out[1], 16 + 16 * 2 * NPROMPT)
            for c, out in ((0, v["new_pool_prompt"]), (1, v["new_pool_sample"])):
                sp.wait_ge(hist_ok, c + 1)
                sp.dma_start(out[0, 0, :, :], histT[1:16, c, :]).then_inc(hist_out, 16)
            sp.wait_ge(hist_out, 32)

        @block.gpsimd
        def _(pool):
            nc.gpsimd.memset(state, 0.0).then_inc(setup, 1)
            nc.gpsimd.memset(half_neg[:, :], -0.5).then_inc(setup, 1)
            nc.gpsimd.memset(ones[:, :], 1.0).then_inc(setup, 1)
            nc.gpsimd.memset(zero_i, 0).then_inc(setup, 1)
            nc.gpsimd.iota(iota16[:, :], pattern=[[1, NE]], base=0, channel_multiplier=0,
                           allow_small_or_imprecise_dtypes=True).then_inc(setup, 1)
            nc.gpsimd.iota(tok_all[:, :], pattern=[[P, NT]], base=0, channel_multiplier=1).then_inc(setup, 1)
            nc.gpsimd.memset(lg[:, :, 4:8], NEG).then_inc(hn_out[0], 16)
            nc.gpsimd.memset(records[:, :, :], 0.0).then_inc(hn_out[1], 16)
            nc.gpsimd.memset(running[:, :], 0.0).then_inc(setup, 1)
            pool.wait_ge(setup, 7)
            nc.gpsimd.affine_select(out=ident[:, :], in_=ones[:, :], compare_op=ALU.is_equal, fill=0.0, base=0,
                                    pattern=[[-1, P]], channel_multiplier=1).then_inc(setup, 1)
            nc.gpsimd.affine_select(out=upper[:, :], in_=ones[:, :], compare_op=ALU.is_gt, fill=0.0, base=0,
                                    pattern=[[1, P]], channel_multiplier=-1).then_inc(setup, 1)
            pool.wait_ge(const_in, 16 * 12)
            nc.gpsimd.affine_select(out=wsp_raw, in_=wsp_raw, compare_op=ALU.is_ge, fill=0.0, base=0,
                                    pattern=[[0, 4], [-1, P]], channel_multiplier=1).then_inc(setup, 1)
            pool.dma_start(slot_dram.rearrange("(p n) o -> p (n o)", p=P), zero_i).then_inc(scattered, 16)

            def rsqrt(ms_sem, value, rows, col, done):
                pool.wait_ge(ms_sem, value)
                nc.gpsimd.tensor_tensor(rs[0:rows, col:col + 1], ms[0:rows, col:col + 1], half_neg[0:rows, :],
                                        ALU.pow).then_inc(done, 1)

            def scatter(ph):
                pool.wait_ge(dest_ok, ph.g + 1)
                wait_apart(pool, scattered, 16 + 32 * TPG * ph.g, passed_pool)
                for t in range(ph.nt):
                    for c in range(2):
                        nc.gpsimd.indirect_dma_start(
                            out=slot_dram,
                            out_offset=bass.IndirectOffsetOnAxis(ap=dest[0:ph.rows, c, t:t + 1], axis=0),
                            in_=tok[0:ph.rows, t:t + 1], in_offset=None).then_inc(scattered, 16)

            def body(ph):
                first = (ph.g + 1) * TPG
                if ph.prev and not ph.next:
                    scatter(ph.prev)
                for t in range(ph.nt2):
                    if t >= 2 or not ph.pro:
                        pool.wait_ge(xT_hi, 2 * (first + t - 1))
                    pool.dma_start(xb[0:ph.rows2, t % 2, :], x_rows(ph, t)).then_inc(x_in[t % 2], 16)
                    if ph.prev and t == min(1, ph.nt2 - 1):
                        scatter(ph.prev)
                    if t:
                        rsqrt(x_ms, first + t, ph.rows2, (t - 1) % 2, x_rs)
                if ph.nt2:
                    rsqrt(x_ms, first + ph.nt2, ph.rows2, (ph.nt2 - 1) % 2, x_rs)
                for t in range(ph.nt):
                    rsqrt(h_ms, ph.g * TPG + t + 1, ph.rows, 8 + t, h_rs)
                for t in range(ph.nt2):
                    rsqrt(v_ms, first + t + 1, ph.rows2, 4 + t, v_rs)
                if not ph.next:
                    scatter(ph)
            passes(pool, body)
            pool.wait_ge(scattered, 16 + 32 * NT)

        @block.scalar
        def _(act):
            act.wait_ge(const_in, 16 * 12)
            act.wait_ge(setup, 10)
            nc.scalar.activation(wp[0][:, :, :], wp_raw, ACT.Copy).then_inc(const_ok, 1)
            act.wait_ge(const_tr, 1)
            nc.scalar.activation(ws[0][:, :, :], bankC[:, :].rearrange("p (h i) -> p h i", h=4),
                                 ACT.Copy).then_inc(const_ok, 1)

            def split(ph, i):
                par, n = ph.panel(i)
                loads = sum(len(panel_sources(q, ph.pro)) for q in range(par, i + 1, 2))
                act.wait_ge(raw_in[par], 16 * (loads if ph.pro else 2 + 13 * ph.g + loads))
                if not (ph.pro and i < 2):
                    panel_done(act, ph, i - 2)
                for q in range(4):
                    nc.scalar.activation(part(wh[par], q), part(raw[par], q), ACT.Copy).then_inc(w_hi, 1)

            def body(ph):
                n, n2, g = ph.n, ph.n2, ph.g
                first = (g + 1) * TPG
                o = 0 if ph.pro else 18
                if ph.pro:
                    split(ph, 0)
                else:
                    for i in range(2):
                        split(ph, i + 1)
                        for m in (2 * i, 2 * i + 1):
                            freed(act, ph, "u", m)
                            if m == 0:
                                act.wait_ge(hn_out[0], 32 * g + 16)
                                act.wait_ge(hn_out[1], 32 * g + 16)
                            nc.scalar.activation(pb[0][:, m, 0:n], win[m % 2][:, 0:n], ACT.Copy).then_inc(pb_hi, 1)
                    for i in range(4):
                        for kind, name in enumerate(("ga", "gb")):
                            split(ph, 3 + 3 * i + kind)
                            for c in range(2):
                                b = full(act, ph, name, 2 * i + c)
                                if kind == 0 and c == 0:
                                    if i:
                                        act.wait_ge(mg_ok, g * 8 + 2 * i)
                                    else:
                                        act.wait_ge(pb_ok, g * 4 + 4)
                                nc.scalar.activation(S[:, 2 * kind + c, 0:n], bankA[b][:, 0:n], ACT.Sigmoid)\
                                    .then_inc(a_free[b], 1)
                        split(ph, 5 + 3 * i)
                        for m in (2 * i, 2 * i + 1):
                            act.wait_ge(mix_ok, g * 8 + m + 1)
                            nc.scalar.activation(mg[0][:, m, 0:n], win[m % 2][:, 0:n], ACT.Copy).then_inc(mg_hi, 1)
                    split(ph, 15)
                for t in range(ph.nt2):
                    r = ph.rows2
                    act.wait_ge(x_in[t % 2], 16 * ((g + 1) * (TPG // 2) + t // 2 + 1))
                    nc.scalar.activation(junk[0:r, :], xb[0:r, t % 2, :], ACT.Square,
                                         accum_out=ss[0:r, t % 2:t % 2 + 1]).then_inc(x_ss, 1)
                    for c in range(2):
                        b = full(act, ph, "x", t, c)
                        nc.scalar.activation(xT[0][:, 4 * c:4 * c + 4, t * P:t * P + r],
                                             bankA[b][:, :].rearrange("p (k i) -> p k i", k=4)[:, :, 0:r],
                                             ACT.Copy).then_inc(xT_hi, 1)
                    if t == min(1, ph.nt2 - 1):
                        split(ph, 1 if ph.pro else 16)
                if not ph.pro:
                    if not ph.next:
                        split(ph, 16)
                    split(ph, 17)
                    if ph.next:
                        split(ph, 18)
                    for t in range(ph.nt):
                        act.wait_ge(h_part, g * 2 * TPG + ph.nt + t + 1)
                        if t:
                            act.wait_ge(h_ss, g * TPG + t)
                        nc.scalar.activation(junk[0:ph.rows, :], h[0:ph.rows, t, :], ACT.Square,
                                             accum_out=ss[0:ph.rows, 8 + t:9 + t]).then_inc(h_ss, 1)
                    if ph.next:
                        split(ph, 19)
                if ph.next:
                    split(ph, o + 2)
                for t in range(max(ph.nt, ph.nt2)):
                    r = ph.rows2
                    if t < ph.nt2:
                        act.wait_ge(v_full, first + t + 1)
                        nc.scalar.activation(junk[0:r, 0:HALF], bankV[t][0:r, :], ACT.Square,
                                             accum_out=ss[0:r, 4 + t:5 + t]).then_inc(v_ss, 1)
                    if t < ph.nt:
                        if t:
                            act.wait_ge(lg_full, TPG * g + t)
                        for c in range(2):
                            b = full(act, ph, "hn", t, c)
                            nc.scalar.activation(hnT[:, 4 * c:4 * c + 4, 0:ph.rows],
                                                 bankA[b][:, :].rearrange("p (k i) -> p k i", k=4)[:, :, 0:ph.rows],
                                                 ACT.Copy).then_inc(a_free[b], 1)
                    if t < ph.nt2:
                        act.wait_ge(vf_ok, first + t + 1)
                        nc.scalar.activation(vn[0][0:r, t, :], vf[0:r, :], ACT.Copy).then_inc(vn_hi, 1)
                if not ph.next:
                    return
                split(ph, o + 3)

                def d_high(m):
                    act.wait_ge(d_ok, (g + 1) * 4 + m + 1)
                    if m >= 2:
                        full(act, ph, "pm", m - 2)
                    nc.scalar.activation(dd[0][:, m % 2, 0:n2], win[(m + 1) % 2][:, 0:n2], ACT.Copy).then_inc(d_hi, 1)

                def pa_high(m):
                    b = full(act, ph, "pm", m)
                    if m == 0 and not ph.pro:
                        act.wait_ge(h_out, 16 * (TPG * g + ph.nt))
                    nc.scalar.activation(pa[0][:, m, 0:n2], bankA[b][:, 0:n2], ACT.Copy,
                                         scale=pscale[:, m:m + 1]).then_inc(pa_hi, 1)
                d_high(0)
                d_high(1)
                split(PhaseOne(g + 1), 0)
                d_high(2)
                pa_high(0)
                d_high(3)
                pa_high(1)
                pa_high(2)
                pa_high(3)
            passes(act, body)

        @block.vector
        def _(dve):
            tt, ts, stt = nc.vector.tensor_tensor, nc.vector.tensor_scalar, nc.vector.scalar_tensor_tensor
            lo = lambda out, x, hi: tt(out, x, hi.bitcast(F32), ALU.subtract)

            dve.wait_ge(setup, 10)
            for m in range(4):
                ts(corr[:, m, :], iota16[:, :], 1.0, float(2 << m), ALU.add, ALU.min)
            nc.vector.memset(hist[0][:, :, :], 0.0)
            dve.drain()
            nc.vector.reciprocal(corr[:, :, :], corr[:, :, :])
            dve.drain()
            for m in range(4):
                ts(corr[:, m, :], corr[:, m, :], float(2 << m), None, ALU.mult)
            dve.wait_ge(const_in, 16 * 12)
            dve.wait_ge(scattered, 16)
            dve.wait_ge(const_ok, 1)
            lo(wp[1][:, :, :], wp_raw, wp[0][:, :, :])
            dve.wait_ge(const_ok, 2)
            lo(ws[1][:, :, :], bankC[:, :].rearrange("p (h i) -> p h i", h=4), ws[0][:, :, :])
            nc.vector.tensor_copy(hist[1][:, :, :], bankA[0][:, 0:64].rearrange("p (g i) -> p g i", g=4))\
                .then_inc(dve_setup, 1)

            def split(ph, i):
                par, n = ph.panel(i)
                for q in range(4):
                    dve.wait_ge(w_hi, 4 * n + q + 1)
                    last = lo(part(wl[par], q), part(raw[par], q), part(wh[par], q))
                last.then_inc(w_lo, 1)

            def mean(ss_sem, value, rows, col, width, done):
                dve.wait_ge(ss_sem, value)
                ts(ms[0:rows, col:col + 1], ss[0:rows, col:col + 1], 1.0 / width, EPS, ALU.mult, ALU.add)\
                    .then_inc(done, 1)

            def rows_of_x(ph, t):
                r, num = ph.rows2, (ph.g + 1) * TPG + t
                mean(x_ss, num + 1, r, t % 2, D, x_ms)
                dve.wait_ge(x_rs, num + 1)
                stt(xb[0:r, t % 2, :], xb[0:r, t % 2, :], rs[0:r, t % 2:t % 2 + 1], gmix[0:r, :], ALU.mult, ALU.mult)\
                    .then_inc(x_scaled, 1)
                for c in range(2):
                    b = full(dve, ph, "x", t, c)
                    dve.wait_ge(xT_hi, 2 * num + c + 1)
                    lo(xT[1][:, 4 * c:4 * c + 4, t * P:t * P + r],
                       bankA[b][:, :].rearrange("p (k i) -> p k i", k=4)[:, :, 0:r],
                       xT[0][:, 4 * c:4 * c + 4, t * P:t * P + r]).then_inc(a_free[b], 1)

            def add_residual(ph, half):
                r = ph.rows
                for t in range(ph.nt):
                    dve.wait_ge(res_in, 16 * (ph.g * TPG + ph.nt))
                    dve.wait_ge(o_full, ph.g * 2 * TPG + half * ph.nt + t + 1)
                    part = h[0:r, t, half * HALF:(half + 1) * HALF]
                    tt(part, bankV[t][0:r, :], part, ALU.add).then_inc(h_part, 1)

            def norm_h(ph, t):
                r, num = ph.rows, ph.g * TPG + t
                mean(h_ss, num + 1, r, 8 + t, D, h_ms)
                dve.wait_ge(h_rs, num + 1)
                if t >= 2:
                    dve.wait_ge(hn_out[t % 2], 16 + 32 * ph.g + 16)
                    full(dve, ph, "hn", t - 2, 1)
                stt(hn[0:r, t % 2, :], h[0:r, t, :], rs[0:r, 8 + t:9 + t], gffn[0:r, :], ALU.mult, ALU.mult)\
                    .then_inc(hn_ok, 1)

            def norm_v(ph, t):
                r, num = ph.rows2, (ph.g + 1) * TPG + t
                mean(v_ss, num + 1, r, 4 + t, HALF, v_ms)
                dve.wait_ge(v_rs, num + 1)
                stt(vf[0:r, :], bankV[t][0:r, :], rs[0:r, 4 + t:5 + t], gv[0:r, :], ALU.mult, ALU.mult)\
                    .then_inc(vf_ok, 1)
                dve.wait_ge(vn_hi, num + 1)
                lo(vn[1][0:r, t, :], vf[0:r, :], vn[0][0:r, t, :]).then_inc(vn_ok, 1)

            def logits(ph, t):
                r = ph.rows
                dve.wait_ge(lg_full, ph.g * TPG + t + 1)
                tt(lg[0:r, t, 0:4], bankR[0:r, 0:4], br[0:r, 0:4], ALU.add)
                tt(lg[0:r, t, 8:24], bankR[0:r, 4:20], br[0:r, 4:20], ALU.add).then_inc(lg_ok, 1)

            def take_a(ph, m):
                hs = hist[1] if ph.n2 == SAMPLE else hist[0]
                b = full(dve, ph, "a", m)
                nc.vector.tensor_copy(ext[:, 0:16], hs[:, m, :])
                nc.vector.tensor_copy(ext[:, 16:16 + ph.n2], bankA[b][:, 0:ph.n2]).then_inc(a_free[b], 1)

            def pooled(ph, m):
                hs, n2 = (hist[1] if ph.n2 == SAMPLE else hist[0]), ph.n2
                end, src = n2 + 16, ext
                for level in range(m + 1):
                    s, dst = 1 << level, win[level % 2]
                    dve.drain()
                    tt(dst[:, 2 * s:end], src[:, 2 * s:end], src[:, s:end - s], ALU.add)
                    src = dst
                nc.vector.tensor_copy(hs[:, m, :], ext[:, n2:end])
                dve.drain()
                if ph.pro:
                    tt(src[:, 16:32], src[:, 16:32], corr[:, m, :], ALU.mult)
                    dve.drain()
                d = win[(m + 1) % 2][:, 0:n2]
                stt(d, src[:, 16:end], 1.0 / (2 << m), ext[:, 16:end], ALU.mult, ALU.subtract).then_inc(d_ok, 1)
                dve.wait_ge(d_hi, (ph.g + 1) * 4 + m + 1)
                lo(dd[1][:, m % 2, 0:n2], d, dd[0][:, m % 2, 0:n2]).then_inc(d_lo, 1)

            def pa_low(ph, m):
                b = full(dve, ph, "pm", m)
                dve.wait_ge(pa_hi, (ph.g + 1) * 4 + m + 1)
                stt(pa[1][:, m, 0:ph.n2], bankA[b][:, 0:ph.n2], pscale[:, m:m + 1], pa[0][:, m, 0:ph.n2].bitcast(F32),
                    ALU.mult, ALU.subtract).then_inc(a_free[b], 1)

            def spatial(ph, t):
                r = ph.rows2
                b = full(dve, ph, "sp", t)
                tt(S[:, :, t * P:t * P + r], bankA[b][:, :].rearrange("p (h i) -> p h i", h=4)[:, :, 0:r],
                   bsp[:, :, 0:r], ALU.add).then_inc(a_free[b], 1)

            def choose(ph):
                r, ts_ = ph.rows, range(ph.nt)
                dve.drain()
                for t in ts_:
                    nc.vector.max(best[0:r, t, :], lg[0:r, t, 0:8])
                dve.drain()
                for t in ts_:
                    nc.vector.max_index(besti[0:r, t, :], best[0:r, t, :], lg[0:r, t, 0:8])
                dve.drain()
                for t in ts_:
                    nc.vector.tensor_copy(gidx[0:r, t:t + 1], besti[0:r, t, 0:1])
                dve.drain()
                for t in ts_:
                    ts(inside[0:r, t, :], iota16[0:r, 0:NG], gidx[0:r, t:t + 1], None, ALU.is_equal)
                dve.drain()
                ts(pen[0:r, :, :], inside[0:r, :, :], -NEG, NEG, ALU.mult, ALU.add)
                for t in ts_:
                    wide = inside[0:r, t, :].unsqueeze(2).broadcast_to([r, NG, EPG])
                    tt(el[0:r, t, :].rearrange("p (a b) -> p a b", a=NG),
                       lg[0:r, t, 8:24].rearrange("p (a b) -> p a b", a=NG), wide, ALU.mult)
                dve.drain()
                for t in ts_:
                    wide = pen[0:r, t, :].unsqueeze(2).broadcast_to([r, NG, EPG])
                    part = el[0:r, t, :].rearrange("p (a b) -> p a b", a=NG)
                    tt(part, part, wide, ALU.add)
                dve.drain()
                for t in ts_:
                    nc.vector.max(best[0:r, t, :], el[0:r, t, :])
                dve.drain()
                for t in ts_:
                    nc.vector.max_index(besti[0:r, t, :], best[0:r, t, :], el[0:r, t, :])
                dve.drain()
                nt = ph.nt
                nc.vector.tensor_copy(rec[0:r, 0:nt, 0:2], best[0:r, 0:nt, 0:2])
                nc.vector.tensor_copy(rec[0:r, 0:nt, 2:4], besti[0:r, 0:nt, 0:2])
                nc.vector.tensor_copy(rec[0:r, 0:nt, 6:10], lg[0:r, 0:nt, 0:4])
                dve.drain()
                for t in ts_:
                    for c in range(2):
                        ts(mask[0:r, c, t, :], iota16[0:r, :], rec[0:r, t, 2 + c:3 + c], None, ALU.is_equal)
                dve.drain()
                tt(msum[0:r, 0:nt, :], mask[0:r, 0, 0:nt, :], mask[0:r, 1, 0:nt, :], ALU.add).then_inc(mask_ok, 1)

            def place(ph):
                r, nt, g = ph.rows, ph.nt, ph.g
                dve.wait_ge(cum_full, g + 1)
                for t in range(nt):
                    tt(rank[0:r, t, :], bankC[0:r, t * NE:(t + 1) * NE], running[0:r, :], ALU.add)
                    dve.drain()
                    tt(running[:, :], bankC[:, 64 + t * NE:64 + (t + 1) * NE], running[:, :], ALU.add)
                    dve.drain()
                for c in range(2):
                    tt(prod[0:r, c, 0:nt, :], mask[0:r, c, 0:nt, :], rank[0:r, 0:nt, :], ALU.mult)
                dve.drain()
                for c in range(2):
                    nc.vector.reduce_sum(dest_f[0:r, c, 0:nt], prod[0:r, c, 0:nt, :], axis=AX)
                dve.drain()
                nc.vector.tensor_copy(low7[0:r, :, 0:nt], dest_f[0:r, :, 0:nt])
                for c in range(2):
                    nc.vector.tensor_copy(rec[0:r, 0:nt, 4 + c], dest_f[0:r, c, 0:nt])
                dve.drain()
                ts(high7[0:r, :, 0:nt], low7[0:r, :, 0:nt], 7, None, ALU.logical_shift_right)
                dve.drain()
                ts(low7[0:r, :, 0:nt], low7[0:r, :, 0:nt], P - 1, None, ALU.bitwise_and)
                if isinstance(g, int):
                    nc.vector.tensor_copy(records[0:r, g * TPG:g * TPG + nt, :], rec[0:r, 0:nt, :])
                else:
                    nc.vector.tensor_copy(records[0:r, bass.ds(g * TPG, TPG), :], rec[0:r, :, :])
                dve.drain()
                stt(dest_f[0:r, :, 0:nt], low7[0:r, :, 0:nt], float(NSLOT), high7[0:r, :, 0:nt], ALU.mult, ALU.add)
                wait_apart(dve, scattered, 16 + 32 * TPG * g, passed_dve)
                dve.drain()
                which = slice(g * TPG, g * TPG + nt) if isinstance(g, int) else bass.ds(g * TPG, TPG)
                nc.vector.tensor_copy(tok[:, 0:nt], tok_all[:, which])
                for c in range(2):
                    last = stt(dest[0:r, c, 0:nt], rec[0:r, 0:nt, 2 + c], float(BPE), dest_f[0:r, c, 0:nt],
                               ALU.mult, ALU.add)
                last.then_inc(dest_ok, 1)

            def body(ph):
                g, n = ph.g, ph.n
                o = 0 if ph.pro else 18
                if ph.pro:
                    split(ph, 0)
                else:
                    for i in range(2):
                        split(ph, i + 1)
                        for m in (2 * i, 2 * i + 1):
                            b = full(dve, ph, "u", m)
                            t1 = win[m % 2][:, 0:n]
                            tt(t1, bankA[b][:, 0:n], S[:, m, 0:n], ALU.mult).then_inc(a_free[b], 1)
                            dve.wait_ge(pb_hi, g * 4 + m + 1)
                            lo(pb[1][:, m, 0:n], t1, pb[0][:, m, 0:n]).then_inc(pb_ok, 1)
                    for i in range(4):
                        split(ph, 3 + 3 * i)
                        split(ph, 4 + 3 * i)
                        split(ph, 5 + 3 * i)
                        if ph.prev and i == 1:
                            choose(ph.prev)
                        if ph.prev and i == 2:
                            place(ph.prev)
                        for c in range(2):
                            m = 2 * i + c
                            for kind, (gate, name) in enumerate((("ga", "P"), ("gb", "Q"))):
                                freed(dve, ph, gate, m)
                                b = full(dve, ph, name, m)
                                part = S[:, 2 * kind + c, 0:n]
                                tt(part, bankA[b][:, 0:n], part, ALU.mult).then_inc(a_free[b], 1)
                            dve.drain()
                            t1 = win[m % 2][:, 0:n]
                            tt(t1, S[:, c, 0:n], S[:, 2 + c, 0:n], ALU.add).then_inc(mix_ok, 1)
                            dve.wait_ge(mg_hi, g * 8 + m + 1)
                            lo(mg[1][:, m, 0:n], t1, mg[0][:, m, 0:n]).then_inc(mg_ok, 1)
                    split(ph, 15)
                for t in range(ph.nt2):
                    rows_of_x(ph, t)
                    if t == min(1, ph.nt2 - 1):
                        split(ph, 1 if ph.pro else 16)
                if not ph.pro:
                    if not ph.next:
                        split(ph, 16)
                    add_residual(ph, 0)
                    split(ph, 17)
                    if ph.next:
                        split(ph, 18)
                    add_residual(ph, 1)
                    for t in range(ph.nt):
                        if t == min(2, ph.nt) and ph.next:
                            split(ph, 19)
                        norm_h(ph, t)
                if ph.next:
                    split(ph, o + 2)
                for t in range(max(ph.nt, ph.nt2)):
                    if t < ph.nt2:
                        norm_v(ph, t)
                    if t < ph.nt and (t < ph.nt - 1 or not ph.next):
                        logits(ph, t)
                if not ph.next:
                    choose(ph)
                    place(ph)
                    return
                split(ph, o + 3)
                if ph.nt:
                    logits(ph, ph.nt - 1)
                take_a(ph, 0)
                pooled(ph, 0)
                take_a(ph, 1)
                pooled(ph, 1)
                split(PhaseOne(g + 1), 0)
                take_a(ph, 2)
                pooled(ph, 2)
                pa_low(ph, 0)
                take_a(ph, 3)
                pooled(ph, 3)
                pa_low(ph, 1)
                for t in range(ph.nt2):
                    spatial(ph, t)
                pa_low(ph, 2)
                pa_low(ph, 3)
            passes(dve, body)
            for c in range(2):
                dve.wait_ge(hist_full, c + 1)
                nc.vector.tensor_copy(histT[:, c, :], (bankA[0], bankA[1])[c][0:16, :]).then_inc(hist_ok, 1)

        @block.tensor
        def _(pe):
            pe.wait_ge(setup, 10)
            pe.wait_ge(const_in, 16 * 12)
            for m in range(4):
                nc.tensor.transpose(bankA[0][:, 16 * m:16 * m + 16], state[:, m * P:(m + 1) * P], ident[0:16, 0:16])
            for hd in range(4):
                last = nc.tensor.transpose(bankC[:, hd * P:(hd + 1) * P], wsp_raw[:, hd, :], ident[:, :])
            last.then_inc(const_tr, 1)
            pe.wait_ge(dve_setup, 1)

            def take(ph, *key):
                b, q = ph.use(*key)
                wait(pe, a_free[b], q)
                return b

            def rows_of_x(ph, t):
                r, num = ph.rows2, (ph.g + 1) * TPG + t
                pe.wait_ge(x_scaled, num + 1)
                for c in range(2):
                    b = take(ph, "x", t, c)
                    for k in range(4):
                        last = nc.tensor.transpose(bankA[b][:, k * P:k * P + r],
                                                   xb[0:r, t % 2, (4 * c + k) * P:(4 * c + k + 1) * P],
                                                   ident[0:r, 0:r])
                    last.then_inc(a_full[b], 1)

            def start_panel(ph, i):
                par, n = ph.panel(i)
                pe.wait_ge(w_lo, n + 1)
                return wh[par], wl[par]

            def chunk(ph, i, c, name, m, src, ks, n):
                wh_, wl_ = start_panel(ph, i)
                b = take(ph, name, m)
                cols = slice(c * P, (c + 1) * P)
                return products(nc, bankA[b][:, 0:n],
                                [((wh_[:, kw, cols], wl_[:, kw, cols]), (src[0][:, ka, 0:n], src[1][:, ka, 0:n]))
                                 for kw, ka in ks]).then_inc(a_full[b], 1)

            def token_major(ph, i, t, src, k0, rows, n_acc):
                wh_, wl_ = start_panel(ph, i)
                view = lambda w: w[:, :, :].rearrange("p (k a) n -> p k (a n)", a=2)
                cols = slice(t * P, t * P + rows)
                last = None
                for k in range(4):
                    ah, al = src[0][:, k0 + k, cols], src[1][:, k0 + k, cols]
                    wh4, wl4 = view(wh_)[:, k, :], view(wl_)[:, k, :]
                    out = bankV[t][0:rows, :]
                    nc.tensor.matmul(out, ah, wh4, start=(n_acc == 0 and k == 0), stop=False)
                    nc.tensor.matmul(out, ah, wl4, start=False, stop=False)
                    last = nc.tensor.matmul(out, al, wh4, start=False, stop=(n_acc == 1 and k == 3))
                return last

            def transpose_hn(ph, t):
                r = ph.rows
                pe.wait_ge(hn_ok, ph.g * TPG + t + 1)
                for c in range(2):
                    b = take(ph, "hn", t, c)
                    for k in range(4):
                        last = nc.tensor.transpose(bankA[b][:, k * P:k * P + r],
                                                   hn[0:r, t % 2, (4 * c + k) * P:(4 * c + k + 1) * P],
                                                   ident[0:r, 0:r])
                    last.then_inc(a_full[b], 1)

            def router(ph, t):
                r = ph.rows
                freed(pe, ph, "hn", t, 0)
                freed(pe, ph, "hn", t, 1)
                if t:
                    pe.wait_ge(lg_ok, ph.g * TPG + t)
                for k in range(KD):
                    last = nc.tensor.matmul(bankR[0:r, 0:20], hnT[:, k, 0:r], wr[:, k, :], start=(k == 0),
                                            stop=(k == KD - 1))
                last.then_inc(lg_full, 1)

            def count(ph):
                r, w = ph.rows, ph.nt * NE
                pe.wait_ge(mask_ok, ph.g + 1)
                flat = msum[0:r, 0:ph.nt, :].rearrange("p t e -> p (t e)")
                nc.tensor.matmul(bankC[0:r, 0:w], upper[0:r, 0:r], flat, start=True, stop=True)
                nc.tensor.matmul(bankC[:, 64:64 + w], ones[0:r, :], flat, start=True, stop=True).then_inc(cum_full, 1)

            def pool_products(ph, m):
                pe.wait_ge(d_lo, (ph.g + 1) * 4 + m + 1)
                b = take(ph, "pm", m)
                products(nc, bankA[b][:, 0:ph.n2],
                         [((wp[0][:, m, :], wp[1][:, m, :]), (dd[0][:, m % 2, 0:ph.n2], dd[1][:, m % 2, 0:ph.n2]))])\
                    .then_inc(a_full[b], 1)

            def spatial(ph, t):
                r = ph.rows2
                pe.wait_ge(vn_ok, (ph.g + 1) * TPG + t + 1)
                b = take(ph, "sp", t)
                for hd in range(4):
                    cols = slice(hd * P, (hd + 1) * P)
                    last = products(nc, bankA[b][:, hd * P:hd * P + r],
                                    [((vn[0][0:r, t, cols], vn[1][0:r, t, cols]),
                                      (ws[0][0:r, hd, 0:r], ws[1][0:r, hd, 0:r]))])
                last.then_inc(a_full[b], 1)

            def body(ph):
                g, n, n2 = ph.g, ph.n, ph.n2
                o = 0 if ph.pro else 18
                every = [(k, k) for k in range(KD)]
                if not ph.pro:
                    for i in range(2):
                        for c in range(2):
                            chunk(ph, i, c, "u", 2 * i + c, xT, every, n)
                    for i in range(4):
                        for kind, name in enumerate(("ga", "gb")):
                            for c in range(2):
                                chunk(ph, 2 + 3 * i + kind, c, name, 2 * i + c, xT, every, n)
                        pe.wait_ge(pb_ok, g * 4 + 4)
                        for c in range(2):
                            chunk(ph, 4 + 3 * i, c, "P", 2 * i + c, pa, [(k, k) for k in range(4)], n)
                            chunk(ph, 4 + 3 * i, c, "Q", 2 * i + c, pb, [(4 + k, k) for k in range(4)], n)
                        if ph.prev and i == 1:
                            count(ph.prev)
                    pe.wait_ge(mg_ok, g * 8 + 8)
                    pe.wait_ge(vn_ok, g * TPG + ph.nt)
                    for t in range(ph.nt):
                        last = token_major(ph, 14, t, mg, 0, ph.rows, 0)
                    last.then_inc(half_used, 1)
                    for t in range(max(ph.nt, ph.nt2)):
                        if t < ph.nt2:
                            rows_of_x(ph, t)
                        if t < ph.nt:
                            token_major(ph, 15, t, mg, 4, ph.rows, 1).then_inc(o_full, 1)
                    for t in range(ph.nt):
                        pe.wait_ge(h_part, g * 2 * TPG + t + 1)
                        last = token_major(ph, 16, t, mg, 0, ph.rows, 0)
                    last.then_inc(half_used, 1)
                    for t in range(ph.nt):
                        token_major(ph, 17, t, mg, 4, ph.rows, 1).then_inc(o_full, 1)
                else:
                    for t in range(ph.nt2):
                        rows_of_x(ph, t)
                if ph.next:
                    freed(pe, ph, "x", ph.nt2 - 1, 0)
                    freed(pe, ph, "x", ph.nt2 - 1, 1)
                    for t in range(ph.nt2):
                        if not ph.pro:
                            pe.wait_ge(h_part, g * 2 * TPG + TPG + t + 1)
                        last = token_major(ph, o, t, xT, 0, ph.rows2, 0)
                    last.then_inc(half_used, 1)
                for t in range(max(ph.nt, ph.nt2)):
                    if t < ph.nt2:
                        token_major(ph, o + 1, t, xT, 4, ph.rows2, 1).then_inc(v_full, 1)
                    if 0 < t < ph.nt:
                        router(ph, t - 1)
                    if t < ph.nt:
                        transpose_hn(ph, t)
                if not ph.next:
                    router(ph, 0)
                    count(ph)
                    return
                chunk(ph, o + 2, 0, "a", 0, xT, every, n2)
                if ph.nt:
                    router(ph, ph.nt - 1)
                chunk(ph, o + 2, 1, "a", 1, xT, every, n2)
                chunk(ph, o + 3, 0, "a", 2, xT, every, n2)
                pool_products(ph, 0)
                chunk(ph, o + 3, 1, "a", 3, xT, every, n2)
                pool_products(ph, 1)
                for t in range(ph.nt2):
                    spatial(ph, t)
                pool_products(ph, 2)
                pool_products(ph, 3)
            passes(pe, body)
            for c in range(2):
                pe.wait_ge(a_free[c], (N_USES + 1 - c) // 2)
                for m in range(4):
                    last = nc.tensor.transpose((bankA[0], bankA[1])[c][0:16, m * P:(m + 1) * P], hist[c][:, m, :],
                                               ident[:, :])
                last.then_inc(hist_full, 1)

        block_stack.close()


def phase_three(nc, v):
    sem, psum, ident, records, running, iota16 = (v[k] for k in
                                                  ("sem", "psum", "ident", "records", "running", "iota16"))
    blk_tab, gains, rows_i = v["blk_tab"], v["gains"], v["rows_i"]
    hn_dram, slot_dram, y_dram = v["hn_dram"], v["slot_dram"], v["y_dram"]
    bankG, bankU, bankY = psum[0], psum[1:3], psum[3:5]
    bankX, bankH = psum[5:7], [psum[7], psum[0]]

    stack = ExitStack()
    with stack:
        sb = v["tiles"](stack)
        raw_gu = sb("raw_gu", [P, 2 * KD, HALF])
        raw_d = sb("raw_d", [P, KH, D])
        gu = [sb("gu_hi", [P, 2 * KD, HALF], F32R), sb("gu_lo", [P, 2 * KD, HALF], F32R)]
        dn = [sb("dn_hi", [P, KH, D], F32R), sb("dn_lo", [P, KH, D], F32R)]
        x = sb("x_rows", [P, D])
        xT = [sb("ex_hi", [P, KD, P], F32R), sb("ex_lo", [P, KD, P], F32R)]
        sg = sb("sg", [P, HALF])
        hid = sb("hid", [P, HALF])
        hT = [sb("hT_hi", [P, KH, P], F32R), sb("hT_lo", [P, KH, P], F32R)]
        y = sb("y_rows", [P, D])
        blank = sb("blank", [P, D])
        slots = sb("slots", [P, NSLOT], I32)
        idx = sb("idx", [P, 1], I32)
        spare = sb("spare", [P, 2])
        blk_f = sb("blk_f", [P, NE])
        blk_i = sb("blk_i", [P, NE], I32)
        sums = [sb("sums0", [P, NE]), sb("sums1", [P, NE])]
        first_row = sb("first_row", [P, NE])
        top = sb("top", [P, NT])
        exps = sb("exps", [P, NT, NG + 1])
        parts = sb("parts", [P, 2, NT])
        onehot = sb("onehot", [P, 2, NT, NE])
        rows_f = sb("rows_f", [P, 2, NT])

        passed_pool, passed_act = sem("passed_pool3"), sem("passed_act")
        slots_in, tab_ok, exps_in, exps_ok = (sem(n) for n in ("slots_in", "tab_ok", "exps_in", "exps_ok"))
        gate_in, up_in, down_in = sem("gate_in"), sem("up_in"), sem("down_in")
        blank_ok, blanks_out = sem("blank_ok"), sem("blanks_out")
        e_hi, e_lo = sem("e_hi"), sem("e_lo")
        idx_ok, x_rows_in = sem("idx_ok"), sem("x_rows_in")
        x_tr = sem("x_tr")
        ex_hi, ex_lo = sem("ex_hi"), sem("ex_lo")
        g_done, u1_done, sg_ok, hid_ok = (sem(n) for n in ("g_done", "u1_done", "sg_ok", "hid_ok"))
        gu_done = sem("gu_done")
        th_done, hT_hi = sem("th_done"), sem("hT_hi")
        hT_lo = sem("hT_lo")
        y_done = sem("y_done")
        y_read = sem("y_read")
        y_out = sem("y_out")

        def experts(eng, per_expert, per_block, peel=False):
            with eng.Fori(0, NE) as e:
                lo = eng.value_load(blk_tab[0:1, bass.ds(e, 1)], min_val=0, max_val=MAXBLK - 1)
                hi = eng.value_load(blk_tab[0:1, bass.ds(e + NE, 1)], min_val=1, max_val=MAXBLK)
                per_expert(e, lo)
                if peel:
                    per_block(e, lo, lo, True)
                with eng.Fori(lo + 1 if peel else lo, hi) as j:
                    per_block(e, lo, j)

        with nc.Block() as block:

            @block.sync
            def _(sp):
                sp.dma_start(slots[:, :], slot_dram.rearrange("(p n) o -> p (n o)", p=P)).then_inc(slots_in, 16)

                def load(e, first):
                    which = slice(0, 1) if first else bass.ds(e, 1)
                    view = lambda w: w[0, which, :, :].rearrange("a (k p) f -> p (a k) f", p=P)
                    if not first:
                        sp.wait_ge(e_lo, SPLITS * e + (KD - SPLITS))
                    sp.dma_start(raw_gu[:, 0:KD, :], view(v["w_gate"])).then_inc(gate_in, 16)
                    if not first:
                        sp.wait_ge(e_lo, SPLITS * e + (2 * KD - SPLITS))
                    sp.dma_start(raw_gu[:, KD:2 * KD, :], view(v["w_up"])).then_inc(up_in, 16)
                    if not first:
                        sp.wait_ge(e_lo, SPLITS * e)
                    sp.dma_start(raw_d[:, :, :], view(v["w_down"])).then_inc(down_in, 16)
                load(0, True)
                sp.wait_ge(tab_ok, 1)
                sp.wait_ge(blank_ok, 2)
                total = sp.value_load(blk_tab[0:1, 2 * NE - 1:2 * NE], min_val=1, max_val=MAXBLK - 1)
                with sp.Fori(0, total + 1) as j:
                    sp.sem_inc(blanks_out, 16)
                with sp.Fori(total + 1, MAXBLK + 1) as j:
                    sp.dma_start(y_dram[bass.ds(j * P, P), :], blank[:, :]).then_inc(blanks_out, 16)
                with sp.Fori(1, NE) as e:
                    load(e, False)
                sp.wait_ge(blanks_out, 16 * (MAXBLK + 1))

            @block.gpsimd
            def _(pool):
                nc.gpsimd.memset(y[:, :], 0.0).then_inc(y_out, 16)
                nc.gpsimd.memset(spare[:, :], 0.0).then_inc(blank_ok, 1)
                nc.gpsimd.memset(idx[:, :], 0).then_inc(x_tr, 1)
                nc.gpsimd.memset(blank[:, :], 0.0).then_inc(blank_ok, 1)
                pool.wait_ge(slots_in, 16)
                pool.wait_ge(tab_ok, 1)

                def fetch(col, j):
                    wait_apart(pool, x_tr, j + 1, passed_pool)
                    nc.gpsimd.tensor_copy(idx[:, :], slots[:, col]).then_inc(idx_ok, 1)
                    wait_apart(pool, idx_ok, j + 1, passed_pool)
                    nc.gpsimd.indirect_dma_start(out=x[:, :], out_offset=None, in_=hn_dram,
                                                 in_offset=bass.IndirectOffsetOnAxis(ap=idx[:, 0:1], axis=0))\
                        .then_inc(x_rows_in, 16)

                def per_block(e, lo, j):
                    col = nc.s_assert_within(pool.snap(e * BPE + j - lo), 0, NSLOT - 1, 
                                              skip_runtime_bounds_check_because="an expert has at most BPE blocks")
                    fetch(bass.ds(col, 1), j)
                experts(pool, lambda e, lo: None, per_block)
                total = pool.value_load(blk_tab[0:1, 2 * NE - 1:2 * NE], min_val=1, max_val=MAXBLK)
                fetch(slice(0, 1), total)

            @block.scalar
            def _(act):
                act.wait_ge(blank_ok, 2)
                act.wait_ge(exps_in, 1)
                nc.scalar.activation(exps[:, :, :], exps[:, :, :], ACT.Exp).then_inc(exps_ok, 1)
                act.wait_ge(tab_ok, 1)

                def use_sigmoid_table(c):
                    nc.scalar.activation(spare[:, c:c + 1], spare[:, c:c + 1], ACT.Sigmoid)

                def rows_high(count, j2):
                    act.wait_ge(x_tr, count)
                    for c in range(2):
                        nc.scalar.activation(xT[0][:, 4 * c:4 * c + 4, :],
                                             bankX[c][:, :].rearrange("p (k i) -> p k i", k=4), ACT.Copy)\
                            .then_inc(ex_hi, 1)
                rows_high(2, None)

                def split(e, lo):
                    use_sigmoid_table(1)
                    act.wait_ge(gu_done, lo + 1)
                    act.wait_ge(gate_in, 16 * e + 16)
                    for k in range(2 * KD):
                        if k == KD:
                            act.wait_ge(up_in, 16 * e + 16)
                        nc.scalar.activation(gu[0][:, k, :], raw_gu[:, k, :], ACT.Copy).then_inc(e_hi, 1)

                def per_block(e, lo, j, first=False):
                    def down(k):
                        if not first:
                            return
                        if k == 0:
                            act.wait_ge(down_in, 16 * e + 16)
                        nc.scalar.activation(dn[0][:, k, :], raw_d[:, k, :], ACT.Copy).then_inc(e_hi, 1)

                    if not first:
                        use_sigmoid_table(0)
                    act.wait_ge(y_done, j + 1)
                    act.wait_ge(y_out, 16 * j + 16)
                    for c in range(2):
                        nc.scalar.activation(y[:, c * HALF:(c + 1) * HALF], bankY[c][:, :], ACT.Copy).then_inc(y_read, 1)
                    act.wait_ge(g_done, j + 1)
                    nc.scalar.activation(sg[:, :], bankG[:, :], ACT.Sigmoid).then_inc(sg_ok, 1)
                    down(0)
                    act.wait_ge(y_read, 2 * j + 2)
                    act.dma_start(y_dram[bass.ds(j * P, P), :], y[:, :]).then_inc(y_out, 16)
                    act.wait_ge(th_done, 2 * j + 1)
                    nc.scalar.activation(hT[0][:, 0:2, :], bankH[0][:, 0:2 * P].rearrange("p (k i) -> p k i", k=2),
                                         ACT.Copy).then_inc(hT_hi, 1)
                    down(1)
                    rows_high(j + 3, j)
                    down(2)
                    act.wait_ge(th_done, 2 * j + 2)
                    nc.scalar.activation(hT[0][:, 2:4, :], bankH[1][:, 0:2 * P].rearrange("p (k i) -> p k i", k=2),
                                         ACT.Copy).then_inc(hT_hi, 1)
                    down(3)
                experts(act, split, per_block, peel=True)
                total = act.value_load(blk_tab[0:1, 2 * NE - 1:2 * NE], min_val=1, max_val=MAXBLK)
                act.wait_ge(y_done, total + 1)
                act.wait_ge(y_out, 16 * total + 16)
                for c in range(2):
                    nc.scalar.activation(y[:, c * HALF:(c + 1) * HALF], bankY[c][:, :], ACT.Copy).then_inc(y_read, 1)
                act.wait_ge(y_read, 2 * total + 2)
                act.dma_start(y_dram[bass.ds(total * P, P), :], y[:, :]).then_inc(y_out, 16)
                wait_apart(act, y_out, 16 * total + 32, passed_act)

            @block.vector
            def _(dve):
                tt, ts, stt = nc.vector.tensor_tensor, nc.vector.tensor_scalar, nc.vector.scalar_tensor_tensor
                copy = nc.vector.tensor_copy
                lo_half = lambda out, a, hi: tt(out, a, hi.bitcast(F32), ALU.subtract)

                for b in bankY:
                    last = nc.vector.memset(b[:, :], 0.0)
                last.then_inc(y_done, 1)
                ts(blk_i[:, :], running[:, :], float(P - 1), None, ALU.add)
                dve.drain()
                ts(blk_i[:, :], blk_i[:, :], 7, None, ALU.logical_shift_right)
                dve.drain()
                ts(blk_f[:, :], blk_i[:, :], 1.0, None, ALU.max)
                dve.drain()
                src = blk_f
                for n, step in enumerate((1, 2, 4, 8)):
                    dst = sums[n % 2]
                    tt(dst[:, step:], src[:, step:], src[:, :NE - step], ALU.add)
                    copy(dst[:, :step], src[:, :step])
                    dve.drain()
                    src = dst
                copy(blk_tab[:, NE:2 * NE], src[:, :])
                tt(blk_f[:, :], src[:, :], blk_f[:, :], ALU.subtract)
                dve.drain()
                copy(blk_tab[:, 0:NE], blk_f[:, :]).then_inc(tab_ok, 1)
                ts(first_row[:, :], blk_f[:, :], 1.0, float(P), ALU.add, ALU.mult).then_inc(hT_lo, 1)
                nc.vector.reduce_max(top[:, :], records[:, :, 6:10], axis=AX)
                dve.drain()
                tt(exps[:, :, 0:NG], records[:, :, 6:10], top[:, :].unsqueeze(2).broadcast_to([P, NT, NG]), ALU.subtract)
                tt(exps[:, :, NG:NG + 1], records[:, :, 1:2], records[:, :, 0:1], ALU.subtract).then_inc(exps_in, 1)
                wide_iota = iota16[:, :].unsqueeze(1).broadcast_to([P, NT, NE])
                wide_row = first_row[:, :].unsqueeze(1).broadcast_to([P, NT, NE])
                for c in range(2):
                    tt(onehot[:, c, :, :], wide_iota, records[:, :, 2 + c:3 + c].broadcast_to([P, NT, NE]), ALU.is_equal)
                dve.drain()
                for c in range(2):
                    tt(onehot[:, c, :, :], onehot[:, c, :, :], wide_row, ALU.mult)
                dve.drain()
                for c in range(2):
                    nc.vector.reduce_sum(rows_f[:, c, :], onehot[:, c, :, :], axis=AX)
                dve.drain()
                for c in range(2):
                    tt(rows_i[:, c, :], rows_f[:, c, :], records[:, :, 4 + c:5 + c].rearrange("p t o -> p (t o)"), ALU.add)
                dve.wait_ge(exps_ok, 1)
                nc.vector.reduce_sum(parts[:, 0, :], exps[:, :, 0:NG], axis=AX)
                second = exps[:, :, NG:NG + 1].rearrange("p t o -> p (t o)")
                ts(parts[:, 1, :], second, 1.0, None, ALU.add)
                dve.drain()
                tt(parts[:, 0, :], parts[:, 0, :], parts[:, 1, :], ALU.mult)
                dve.drain()
                nc.vector.reciprocal(gains[:, 0, :], parts[:, 0, :])
                dve.drain()
                tt(gains[:, 1, :], gains[:, 0, :], second, ALU.mult).then_inc(gu_done, 1)

                def rows_low(count):
                    for c in range(2):
                        dve.wait_ge(ex_hi, count + c)
                        lo_half(xT[1][:, 4 * c:4 * c + 4, :], bankX[c][:, :].rearrange("p (k i) -> p k i", k=4),
                                xT[0][:, 4 * c:4 * c + 4, :]).then_inc(ex_lo, 1)
                rows_low(1)

                def split(e, lo):
                    for k in range(2 * KD):
                        dve.wait_ge(e_hi, SPLITS * e + k + 1)
                        lo_half(gu[1][:, k, :], raw_gu[:, k, :], gu[0][:, k, :]).then_inc(e_lo, 1)

                def hidden_low(c):
                    lo_half(hT[1][:, 2 * c:2 * c + 2, :], bankH[c][:, 0:2 * P].rearrange("p (k i) -> p k i", k=2),
                            hT[0][:, 2 * c:2 * c + 2, :]).then_inc(hT_lo, 1)

                def per_block(e, lo, j, first=False):
                    def down(k):
                        if first:
                            dve.wait_ge(e_hi, SPLITS * e + 2 * KD + k + 1)
                            lo_half(dn[1][:, k, :], raw_d[:, k, :], dn[0][:, k, :]).then_inc(e_lo, 1)

                    dve.wait_ge(sg_ok, j + 1)
                    tt(sg[:, :], bankG[:, :], sg[:, :], ALU.mult)
                    dve.drain()
                    dve.wait_ge(u1_done, j + 1)
                    tt(hid[:, 0:256], bankU[0][:, 0:256], sg[:, 0:256], ALU.mult).then_inc(hid_ok, 1)
                    down(0)
                    dve.wait_ge(hT_hi, 2 * j + 1)
                    hidden_low(0)
                    dve.wait_ge(gu_done, j + 2)
                    tt(hid[:, 256:512], bankU[1][:, 0:256], sg[:, 256:512], ALU.mult).then_inc(hid_ok, 1)
                    down(1)
                    rows_low(2 * j + 3)
                    down(2)
                    dve.wait_ge(hT_hi, 2 * j + 2)
                    hidden_low(1)
                    down(3)
                experts(dve, split, per_block, peel=True)

            @block.tensor
            def _(pe):
                def rows_of_x(count):
                    pe.wait_ge(x_rows_in, count)
                    for c in range(2):
                        for k in range(4):
                            last = nc.tensor.transpose(bankX[c][:, k * P:(k + 1) * P],
                                                       x[:, (4 * c + k) * P:(4 * c + k + 1) * P], ident[:, :])
                    last.then_inc(x_tr, 1)

                pe.wait_ge(tab_ok, 1)
                rows_of_x(16)

                def accumulate(out, a, ka, w, kw, cols, n, total):
                    nc.tensor.matmul(out, a[0][:, ka, :], w[0][:, kw, cols], start=(n == 0), stop=False)
                    nc.tensor.matmul(out, a[0][:, ka, :], w[1][:, kw, cols], start=False, stop=False)
                    return nc.tensor.matmul(out, a[1][:, ka, :], w[0][:, kw, cols], start=False, stop=(n == total - 1))

                def hidden_transposed(c):
                    for k in range(2):
                        last = nc.tensor.transpose(bankH[c][:, k * P:(k + 1) * P],
                                                   hid[:, (2 * c + k) * P:(2 * c + k + 1) * P], ident[:, :])
                    last.then_inc(th_done, 1)

                def per_block(e, lo, j):
                    pe.wait_ge(ex_lo, 2 * j + 2)
                    pe.wait_ge(hT_lo, 2 * j + 1)
                    for k in range(KD):
                        pe.wait_ge(e_lo, SPLITS * e + k + 1)
                        last = accumulate(bankG[:, :], xT, k, gu, k, slice(0, HALF), k, KD)
                    last.then_inc(g_done, 1)
                    for k in range(KD):
                        pe.wait_ge(e_lo, SPLITS * e + KD + k + 1)
                        last = accumulate(bankU[0][:, 0:256], xT, k, gu, KD + k, slice(0, 256), k, KD)
                    last.then_inc(u1_done, 1)
                    for k in range(KD):
                        last = accumulate(bankU[1][:, 0:256], xT, k, gu, KD + k, slice(256, 512), k, KD)
                        if k == 4:
                            pe.wait_ge(hid_ok, 2 * j + 1)
                            hidden_transposed(0)
                    last.then_inc(gu_done, 1)
                    rows_of_x(16 * j + 32)
                    pe.wait_ge(y_read, 2 * j + 2)
                    pe.wait_ge(hT_lo, 2 * j + 2)
                    for k in range(KH):
                        pe.wait_ge(e_lo, SPLITS * e + 2 * KD + k + 1)
                        if k == 2:
                            pe.wait_ge(hT_lo, 2 * j + 3)
                        for half in range(2):
                            last = accumulate(bankY[half][:, :], hT, k, dn, k, slice(half * HALF, (half + 1) * HALF),
                                              k, KH)
                        if k == 0:
                            pe.wait_ge(hid_ok, 2 * j + 2)
                            hidden_transposed(1)
                    last.then_inc(y_done, 1)
                experts(pe, lambda e, lo: None, per_block)


def phase_four(nc, v):
    sem, gains, rows_i, h_dram, y_dram = (v[k] for k in ("sem", "gains", "rows_i", "h_dram", "y_dram"))
    DEPTH = 4
    stack = ExitStack()
    with stack:
        sb = v["tiles"](stack)
        gf = sb("gf", [P, D])
        hb = sb("hb", [P, DEPTH, D])
        yr = [[sb(f"yr{b}{c}", [P, D]) for c in range(2)] for b in range(DEPTH)]
        out = sb("out", [P, DEPTH, D])
        idx = [sb(f"idx{b}", [P, 2], I32) for b in range(DEPTH)]
        gc = sb("gc", [P, DEPTH, 2])
        sq = sb("sq", [P, D], BF16)
        ss = sb("ss4", [P, DEPTH])
        ms = sb("ms4", [P, DEPTH])
        rs = sb("rs4", [P, DEPTH])

        gf_in, idx4, passed_pool = sem("gf_in"), sem("idx4"), sem("passed_pool4")
        h_in = [sem(f"h_in{b}") for b in range(DEPTH)]
        r_in = [sem(f"r_in{b}") for b in range(DEPTH)]
        sum_ok, ss_ok, ms_ok, root_ok, out_ok = (sem(n) for n in ("sum_ok", "ss_ok", "ms_ok", "root_ok", "out_ok"))
        stored = [sem(f"stored{b}") for b in range(DEPTH)]

        def tile_loop(eng, per_tile):
            with eng.Fori(0, (NT - 1) // DEPTH) as i:
                for b in range(DEPTH):
                    per_tile(i, b, P)
            per_tile((NT - 1) // DEPTH, 0, SAMPLE)

        with nc.Block() as block:
            @block.sync
            def _(sp):
                sp.dma_start(gf[:, :], v["g_final"].rearrange("(a n) -> a n", a=1).broadcast_to([P, D])).then_inc(gf_in, 16)

                def load(i, b, r):
                    sp.wait_ge(out_ok, DEPTH * i + b + 1)
                    sp.dma_start(hb[0:r, b, :], h_dram[bass.ds((i * DEPTH + b) * P, r), :]).then_inc(h_in[b], 16)
                tile_loop(sp, load)

            @block.gpsimd
            def _(pool):
                for b in range(DEPTH):
                    nc.gpsimd.memset(out[:, b, :], 0.0).then_inc(stored[b], 16)
                for b in range(DEPTH):
                    nc.gpsimd.memset(idx[b][:, :], 0).then_inc(out_ok, 1)

                def gather(i, b, r):
                    pool.wait_ge(out_ok, DEPTH * i + b + 1)
                    col = bass.ds(i * DEPTH + b, 1)
                    nc.gpsimd.tensor_copy(idx[b][:, :], rows_i[:, :, col].rearrange("p c o -> p (c o)")).then_inc(idx4, 1)
                    wait_apart(pool, idx4, DEPTH * i + b + 1, passed_pool)
                    for c in range(2):
                        nc.gpsimd.indirect_dma_start(out=yr[b][c][0:r, :], out_offset=None, in_=y_dram,
                                                     in_offset=bass.IndirectOffsetOnAxis(ap=idx[b][0:r, c:c + 1], axis=0))\
                            .then_inc(r_in[b], 16)
                tile_loop(pool, gather)

            @block.vector
            def _(dve):
                ts, stt = nc.vector.tensor_scalar, nc.vector.scalar_tensor_tensor
                dve.wait_ge(gf_in, 16)

                def add_up(i, b, r):
                    n = DEPTH * i + b + 1
                    nc.vector.tensor_copy(gc[:, b, :], gains[:, :, bass.ds(i * DEPTH + b, 1)].rearrange("p c o -> p (c o)"))
                    dve.drain()
                    dve.wait_ge(h_in[b], 16 * i + 16)
                    dve.wait_ge(r_in[b], 32 * i + 32)
                    hr = hb[0:r, b, :]
                    stt(hr, yr[b][0][0:r, :], gc[0:r, b, 0:1], hr, ALU.mult, ALU.add)
                    dve.drain()
                    stt(hr, yr[b][1][0:r, :], gc[0:r, b, 1:2], hr, ALU.mult, ALU.add).then_inc(sum_ok, 1)
                    dve.wait_ge(ss_ok, n)
                    ts(ms[0:r, b:b + 1], ss[0:r, b:b + 1], 1.0 / D, EPS, ALU.mult, ALU.add).then_inc(ms_ok, 1)
                    dve.wait_ge(root_ok, n)
                    nc.vector.reciprocal(rs[0:r, b:b + 1], rs[0:r, b:b + 1])
                    dve.drain()
                    dve.wait_ge(stored[b], 16 * i + 16)
                    stt(out[0:r, b, :], hr, rs[0:r, b:b + 1], gf[0:r, :], ALU.mult, ALU.mult).then_inc(out_ok, 1)
                tile_loop(dve, add_up)

            @block.scalar
            def _(act):
                def root(i, b, r):
                    n = DEPTH * i + b + 1
                    act.wait_ge(sum_ok, n)
                    nc.scalar.activation(sq[0:r, :], hb[0:r, b, :], ACT.Square, accum_out=ss[0:r, b:b + 1]).then_inc(ss_ok, 1)
                    act.wait_ge(ms_ok, n)
                    nc.scalar.activation(rs[0:r, b:b + 1], ms[0:r, b:b + 1], ACT.Sqrt).then_inc(root_ok, 1)
                    act.wait_ge(out_ok, n + DEPTH)
                    if r == P:
                        act.dma_start(v["y_prompt"][0, bass.ds((i * DEPTH + b) * P, P), :], out[:, b, :])\
                            .then_inc(stored[b], 16)
                    else:
                        act.dma_start(v["y_sample"][0, :, :], out[0:r, b, :]).then_inc(stored[b], 16)
                tile_loop(act, root)
                for b in range(DEPTH):
                    act.wait_ge(stored[b], 16 + 16 * ((NT - 1) // DEPTH) + (16 if b == 0 else 0))


_INS = ["x_prompt", "x_sample", "state_pool", "g_mix", "w_in", "w_pool", "pool_scale", "g_v", "w_spatial",
        "b_spatial", "w_up_pool", "w_up_gmlp", "w_out", "g_ffn", "w_group", "b_group", "w_router", "b_router",
        "w_gate", "w_up", "w_down", "g_final"]
_OUTS = [(1, SEQ, D), (1, SAMPLE, D), (1, 1, HIST, HALF), (1, 1, HIST, HALF), (1, 1, SAMPLE, HALF)]


def kernel(**inputs):
    import numpy as np
    import concourse.bacc as bacc
    from concourse.bass_utils import run_bass_kernel_spmd

    nc = bacc.Bacc("TRN2", target_bir_lowering=False, num_devices=1)
    arrays, args = {}, []
    for name in _INS:
        a = np.ascontiguousarray(inputs[name])
        arrays[f"in_{name}"] = a
        args.append(nc.dram_tensor(f"in_{name}", a.shape, mybir.dt.from_np(a.dtype), kind="ExternalInput").ap())
    for i, shape in enumerate(_OUTS):
        args.append(nc.dram_tensor(f"out_{i}", shape, F32, kind="ExternalOutput").ap())
    build(nc, *args)
    r = run_bass_kernel_spmd(nc, [arrays], core_ids=[0])
    return tuple(r.results[0][f"out_{i}"] for i in range(len(_OUTS)))
```

```python
from contextlib import ExitStack

import concourse.bass as bass
from concourse import mybir

F32 = mybir.dt.float32
F32R = mybir.dt.float32r
BF16 = mybir.dt.bfloat16
I32 = mybir.dt.int32
U32 = mybir.dt.uint32
ALU = mybir.AluOpType
ACT = mybir.ActivationFunctionType
AX = mybir.AxisListType.X

P = 128
D = 1024
KD = D // P
SEQ = 2048
SAMPLE = 32
HALF = 512
KH = HALF // P
IN_COLS = 3 * HALF + 2 * D
HIST = 15
GROUP = 512
TPG = GROUP // P
NPROMPT = SEQ // GROUP
NT = SEQ // P + 1
NG, EPG = 4, 4
NE = NG * EPG
BPE = (SEQ + SAMPLE + P - 1) // P
NSLOT = NE * BPE
MAXBLK = (2 * (SEQ + SAMPLE)) // P + NE + 1
EPS = 1e-6
NEG = -3.0e38

NPAN = 22
PRE = 4
SPLITS = 20


def products(nc, out, pairs):
    n = len(pairs)
    last = None
    for i, ((lh, ll), (rh, rl)) in enumerate(pairs):
        nc.tensor.matmul(out, lh, rh, start=(i == 0), stop=False)
        nc.tensor.matmul(out, lh, rl, start=False, stop=False)
        last = nc.tensor.matmul(out, ll, rh, start=False, stop=(i == n - 1))
    return last


def bank_uses(nt, nt_next, first):
    seq = []
    if not first:
        seq += [("u", m) for m in range(4)]
        for i in range(4):
            seq += [("ga", 2 * i), ("ga", 2 * i + 1), ("gb", 2 * i), ("gb", 2 * i + 1)]
            seq += [("P", 2 * i), ("Q", 2 * i), ("P", 2 * i + 1), ("Q", 2 * i + 1)]
    seq += [("x", t, c) for t in range(nt_next) for c in range(2)]
    if not first:
        seq += [("hn", t, c) for t in range(nt) for c in range(2)]
    if nt_next:
        seq += [("a", 0), ("a", 1), ("a", 2), ("pm", 0), ("a", 3), ("pm", 1), ("pm", 2), ("pm", 3)]
    return {key: i for i, key in enumerate(seq)}, len(seq)


PRO_USES, N_PRO = bank_uses(0, TPG, True)
MID_USES, N_MID = bank_uses(TPG, TPG, False)
LAST_P_USES, N_LAST_P = bank_uses(TPG, 1, False)
SAM_USES, N_SAM = bank_uses(1, 0, False)
assert N_PRO % 2 == N_MID % 2 == 0
N_USES = N_PRO + (NPROMPT - 1) * N_MID + N_LAST_P + N_SAM


def wait_apart(eng, s, value, passed):
    eng.wait_ge(s, value)
    eng.sem_inc(passed, 1)


class PhaseOne:

    def __init__(self, g):
        self.g = g
        static = isinstance(g, int)
        self.pro = static and g < 0
        self.nt = 0 if self.pro else (1 if static and g == NPROMPT else TPG)
        self.n = SAMPLE if static and g == NPROMPT else GROUP
        self.rows = SAMPLE if static and g == NPROMPT else P
        self.next = not (static and g == NPROMPT)
        self.nt2 = 0 if not self.next else (1 if static and g == NPROMPT - 1 else TPG)
        self.n2 = SAMPLE if static and g == NPROMPT - 1 else GROUP
        self.rows2 = SAMPLE if static and g == NPROMPT - 1 else P
        before_last = N_PRO + (NPROMPT - 1) * N_MID
        if self.pro:
            self.uses, self.start = PRO_USES, 0
        elif static and g == NPROMPT:
            self.uses, self.start = SAM_USES, before_last + N_LAST_P
        elif static and g == NPROMPT - 1:
            self.uses, self.start = LAST_P_USES, before_last
        else:
            self.uses, self.start = MID_USES, (N_PRO + g * N_MID if static else None)
        self.before = None if self.pro else (
            (LAST_P_USES, N_LAST_P) if static and g == NPROMPT else (MID_USES, N_MID))

    @property
    def prev(self):
        return None if isinstance(self.g, int) and self.g < 1 else PhaseOne(self.g - 1)

    def use(self, *key):
        return self._place(self.uses[key])

    def use_before(self, *key):
        table, n = self.before
        return self._place(table[key] - n)

    def _place(self, i):
        if self.start is None:
            return i % 2, self.g * (N_MID // 2) + (N_PRO + i) // 2
        return (self.start + i) % 2, (self.start + i) // 2

    def panel(self, i):
        if self.pro:
            return i % 2, i
        return i % 2, self.g * NPAN + PRE + i


def build(nc, x_prompt, x_sample, state_pool, g_mix, w_in, w_pool, pool_scale, g_v, w_spatial, b_spatial,
          w_up_pool, w_up_gmlp, w_out, g_ffn, w_group, b_group, w_router, b_router, w_gate, w_up, w_down,
          g_final, y_prompt, y_sample, new_pool_prompt, new_pool_sample, new_v):
    outer = ExitStack()

    def sem(name):
        return outer.enter_context(nc.semaphore(name))

    def tiles(stack):
        def sb(name, shape, dt=F32):
            return stack.enter_context(nc.sbuf_tensor(name, shape, dt))
        return sb

    h_dram = nc.dram_tensor("h_rows", [SEQ + SAMPLE + P, D], F32).ap()
    hn_dram = nc.dram_tensor("hn_rows", [SEQ + SAMPLE + P, D], F32).ap()
    slot_dram = nc.dram_tensor("slot_table", [P * NSLOT, 2], I32).ap()

    with outer:
        keep = tiles(outer)
        ident = keep("ident", [P, P])
        running = keep("running", [P, NE])
        iota16 = keep("iota16", [P, NE])
        blk_tab = keep("blk_tab", [P, 2 * NE], I32)
        psum = [outer.enter_context(nc.psum_tensor(f"bank{b}", [P, 512], F32)) for b in range(8)]

        shared = dict(locals())
        phase_one(nc, shared)
        phase_three(nc, shared)
        phase_four(nc, shared)


def phase_one(nc, v):
    sem, psum, ident, running, iota16 = (v[k] for k in ("sem", "psum", "ident", "running", "iota16"))
    x_prompt, x_sample = v["x_prompt"], v["x_sample"]
    w_in, w_out = v["w_in"], v["w_out"]
    h_dram, hn_dram, slot_dram = v["h_dram"], v["hn_dram"], v["slot_dram"]
    bankA = [psum[5], psum[6]]
    bankR, bankC = psum[4], psum[7]
    bankV = psum[0:4]

    stack = ExitStack()
    with stack:
        sb = v["tiles"](stack)
        xT = [sb("xT_hi", [P, KD, GROUP], F32R), sb("xT_lo", [P, KD, GROUP], F32R)]
        mg = [sb("mg_hi", [P, KD, GROUP], F32R), sb("mg_lo", [P, KD, GROUP], F32R)]
        with ExitStack() as shared:
            s1 = v["tiles"](shared)
            pa = [s1("pa_hi", [P, KH, GROUP], F32R), s1("pa_lo", [P, KH, GROUP], F32R)]
            pb = [s1("pb_hi", [P, KH, GROUP], F32R), s1("pb_lo", [P, KH, GROUP], F32R)]
        h = sb("h", [P, TPG, D])
        hn = sb("hn", [P, 2, D])
        hnT = sb("hnT", [P, KD, P])
        sb("shared_tail", [P, 4 * KH * GROUP - TPG * D - 2 * D - KD * P])
        raw = [sb("raw0", [P, 8, 256]), sb("raw1", [P, 8, 256])]
        wh = [sb("wh0", [P, 8, 256], F32R), sb("wh1", [P, 8, 256], F32R)]
        wl = [sb("wl0", [P, 8, 256], F32R), sb("wl1", [P, 8, 256], F32R)]
        xb = sb("xb", [P, TPG, D])
        S = sb("S", [P, 4, GROUP])
        vf = sb("vf", [P, HALF])
        vn = [m[:, 4:8, :] for m in mg]
        ext = sb("ext", [P, GROUP + 16])
        win = [sb("win0", [P, GROUP + 16]), sb("win1", [P, GROUP + 16])]
        dd = [m[:, 0:2, :] for m in mg]
        junk = sb("junk", [P, D], BF16)
        hist = [sb("hist_prompt", [P, 4, 16]), sb("hist_sample", [P, 4, 16])]
        state = vf[0:16, :]
        corr = sb("corr", [P, 4, 16])
        wp_raw = win[0][:, 0:HALF].rearrange("p (g d) -> p g d", g=4)
        wsp_raw = win[1][:, 0:HALF].rearrange("p (g d) -> p g d", g=4)
        wp = [sb("wp_hi", [P, 4, P], F32R), sb("wp_lo", [P, 4, P], F32R)]
        ws = [sb("ws_hi", [P, 4, P], F32R), sb("ws_lo", [P, 4, P], F32R)]
        bsp = sb("bsp", [P, 4, P])
        gv = sb("gv", [P, HALF])
        gmix = sb("gmix", [P, D])
        gffn = sb("gffn", [P, D])
        pscale = sb("pscale", [P, 4])
        wr = sb("wr", [P, KD, 20])
        br = sb("br", [P, 20])
        upper = sb("upper", [P, P])
        ones = sb("ones", [P, P])
        half_neg = sb("half_neg", [P, 1])
        ss = sb("ss", [P, 12])
        ms = sb("ms", [P, 12])
        rs = sb("rs", [P, 12])
        lg = sb("lg", [P, TPG, 24])
        best = sb("best", [P, TPG, 8])
        besti = sb("besti", [P, TPG, 8], U32)
        inside = sb("inside", [P, TPG, NG])
        el = sb("el", [P, TPG, NE])
        gidx = sb("gidx", [P, TPG])
        mask = sb("mask", [P, 2, TPG, NE])
        msum = sb("msum", [P, TPG, NE])
        rank = sb("rank", [P, TPG, NE])
        prod = sb("prod", [P, 2, TPG, NE])
        pen = sb("pen", [P, TPG, NG])
        rec = sb("rec", [P, TPG, 2])
        exps = sb("exps", [P, TPG, NG + 1])
        parts = sb("parts", [P, 2, TPG])
        pay = sb("pay", [P, 2, TPG, 2], I32)
        dest_f = sb("dest_f", [P, 2, TPG])
        dest = sb("dest", [P, 2, TPG], I32)
        tok_all = sb("tok_all", [P, NT], I32)
        empty = S[:, 2:4, :].rearrange("p a n -> p (a n)")[:, 0:2 * NSLOT].rearrange("p (n o) -> p n o", o=2).bitcast(I32)
        zero_rows = S[:, 0:2, :].rearrange("p a n -> p (a n)")
        histT = xb[0:16, 0:2, 0:HALF]
        low7 = sb("low7", [P, 2, TPG], I32)
        high7 = sb("high7", [P, 2, TPG], I32)

        const_in, const_tr, const_ok, setup, dve_setup = (sem(s) for s in (
            "const_in", "const_tr", "const_ok", "setup", "dve_setup"))
        passed_pool, passed_dve = sem("passed_pool"), sem("passed_dve")
        raw_in = [sem("raw_in0"), sem("raw_in1")]
        w_hi, w_lo, half_used = sem("w_hi"), sem("w_lo"), sem("half_used")
        a_full = [sem("a0_full"), sem("a1_full")]
        a_free = [sem("a0_free"), sem("a1_free")]
        x_in = sem("x_in")
        sp_full, sp_read = sem("sp_full"), sem("sp_read")
        x_ss, x_ms, x_rs, x_scaled, xT_hi = (sem(s) for s in ("x_ss", "x_ms", "x_rs", "x_scaled", "xT_hi"))
        v_full, v_ss, v_ms, v_rs, vf_ok, vn_hi, vn_ok, v_out = (sem(s) for s in (
            "v_full", "v_ss", "v_ms", "v_rs", "vf_ok", "vn_hi", "vn_ok", "v_out"))
        d_ok, d_hi, d_lo, pa_hi = sem("d_ok"), sem("d_hi"), sem("d_lo"), sem("pa_hi")
        pb_hi, pb_ok = sem("pb_hi"), sem("pb_ok")
        mix_ok, mg_hi, mg_ok = sem("mix_ok"), sem("mg_hi"), sem("mg_ok")
        res_in, o_full, h_part, h_ss, h_ms, h_rs, hn_ok, h_out = (sem(s) for s in (
            "res_in", "o_full", "h_part", "h_ss", "h_ms", "h_rs", "hn_ok", "h_out"))
        hn_out = [sem("hn_out0"), sem("hn_out1")]
        exps_in, exps_ok, spare_out = sem("exps_in"), sem("exps_ok"), sem("spare_out")
        lg_full, lg_ok, mask_ok, cum_full, dest_ok, scattered = (sem(s) for s in (
            "lg_full", "lg_ok", "mask_ok", "cum_full", "dest_ok", "scattered"))
        hist_full, hist_ok, hist_out = sem("hist_full"), sem("hist_ok"), sem("hist_out")

        def win_view(c0, k0, nk, width):
            return w_in[0, k0 * P:(k0 + nk) * P, c0:c0 + width].rearrange("(k p) n -> p k n", p=P)

        def panel_sources(i, pro):
            whole = lambda r: r[:, :, :]
            wide = lambda r: r[:, :, :].rearrange("p (k a) n -> p k (a n)", a=2)
            if pro:
                i += NPAN - PRE
            if i < 2:
                return [(whole, win_view(HALF + i * 256, 0, 8, 256))]
            if i < 14:
                j, kind = (i - 2) // 3, (i - 2) % 3
                if kind < 2:
                    return [(whole, win_view(3 * HALF + kind * D + j * 256, 0, 8, 256))]
                view = lambda w: w[0, :, j * 256:(j + 1) * 256].rearrange("(k p) n -> p k n", p=P)
                return [(lambda r: r[:, 0:4, :], view(v["w_up_pool"])),
                        (lambda r: r[:, 4:8, :], view(v["w_up_gmlp"]))]
            if i < 18:
                half, kh = (i - 14) // 2, (i - 14) % 2
                return [(wide, w_out[0, kh * 512:(kh + 1) * 512, half * 512:(half + 1) * 512]
                         .rearrange("(k p) n -> p k n", p=P))]
            if i < 20:
                return [(wide, win_view(2 * HALF, 4 * (i - 18), 4, 512))]
            return [(whole, win_view((i - 20) * 256, 0, 8, 256))]

        def part(w, q):
            return w[:, 2 * q:2 * q + 2, :]

        def x_rows(ph, t, nxt=True):
            g = ph.g + 1 if nxt else ph.g
            if isinstance(g, int) and g == NPROMPT:
                return x_sample[0, :, :]
            return x_prompt[0, bass.ds(g * GROUP + t * P, P), :]

        def passes(eng, body):
            body(PhaseOne(-1))
            body(PhaseOne(0))
            with eng.Fori(1, NPROMPT - 1) as g:
                body(PhaseOne(g))
            body(PhaseOne(NPROMPT - 1))
            body(PhaseOne(NPROMPT))

        def wait(eng, s, value):
            if not (isinstance(value, int) and value <= 0):
                eng.wait_ge(s, value)

        def full(eng, ph, *key):
            b, q = ph.use(*key)
            eng.wait_ge(a_full[b], q + 1)
            return b

        def freed(eng, ph, *key):
            b, q = ph.use(*key)
            eng.wait_ge(a_free[b], q + 1)

        def panel_done(eng, ph, i):
            if ph.pro:
                i += 18
            if i < 0:
                b, q = ph.use_before("a", 5 + 2 * i)
            elif i < 2:
                b, q = ph.use("u", 2 * i + 1)
            elif i < 14:
                b, q = ph.use(("ga", "gb", "Q")[(i - 2) % 3], 2 * ((i - 2) // 3) + 1)
            elif i in (14, 16, 18):
                eng.wait_ge(half_used, 3 * ph.g + 2 + (i - 14) // 2)
                return
            elif i in (15, 17):
                eng.wait_ge(o_full, ph.g * 2 * TPG + (1 if i == 15 else 2) * ph.nt)
                return
            elif i == 19:
                eng.wait_ge(v_full, (ph.g + 1) * TPG + ph.nt2)
                return
            else:
                b, q = ph.use("a", 2 * (i - 20) + 1)
            eng.wait_ge(a_full[b], q + 1)

        block_stack = ExitStack()
        block = block_stack.enter_context(nc.Block())

        @block.sync
        def _(sp):
            consts = [
                (wp_raw, v["w_pool"][0].rearrange("g c d -> c g d")),
                (wsp_raw, v["w_spatial"][0].rearrange("h i j -> i h j")),
                (bsp[:, :, :].rearrange("p h i -> p (h i)"),
                 v["b_spatial"].rearrange("a h i -> a (h i)").broadcast_to([P, HALF])),
                (gv[:, :], v["g_v"].broadcast_to([P, HALF])),
                (gmix[:, :], v["g_mix"].broadcast_to([P, D])),
                (gffn[:, :], v["g_ffn"].broadcast_to([P, D])),
                (pscale[:, :], v["pool_scale"][0].rearrange("(k p) -> p k", p=P)),
                (wr[:, :, 0:4], v["w_group"][0].rearrange("(k p) n -> p k n", p=P)),
                (wr[:, :, 4:20], v["w_router"][0].rearrange("(k p) n -> p k n", p=P)),
                (br[:, 0:4], v["b_group"].broadcast_to([P, NG])),
                (br[:, 4:20], v["b_router"].broadcast_to([P, NE])),
            ]
            assert len(consts) == 11
            sp.wait_ge(setup, 1)
            sp.dma_start(state[1:16, :], v["state_pool"][0, 0, :, :]).then_inc(const_in, 16)
            with nc.allow_non_contiguous_dma(reason="short columns of constants"):
                for dst, src in consts:
                    sp.dma_start(dst, src).then_inc(const_in, 16)

            def load_panel(ph, i):
                par, n = ph.panel(i)
                if not (ph.pro and i < 2):
                    sp.wait_ge(w_lo, n - 1)
                for view, src in panel_sources(i, ph.pro):
                    sp.dma_start(view(raw[par]), src).then_inc(raw_in[par], 16)

            def store_h(ph, tiles):
                for t in tiles:
                    sp.wait_ge(hn_ok, ph.g * TPG + t + 1)
                    rows = bass.ds(ph.g * GROUP + t * P, ph.rows)
                    sp.dma_start(h_dram[rows, :], h[0:ph.rows, t, :]).then_inc(h_out, 16)
                    sp.dma_start(hn_dram[rows, :], hn[0:ph.rows, t % 2, :]).then_inc(hn_out[t % 2], 16)

            def body(ph):
                count = PRE if ph.pro else (NPAN if ph.next else NPAN - PRE)
                for i in range(count):
                    load_panel(ph, i)
                    if not ph.pro and i == 15:
                        panel_done(sp, ph, 13)
                        for t in range(ph.nt):
                            sp.dma_start(h[0:ph.rows, t, :], x_rows(ph, t, False)).then_inc(res_in, 16)
                    if not ph.pro and i == 19:
                        store_h(ph, range(0, ph.nt - 2))
                    if not ph.pro and i == 20:
                        store_h(ph, range(ph.nt - 2, ph.nt))
                if not ph.next:
                    store_h(ph, range(ph.nt))
                if isinstance(ph.g, int) and ph.g == NPROMPT - 1:
                    sp.wait_ge(vf_ok, NT)
                    sp.dma_start(v["new_v"][0, 0, :, :], vf[0:SAMPLE, :]).then_inc(v_out, 16)
            passes(sp, body)
            sp.wait_ge(v_out, 16)
            sp.wait_ge(h_out, 16 * NT)
            sp.wait_ge(hn_out[0], 16 + 16 * (2 * NPROMPT + 1))
            sp.wait_ge(hn_out[1], 16 + 16 * 2 * NPROMPT)
            for c, out in ((0, v["new_pool_prompt"]), (1, v["new_pool_sample"])):
                sp.wait_ge(hist_ok, c + 1)
                sp.dma_start(out[0, 0, :, :], histT[1:16, c, :]).then_inc(hist_out, 16)
            sp.wait_ge(hist_out, 32)

        @block.gpsimd
        def _(pool):
            nc.gpsimd.memset(state, 0.0).then_inc(setup, 1)
            nc.gpsimd.memset(half_neg[:, :], -0.5).then_inc(setup, 1)
            nc.gpsimd.memset(ones[:, :], 1.0).then_inc(setup, 1)
            nc.gpsimd.memset(zero_rows, 0.0).then_inc(setup, 1)
            nc.gpsimd.memset(empty[:, :, 1:2], 0).then_inc(setup, 1)
            nc.gpsimd.iota(empty[:, :, 0:1], pattern=[[0, NSLOT], [0, 1]], base=SEQ + SAMPLE, channel_multiplier=1)\
                .then_inc(setup, 1)
            nc.gpsimd.iota(iota16[:, :], pattern=[[1, NE]], base=0, channel_multiplier=0,
                           allow_small_or_imprecise_dtypes=True).then_inc(setup, 1)
            nc.gpsimd.iota(tok_all[:, :], pattern=[[P, NT]], base=0, channel_multiplier=1).then_inc(setup, 1)
            nc.gpsimd.memset(lg[:, :, 4:8], NEG).then_inc(hn_out[0], 16)
            nc.gpsimd.memset(running[:, :], 0.0).then_inc(hn_out[1], 16)
            nc.gpsimd.memset(msum[:, :, :], 0.0).then_inc(setup, 1)
            pool.wait_ge(setup, 9)
            nc.gpsimd.affine_select(out=ident[:, :], in_=ones[:, :], compare_op=ALU.is_equal, fill=0.0, base=0,
                                    pattern=[[-1, P]], channel_multiplier=1).then_inc(setup, 1)
            nc.gpsimd.affine_select(out=upper[:, :], in_=ones[:, :], compare_op=ALU.is_gt, fill=0.0, base=0,
                                    pattern=[[1, P]], channel_multiplier=-1).then_inc(setup, 1)
            pool.wait_ge(const_in, 16 * 12)
            nc.gpsimd.affine_select(out=wsp_raw, in_=wsp_raw, compare_op=ALU.is_ge, fill=0.0, base=0,
                                    pattern=[[0, 4], [-1, P]], channel_multiplier=1).then_inc(setup, 1)
            pool.dma_start(slot_dram.rearrange("(p n) o -> p n o", p=P), empty).then_inc(scattered, 16)
            for rows in (h_dram, hn_dram):
                pool.dma_start(rows[SEQ + SAMPLE:SEQ + SAMPLE + P, :], zero_rows).then_inc(spare_out, 16)

            def rsqrt(ms_sem, value, rows, col, done):
                pool.wait_ge(ms_sem, value)
                nc.gpsimd.tensor_tensor(rs[0:rows, col:col + 1], ms[0:rows, col:col + 1], half_neg[0:rows, :],
                                        ALU.pow).then_inc(done, 1)

            def scatter(ph):
                pool.wait_ge(dest_ok, ph.g + 1)
                wait_apart(pool, scattered, 16 + 32 * TPG * ph.g, passed_pool)
                for t in range(ph.nt):
                    for c in range(2):
                        nc.gpsimd.indirect_dma_start(
                            out=slot_dram,
                            out_offset=bass.IndirectOffsetOnAxis(ap=dest[0:ph.rows, c, t:t + 1], axis=0),
                            in_=pay[0:ph.rows, c, t, :], in_offset=None).then_inc(scattered, 16)

            def body(ph):
                first = (ph.g + 1) * TPG
                if ph.nt2:
                    if not ph.pro:
                        pool.wait_ge(xT_hi, 2 * first)
                    if ph.n2 == GROUP:
                        src = x_prompt[0, bass.ds((ph.g + 1) * GROUP, GROUP), :].rearrange("(t p) d -> p t d", p=P)
                        pool.dma_start(xb[:, :, :], src).then_inc(x_in, 16)
                    else:
                        pool.dma_start(xb[0:SAMPLE, 0, :], x_sample[0, :, :]).then_inc(x_in, 16)
                if ph.prev:
                    scatter(ph.prev)
                for t in range(ph.nt2):
                    rsqrt(x_ms, first + t + 1, ph.rows2, t, x_rs)
                for t in range(ph.nt):
                    rsqrt(h_ms, ph.g * TPG + t + 1, ph.rows, 8 + t, h_rs)
                for t in range(ph.nt2):
                    rsqrt(v_ms, first + t + 1, ph.rows2, 4 + t, v_rs)
                if not ph.next:
                    scatter(ph)
            passes(pool, body)
            pool.wait_ge(scattered, 16 + 32 * NT)

        @block.scalar
        def _(act):
            act.wait_ge(const_in, 16 * 12)
            act.wait_ge(setup, 12)
            nc.scalar.activation(wp[0][:, :, :], wp_raw, ACT.Copy).then_inc(const_ok, 1)
            act.wait_ge(const_tr, 1)
            nc.scalar.activation(ws[0][:, :, :], bankC[:, :].rearrange("p (h i) -> p h i", h=4),
                                 ACT.Copy).then_inc(const_ok, 1)

            def split(ph, i):
                par, n = ph.panel(i)
                loads = sum(len(panel_sources(q, ph.pro)) for q in range(par, i + 1, 2))
                act.wait_ge(raw_in[par], 16 * (loads if ph.pro else 2 + 13 * ph.g + loads))
                if not (ph.pro and i < 2):
                    panel_done(act, ph, i - 2)
                for q in range(4):
                    nc.scalar.activation(part(wh[par], q), part(raw[par], q), ACT.Copy).then_inc(w_hi, 1)

            def softmaxes(ph):
                act.wait_ge(exps_in, ph.g + 1)
                nc.scalar.activation(exps[0:ph.rows, 0:ph.nt, :], exps[0:ph.rows, 0:ph.nt, :], ACT.Exp)\
                    .then_inc(exps_ok, 1)

            def squares_of_x(ph):
                if ph.nt2:
                    act.wait_ge(x_in, 16 * (ph.g + 2))
                for t in range(ph.nt2):
                    r, num = ph.rows2, (ph.g + 1) * TPG + t
                    if t:
                        act.wait_ge(x_ss, num)
                    nc.scalar.activation(junk[0:r, :], xb[0:r, t, :], ACT.Square,
                                         accum_out=ss[0:r, t:t + 1]).then_inc(x_ss, 1)

            def body(ph):
                n, n2, g = ph.n, ph.n2, ph.g
                first = (g + 1) * TPG
                o = 0 if ph.pro else 18
                if ph.pro:
                    split(ph, 0)
                    squares_of_x(ph)
                else:
                    for i in range(2):
                        split(ph, i + 1)
                        for m in (2 * i, 2 * i + 1):
                            freed(act, ph, "u", m)
                            if m == 0:
                                act.wait_ge(hn_out[0], 32 * g + 16)
                                act.wait_ge(hn_out[1], 32 * g + 16)
                            nc.scalar.activation(pb[0][:, m, 0:n], win[m % 2][:, 0:n], ACT.Copy).then_inc(pb_hi, 1)
                    for i in range(4):
                        for kind, name in enumerate(("ga", "gb")):
                            split(ph, 3 + 3 * i + kind)
                            for c in range(2):
                                b = full(act, ph, name, 2 * i + c)
                                if kind == 0 and c == 0:
                                    if i:
                                        act.wait_ge(mg_ok, g * 8 + 2 * i)
                                    else:
                                        act.wait_ge(pb_ok, g * 4 + 4)
                                nc.scalar.activation(S[:, 2 * kind + c, 0:n], bankA[b][:, 0:n], ACT.Sigmoid)\
                                    .then_inc(a_free[b], 1)
                            if i == 3 and kind == 0:
                                squares_of_x(ph)
                        split(ph, 5 + 3 * i)
                        for m in (2 * i, 2 * i + 1):
                            act.wait_ge(mix_ok, g * 8 + m + 1)
                            nc.scalar.activation(mg[0][:, m, 0:n], win[m % 2][:, 0:n], ACT.Copy).then_inc(mg_hi, 1)
                        if ph.prev and i == 1:
                            softmaxes(ph.prev)
                    split(ph, 15)
                for t in range(ph.nt2):
                    r = ph.rows2
                    for c in range(2):
                        b = full(act, ph, "x", t, c)
                        nc.scalar.activation(xT[0][:, 4 * c:4 * c + 4, t * P:t * P + r],
                                             bankA[b][:, :].rearrange("p (k i) -> p k i", k=4)[:, :, 0:r],
                                             ACT.Copy).then_inc(xT_hi, 1)
                    if t == min(1, ph.nt2 - 1):
                        split(ph, 1 if ph.pro else 16)
                if not ph.pro:
                    if not ph.next:
                        split(ph, 16)
                    split(ph, 17)
                    if ph.next:
                        split(ph, 18)
                    for t in range(ph.nt):
                        act.wait_ge(h_part, g * 2 * TPG + ph.nt + t + 1)
                        if t:
                            act.wait_ge(h_ss, g * TPG + t)
                        nc.scalar.activation(junk[0:ph.rows, :], h[0:ph.rows, t, :], ACT.Square,
                                             accum_out=ss[0:ph.rows, 8 + t:9 + t]).then_inc(h_ss, 1)
                    if ph.next:
                        split(ph, 19)
                if ph.next:
                    split(ph, o + 2)
                for t in range(max(ph.nt, ph.nt2)):
                    r = ph.rows2
                    if t < ph.nt2:
                        act.wait_ge(v_full, first + t + 1)
                        nc.scalar.activation(junk[0:r, 0:HALF], bankV[t][0:r, :], ACT.Square,
                                             accum_out=ss[0:r, 4 + t:5 + t]).then_inc(v_ss, 1)
                    if t < ph.nt:
                        if t:
                            act.wait_ge(lg_full, TPG * g + t)
                        for c in range(2):
                            b = full(act, ph, "hn", t, c)
                            nc.scalar.activation(hnT[:, 4 * c:4 * c + 4, 0:ph.rows],
                                                 bankA[b][:, :].rearrange("p (k i) -> p k i", k=4)[:, :, 0:ph.rows],
                                                 ACT.Copy).then_inc(a_free[b], 1)
                    if t < ph.nt2:
                        act.wait_ge(vf_ok, first + t + 1)
                        nc.scalar.activation(vn[0][0:r, t, :], vf[0:r, :], ACT.Copy).then_inc(vn_hi, 1)
                if not ph.next:
                    softmaxes(ph)
                    return
                split(ph, o + 3)

                def d_high(m):
                    act.wait_ge(d_ok, (g + 1) * 4 + m + 1)
                    if m >= 2:
                        full(act, ph, "pm", m - 2)
                    nc.scalar.activation(dd[0][:, m % 2, 0:n2], win[(m + 1) % 2][:, 0:n2], ACT.Copy).then_inc(d_hi, 1)

                def pa_high(m):
                    b = full(act, ph, "pm", m)
                    if m == 0 and not ph.pro:
                        act.wait_ge(h_out, 16 * (TPG * g + ph.nt))
                    nc.scalar.activation(pa[0][:, m, 0:n2], bankA[b][:, 0:n2], ACT.Copy,
                                         scale=pscale[:, m:m + 1]).then_inc(pa_hi, 1)
                d_high(0)
                d_high(1)
                split(PhaseOne(g + 1), 0)
                d_high(2)
                pa_high(0)
                d_high(3)
                pa_high(1)
                pa_high(2)
                pa_high(3)
            passes(act, body)

        @block.vector
        def _(dve):
            tt, ts, stt = nc.vector.tensor_tensor, nc.vector.tensor_scalar, nc.vector.scalar_tensor_tensor
            lo = lambda out, x, hi: tt(out, x, hi.bitcast(F32), ALU.subtract)

            dve.wait_ge(setup, 12)
            for m in range(4):
                ts(corr[:, m, :], iota16[:, :], 1.0, float(2 << m), ALU.add, ALU.min)
            nc.vector.memset(hist[0][:, :, :], 0.0)
            dve.drain()
            nc.vector.reciprocal(corr[:, :, :], corr[:, :, :])
            dve.drain()
            for m in range(4):
                ts(corr[:, m, :], corr[:, m, :], float(2 << m), None, ALU.mult)
            dve.wait_ge(const_in, 16 * 12)
            dve.wait_ge(scattered, 16)
            dve.wait_ge(spare_out, 32)
            dve.wait_ge(const_ok, 1)
            lo(wp[1][:, :, :], wp_raw, wp[0][:, :, :])
            dve.wait_ge(const_ok, 2)
            lo(ws[1][:, :, :], bankC[:, :].rearrange("p (h i) -> p h i", h=4), ws[0][:, :, :])
            nc.vector.tensor_copy(hist[1][:, :, :], bankA[0][:, 0:64].rearrange("p (g i) -> p g i", g=4))\
                .then_inc(dve_setup, 1)

            def split(ph, i):
                par, n = ph.panel(i)
                for q in range(4):
                    dve.wait_ge(w_hi, 4 * n + q + 1)
                    last = lo(part(wl[par], q), part(raw[par], q), part(wh[par], q))
                last.then_inc(w_lo, 1)

            def mean(ss_sem, value, rows, col, width, done):
                dve.wait_ge(ss_sem, value)
                ts(ms[0:rows, col:col + 1], ss[0:rows, col:col + 1], 1.0 / width, EPS, ALU.mult, ALU.add)\
                    .then_inc(done, 1)

            def norm_x(ph):
                r, first = ph.rows2, (ph.g + 1) * TPG
                for t in range(ph.nt2):
                    mean(x_ss, first + t + 1, r, t, D, x_ms)
                for t in range(ph.nt2):
                    dve.wait_ge(x_rs, first + t + 1)
                    stt(xb[0:r, t, :], xb[0:r, t, :], rs[0:r, t:t + 1], gmix[0:r, :], ALU.mult, ALU.mult)\
                        .then_inc(x_scaled, 1)

            def rows_of_x(ph, t):
                r, num = ph.rows2, (ph.g + 1) * TPG + t
                for c in range(2):
                    b = full(dve, ph, "x", t, c)
                    dve.wait_ge(xT_hi, 2 * num + c + 1)
                    lo(xT[1][:, 4 * c:4 * c + 4, t * P:t * P + r],
                       bankA[b][:, :].rearrange("p (k i) -> p k i", k=4)[:, :, 0:r],
                       xT[0][:, 4 * c:4 * c + 4, t * P:t * P + r]).then_inc(a_free[b], 1)

            def add_residual(ph, half):
                r = ph.rows
                for t in range(ph.nt):
                    dve.wait_ge(res_in, 16 * (ph.g * TPG + ph.nt))
                    dve.wait_ge(o_full, ph.g * 2 * TPG + half * ph.nt + t + 1)
                    part = h[0:r, t, half * HALF:(half + 1) * HALF]
                    tt(part, bankV[t][0:r, :], part, ALU.add).then_inc(h_part, 1)

            def norm_h(ph, t):
                r, num = ph.rows, ph.g * TPG + t
                mean(h_ss, num + 1, r, 8 + t, D, h_ms)
                dve.wait_ge(h_rs, num + 1)
                if t >= 2:
                    dve.wait_ge(hn_out[t % 2], 16 + 32 * ph.g + 16)
                    full(dve, ph, "hn", t - 2, 1)
                stt(hn[0:r, t % 2, :], h[0:r, t, :], rs[0:r, 8 + t:9 + t], gffn[0:r, :], ALU.mult, ALU.mult)\
                    .then_inc(hn_ok, 1)

            def norm_v(ph, t):
                r, num = ph.rows2, (ph.g + 1) * TPG + t
                mean(v_ss, num + 1, r, 4 + t, HALF, v_ms)
                dve.wait_ge(v_rs, num + 1)
                stt(vf[0:r, :], bankV[t][0:r, :], rs[0:r, 4 + t:5 + t], gv[0:r, :], ALU.mult, ALU.mult)\
                    .then_inc(vf_ok, 1)
                dve.wait_ge(vn_hi, num + 1)
                lo(vn[1][0:r, t, :], vf[0:r, :], vn[0][0:r, t, :]).then_inc(vn_ok, 1)

            def logits(ph, t):
                r = ph.rows
                dve.wait_ge(lg_full, ph.g * TPG + t + 1)
                tt(lg[0:r, t, 0:4], bankR[0:r, 0:4], br[0:r, 0:4], ALU.add)
                tt(lg[0:r, t, 8:24], bankR[0:r, 4:20], br[0:r, 4:20], ALU.add).then_inc(lg_ok, 1)

            def take_a(ph, m):
                hs = hist[1] if ph.n2 == SAMPLE else hist[0]
                b = full(dve, ph, "a", m)
                nc.vector.tensor_copy(ext[:, 0:16], hs[:, m, :])
                nc.vector.tensor_copy(ext[:, 16:16 + ph.n2], bankA[b][:, 0:ph.n2]).then_inc(a_free[b], 1)

            def pooled(ph, m):
                hs, n2 = (hist[1] if ph.n2 == SAMPLE else hist[0]), ph.n2
                end, src = n2 + 16, ext
                for level in range(m + 1):
                    s, dst = 1 << level, win[level % 2]
                    dve.drain()
                    tt(dst[:, 2 * s:end], src[:, 2 * s:end], src[:, s:end - s], ALU.add)
                    src = dst
                nc.vector.tensor_copy(hs[:, m, :], ext[:, n2:end])
                dve.drain()
                if ph.pro:
                    tt(src[:, 16:32], src[:, 16:32], corr[:, m, :], ALU.mult)
                    dve.drain()
                d = win[(m + 1) % 2][:, 0:n2]
                stt(d, src[:, 16:end], 1.0 / (2 << m), ext[:, 16:end], ALU.mult, ALU.subtract).then_inc(d_ok, 1)
                dve.wait_ge(d_hi, (ph.g + 1) * 4 + m + 1)
                lo(dd[1][:, m % 2, 0:n2], d, dd[0][:, m % 2, 0:n2]).then_inc(d_lo, 1)

            def pa_low(ph, m):
                b = full(dve, ph, "pm", m)
                dve.wait_ge(pa_hi, (ph.g + 1) * 4 + m + 1)
                stt(pa[1][:, m, 0:ph.n2], bankA[b][:, 0:ph.n2], pscale[:, m:m + 1], pa[0][:, m, 0:ph.n2].bitcast(F32),
                    ALU.mult, ALU.subtract).then_inc(a_free[b], 1)

            def spatial(ph, t):
                r = ph.rows2
                dve.wait_ge(sp_full, (ph.g + 1) * TPG + t + 1)
                tt(S[:, :, t * P:t * P + r], bankV[t][:, :].rearrange("p (h i) -> p h i", h=4)[:, :, 0:r],
                   bsp[:, :, 0:r], ALU.add).then_inc(sp_read, 1)

            def choose(ph):
                r, ts_ = ph.rows, range(ph.nt)
                dve.drain()
                for t in ts_:
                    nc.vector.max(best[0:r, t, :], lg[0:r, t, 0:8])
                dve.drain()
                for t in ts_:
                    nc.vector.max_index(besti[0:r, t, :], best[0:r, t, :], lg[0:r, t, 0:8])
                dve.drain()
                for t in ts_:
                    nc.vector.tensor_copy(gidx[0:r, t:t + 1], besti[0:r, t, 0:1])
                tt(exps[0:r, 0:ph.nt, 0:NG], lg[0:r, 0:ph.nt, 0:NG],
                   best[0:r, 0:ph.nt, 0:1].broadcast_to([r, ph.nt, NG]), ALU.subtract)
                dve.drain()
                for t in ts_:
                    ts(inside[0:r, t, :], iota16[0:r, 0:NG], gidx[0:r, t:t + 1], None, ALU.is_equal)
                dve.drain()
                ts(pen[0:r, :, :], inside[0:r, :, :], -NEG, NEG, ALU.mult, ALU.add)
                for t in ts_:
                    wide = inside[0:r, t, :].unsqueeze(2).broadcast_to([r, NG, EPG])
                    tt(el[0:r, t, :].rearrange("p (a b) -> p a b", a=NG),
                       lg[0:r, t, 8:24].rearrange("p (a b) -> p a b", a=NG), wide, ALU.mult)
                dve.drain()
                for t in ts_:
                    wide = pen[0:r, t, :].unsqueeze(2).broadcast_to([r, NG, EPG])
                    part = el[0:r, t, :].rearrange("p (a b) -> p a b", a=NG)
                    tt(part, part, wide, ALU.add)
                dve.drain()
                for t in ts_:
                    nc.vector.max(best[0:r, t, :], el[0:r, t, :])
                dve.drain()
                for t in ts_:
                    nc.vector.max_index(besti[0:r, t, :], best[0:r, t, :], el[0:r, t, :])
                dve.drain()
                nt = ph.nt
                nc.vector.tensor_copy(rec[0:r, 0:nt, :], besti[0:r, 0:nt, 0:2])
                tt(exps[0:r, 0:nt, NG:NG + 1], best[0:r, 0:nt, 1:2], best[0:r, 0:nt, 0:1], ALU.subtract)\
                    .then_inc(exps_in, 1)
                dve.drain()
                for t in ts_:
                    for c in range(2):
                        ts(mask[0:r, c, t, :], iota16[0:r, :], rec[0:r, t, c:c + 1], None, ALU.is_equal)
                dve.drain()
                tt(msum[0:r, 0:nt, :], mask[0:r, 0, 0:nt, :], mask[0:r, 1, 0:nt, :], ALU.add).then_inc(mask_ok, 1)

            def place(ph):
                r, nt, g = ph.rows, ph.nt, ph.g
                dve.wait_ge(cum_full, g + 1)
                for t in range(nt):
                    tt(rank[0:r, t, :], bankC[0:r, t * NE:(t + 1) * NE], running[0:r, :], ALU.add)
                    dve.drain()
                    tt(running[:, :], bankC[:, 64 + t * NE:64 + (t + 1) * NE], running[:, :], ALU.add)
                    dve.drain()
                for c in range(2):
                    tt(prod[0:r, c, 0:nt, :], mask[0:r, c, 0:nt, :], rank[0:r, 0:nt, :], ALU.mult)
                dve.drain()
                for c in range(2):
                    nc.vector.reduce_sum(dest_f[0:r, c, 0:nt], prod[0:r, c, 0:nt, :], axis=AX)
                dve.drain()
                nc.vector.tensor_copy(low7[0:r, :, 0:nt], dest_f[0:r, :, 0:nt])
                dve.wait_ge(exps_ok, g + 1)
                second = exps[0:r, 0:nt, NG:NG + 1].rearrange("p t o -> p (t o)")
                nc.vector.reduce_sum(parts[0:r, 0, 0:nt], exps[0:r, 0:nt, 0:NG], axis=AX)
                ts(parts[0:r, 1, 0:nt], second, 1.0, None, ALU.add)
                dve.drain()
                ts(high7[0:r, :, 0:nt], low7[0:r, :, 0:nt], 7, None, ALU.logical_shift_right)
                dve.drain()
                ts(low7[0:r, :, 0:nt], low7[0:r, :, 0:nt], P - 1, None, ALU.bitwise_and)
                tt(parts[0:r, 0, 0:nt], parts[0:r, 0, 0:nt], parts[0:r, 1, 0:nt], ALU.mult)
                dve.drain()
                stt(dest_f[0:r, :, 0:nt], low7[0:r, :, 0:nt], float(NSLOT), high7[0:r, :, 0:nt], ALU.mult, ALU.add)
                nc.vector.reciprocal(parts[0:r, 0, 0:nt], parts[0:r, 0, 0:nt])
                wait_apart(dve, scattered, 16 + 32 * TPG * g, passed_dve)
                dve.drain()
                which = slice(g * TPG, g * TPG + nt) if isinstance(g, int) else bass.ds(g * TPG, TPG)
                weight = pay[0:r, :, 0:nt, 1:2].rearrange("p c t o -> p c (t o)").bitcast(F32)
                for c in range(2):
                    nc.vector.tensor_copy(pay[:, c, 0:nt, 0:1].rearrange("p t o -> p (t o)"), tok_all[:, which])
                nc.vector.tensor_copy(weight[:, 0, :], parts[0:r, 0, 0:nt])
                tt(weight[:, 1, :], parts[0:r, 0, 0:nt], second, ALU.mult)
                for c in range(2):
                    last = stt(dest[0:r, c, 0:nt], rec[0:r, 0:nt, c], float(BPE), dest_f[0:r, c, 0:nt],
                               ALU.mult, ALU.add)
                last.then_inc(dest_ok, 1)

            def body(ph):
                g, n = ph.g, ph.n
                o = 0 if ph.pro else 18
                if ph.pro:
                    split(ph, 0)
                    norm_x(ph)
                else:
                    for i in range(2):
                        split(ph, i + 1)
                        for m in (2 * i, 2 * i + 1):
                            b = full(dve, ph, "u", m)
                            t1 = win[m % 2][:, 0:n]
                            if m == 0:
                                dve.wait_ge(sp_read, g * TPG + ph.nt)
                            tt(t1, bankA[b][:, 0:n], S[:, m, 0:n], ALU.mult).then_inc(a_free[b], 1)
                            dve.wait_ge(pb_hi, g * 4 + m + 1)
                            lo(pb[1][:, m, 0:n], t1, pb[0][:, m, 0:n]).then_inc(pb_ok, 1)
                    for i in range(4):
                        split(ph, 3 + 3 * i)
                        if ph.prev and i == 1:
                            choose(ph.prev)
                        if ph.prev and i == 2:
                            place(ph.prev)
                        if i == 3:
                            norm_x(ph)
                        split(ph, 4 + 3 * i)
                        split(ph, 5 + 3 * i)
                        for c in range(2):
                            m = 2 * i + c
                            for kind, (gate, name) in enumerate((("ga", "P"), ("gb", "Q"))):
                                freed(dve, ph, gate, m)
                                b = full(dve, ph, name, m)
                                part = S[:, 2 * kind + c, 0:n]
                                tt(part, bankA[b][:, 0:n], part, ALU.mult).then_inc(a_free[b], 1)
                            dve.drain()
                            t1 = win[m % 2][:, 0:n]
                            tt(t1, S[:, c, 0:n], S[:, 2 + c, 0:n], ALU.add).then_inc(mix_ok, 1)
                            dve.wait_ge(mg_hi, g * 8 + m + 1)
                            lo(mg[1][:, m, 0:n], t1, mg[0][:, m, 0:n]).then_inc(mg_ok, 1)
                    split(ph, 15)
                for t in range(ph.nt2):
                    rows_of_x(ph, t)
                    if t == min(1, ph.nt2 - 1):
                        split(ph, 1 if ph.pro else 16)
                if not ph.pro:
                    if not ph.next:
                        split(ph, 16)
                    add_residual(ph, 0)
                    split(ph, 17)
                    if ph.next:
                        split(ph, 18)
                    add_residual(ph, 1)
                    for t in range(ph.nt):
                        if t == min(2, ph.nt) and ph.next:
                            split(ph, 19)
                        norm_h(ph, t)
                if ph.next:
                    split(ph, o + 2)
                for t in range(max(ph.nt, ph.nt2)):
                    if t < ph.nt2:
                        norm_v(ph, t)
                    if t < ph.nt and (t < ph.nt - 1 or not ph.next):
                        logits(ph, t)
                if not ph.next:
                    choose(ph)
                    place(ph)
                    return
                split(ph, o + 3)
                if ph.nt:
                    logits(ph, ph.nt - 1)
                take_a(ph, 0)
                pooled(ph, 0)
                take_a(ph, 1)
                pooled(ph, 1)
                split(PhaseOne(g + 1), 0)
                take_a(ph, 2)
                pooled(ph, 2)
                pa_low(ph, 0)
                take_a(ph, 3)
                pooled(ph, 3)
                pa_low(ph, 1)
                pa_low(ph, 2)
                for t in range(ph.nt2):
                    spatial(ph, t)
                pa_low(ph, 3)
            passes(dve, body)
            for c in range(2):
                dve.wait_ge(hist_full, c + 1)
                nc.vector.tensor_copy(histT[:, c, :], (bankA[0], bankA[1])[c][0:16, :]).then_inc(hist_ok, 1)

        @block.tensor
        def _(pe):
            pe.wait_ge(setup, 12)
            pe.wait_ge(const_in, 16 * 12)
            for m in range(4):
                nc.tensor.transpose(bankA[0][:, 16 * m:16 * m + 16], state[:, m * P:(m + 1) * P], ident[0:16, 0:16])
            for hd in range(4):
                last = nc.tensor.transpose(bankC[:, hd * P:(hd + 1) * P], wsp_raw[:, hd, :], ident[:, :])
            last.then_inc(const_tr, 1)
            pe.wait_ge(dve_setup, 1)

            def take(ph, *key):
                b, q = ph.use(*key)
                wait(pe, a_free[b], q)
                return b

            def rows_of_x(ph, t):
                r, num = ph.rows2, (ph.g + 1) * TPG + t
                pe.wait_ge(x_scaled, num + 1)
                for c in range(2):
                    b = take(ph, "x", t, c)
                    for k in range(4):
                        last = nc.tensor.transpose(bankA[b][:, k * P:k * P + r],
                                                   xb[0:r, t, (4 * c + k) * P:(4 * c + k + 1) * P],
                                                   ident[0:r, 0:r])
                    last.then_inc(a_full[b], 1)

            def start_panel(ph, i):
                par, n = ph.panel(i)
                pe.wait_ge(w_lo, n + 1)
                return wh[par], wl[par]

            def chunk(ph, i, c, name, m, src, ks, n):
                wh_, wl_ = start_panel(ph, i)
                b = take(ph, name, m)
                cols = slice(c * P, (c + 1) * P)
                return products(nc, bankA[b][:, 0:n],
                                [((wh_[:, kw, cols], wl_[:, kw, cols]), (src[0][:, ka, 0:n], src[1][:, ka, 0:n]))
                                 for kw, ka in ks]).then_inc(a_full[b], 1)

            def token_major(ph, i, t, src, k0, rows, n_acc):
                wh_, wl_ = start_panel(ph, i)
                view = lambda w: w[:, :, :].rearrange("p (k a) n -> p k (a n)", a=2)
                cols = slice(t * P, t * P + rows)
                last = None
                for k in range(4):
                    ah, al = src[0][:, k0 + k, cols], src[1][:, k0 + k, cols]
                    wh4, wl4 = view(wh_)[:, k, :], view(wl_)[:, k, :]
                    out = bankV[t][0:rows, :]
                    nc.tensor.matmul(out, ah, wh4, start=(n_acc == 0 and k == 0), stop=False)
                    nc.tensor.matmul(out, ah, wl4, start=False, stop=False)
                    last = nc.tensor.matmul(out, al, wh4, start=False, stop=(n_acc == 1 and k == 3))
                return last

            def transpose_hn(ph, t):
                r = ph.rows
                pe.wait_ge(hn_ok, ph.g * TPG + t + 1)
                for c in range(2):
                    b = take(ph, "hn", t, c)
                    for k in range(4):
                        last = nc.tensor.transpose(bankA[b][:, k * P:k * P + r],
                                                   hn[0:r, t % 2, (4 * c + k) * P:(4 * c + k + 1) * P],
                                                   ident[0:r, 0:r])
                    last.then_inc(a_full[b], 1)

            def router(ph, t):
                r = ph.rows
                freed(pe, ph, "hn", t, 0)
                freed(pe, ph, "hn", t, 1)
                if t:
                    pe.wait_ge(lg_ok, ph.g * TPG + t)
                for k in range(KD):
                    last = nc.tensor.matmul(bankR[0:r, 0:20], hnT[:, k, 0:r], wr[:, k, :], start=(k == 0),
                                            stop=(k == KD - 1))
                last.then_inc(lg_full, 1)

            def count(ph):
                r, w = ph.rows, ph.nt * NE
                pe.wait_ge(mask_ok, ph.g + 1)
                flat = msum[0:r, 0:ph.nt, :].rearrange("p t e -> p (t e)")
                nc.tensor.matmul(bankC[0:r, 0:w], upper[0:r, 0:r], flat, start=True, stop=True)
                nc.tensor.matmul(bankC[:, 64:64 + w], ones[0:r, :], flat, start=True, stop=True).then_inc(cum_full, 1)

            def pool_products(ph, m):
                pe.wait_ge(d_lo, (ph.g + 1) * 4 + m + 1)
                b = take(ph, "pm", m)
                products(nc, bankA[b][:, 0:ph.n2],
                         [((wp[0][:, m, :], wp[1][:, m, :]), (dd[0][:, m % 2, 0:ph.n2], dd[1][:, m % 2, 0:ph.n2]))])\
                    .then_inc(a_full[b], 1)

            def spatial(ph, t):
                r = ph.rows2
                pe.wait_ge(vn_ok, (ph.g + 1) * TPG + t + 1)
                for hd in range(4):
                    cols = slice(hd * P, (hd + 1) * P)
                    last = products(nc, bankV[t][:, hd * P:hd * P + r],
                                    [((vn[0][0:r, t, cols], vn[1][0:r, t, cols]),
                                      (ws[0][0:r, hd, 0:r], ws[1][0:r, hd, 0:r]))])
                last.then_inc(sp_full, 1)

            def body(ph):
                g, n, n2 = ph.g, ph.n, ph.n2
                o = 0 if ph.pro else 18
                every = [(k, k) for k in range(KD)]
                if not ph.pro:
                    for i in range(2):
                        for c in range(2):
                            chunk(ph, i, c, "u", 2 * i + c, xT, every, n)
                    for i in range(4):
                        for kind, name in enumerate(("ga", "gb")):
                            for c in range(2):
                                chunk(ph, 2 + 3 * i + kind, c, name, 2 * i + c, xT, every, n)
                        pe.wait_ge(pb_ok, g * 4 + 4)
                        for c in range(2):
                            chunk(ph, 4 + 3 * i, c, "P", 2 * i + c, pa, [(k, k) for k in range(4)], n)
                            chunk(ph, 4 + 3 * i, c, "Q", 2 * i + c, pb, [(4 + k, k) for k in range(4)], n)
                        if ph.prev and i == 1:
                            count(ph.prev)
                    pe.wait_ge(mg_ok, g * 8 + 4)
                    pe.wait_ge(sp_read, g * TPG + ph.nt)
                    for t in range(ph.nt):
                        last = token_major(ph, 14, t, mg, 0, ph.rows, 0)
                    last.then_inc(half_used, 1)
                    pe.wait_ge(mg_ok, g * 8 + 8)
                    for t in range(max(ph.nt, ph.nt2)):
                        if t < ph.nt2:
                            rows_of_x(ph, t)
                        if t < ph.nt:
                            token_major(ph, 15, t, mg, 4, ph.rows, 1).then_inc(o_full, 1)
                    for t in range(ph.nt):
                        pe.wait_ge(h_part, g * 2 * TPG + t + 1)
                        last = token_major(ph, 16, t, mg, 0, ph.rows, 0)
                    last.then_inc(half_used, 1)
                    for t in range(ph.nt):
                        token_major(ph, 17, t, mg, 4, ph.rows, 1).then_inc(o_full, 1)
                else:
                    for t in range(ph.nt2):
                        rows_of_x(ph, t)
                if ph.next:
                    freed(pe, ph, "x", ph.nt2 - 1, 0)
                    freed(pe, ph, "x", ph.nt2 - 1, 1)
                    for t in range(ph.nt2):
                        if not ph.pro:
                            pe.wait_ge(h_part, g * 2 * TPG + TPG + t + 1)
                        last = token_major(ph, o, t, xT, 0, ph.rows2, 0)
                    last.then_inc(half_used, 1)
                for t in range(max(ph.nt, ph.nt2)):
                    if t < ph.nt2:
                        token_major(ph, o + 1, t, xT, 4, ph.rows2, 1).then_inc(v_full, 1)
                    if 0 < t < ph.nt:
                        router(ph, t - 1)
                    if t < ph.nt:
                        transpose_hn(ph, t)
                if not ph.next:
                    router(ph, 0)
                    count(ph)
                    return
                chunk(ph, o + 2, 0, "a", 0, xT, every, n2)
                if ph.nt:
                    router(ph, ph.nt - 1)
                chunk(ph, o + 2, 1, "a", 1, xT, every, n2)
                chunk(ph, o + 3, 0, "a", 2, xT, every, n2)
                pool_products(ph, 0)
                chunk(ph, o + 3, 1, "a", 3, xT, every, n2)
                pool_products(ph, 1)
                for t in range(ph.nt2):
                    spatial(ph, t)
                    if t == min(1, ph.nt2 - 1):
                        pool_products(ph, 2)
                pool_products(ph, 3)
            passes(pe, body)
            for c in range(2):
                pe.wait_ge(a_free[c], (N_USES + 1 - c) // 2)
                for m in range(4):
                    last = nc.tensor.transpose((bankA[0], bankA[1])[c][0:16, m * P:(m + 1) * P], hist[c][:, m, :],
                                               ident[:, :])
                last.then_inc(hist_full, 1)

        block_stack.close()


def phase_three(nc, v):
    sem, psum, ident, running, iota16 = (v[k] for k in ("sem", "psum", "ident", "running", "iota16"))
    blk_tab, hn_dram, slot_dram, h_dram = v["blk_tab"], v["hn_dram"], v["slot_dram"], v["h_dram"]
    bankG, bankU, bankY = psum[0], psum[1:3], psum[3:5]
    bankX, bankH = psum[5:7], [psum[7], psum[0]]

    stack = ExitStack()
    with stack:
        sb = v["tiles"](stack)
        raw_gu = sb("raw_gu", [P, 2 * KD, HALF])
        raw_d = sb("raw_d", [P, KH, D])
        gu = [sb("gu_hi", [P, 2 * KD, HALF], F32R), sb("gu_lo", [P, 2 * KD, HALF], F32R)]
        dn = [sb("dn_hi", [P, KH, D], F32R), sb("dn_lo", [P, KH, D], F32R)]
        x = sb("x_rows", [P, D])
        xT = [sb("ex_hi", [P, KD, P], F32R), sb("ex_lo", [P, KD, P], F32R)]
        sg = sb("sg", [P, HALF])
        hid = sb("hid", [P, HALF])
        hT = [sb("hT_hi", [P, KH, P], F32R), sb("hT_lo", [P, KH, P], F32R)]
        y = sb("y_rows", [P, D])
        slots = sb("slots", [P, NSLOT, 2], I32)
        idx = sb("idx", [P, 2], I32)
        idx_1 = sb("idx_1", [P, 2], I32)
        idx_2 = sb("idx_2", [P, 2], I32)
        idx_out = sb("idx_out", [P, 2], I32)
        spare = sb("spare", [P, 2])
        blk_f = sb("blk_f", [P, NE])
        blk_i = sb("blk_i", [P, NE], I32)
        sums = [sb("sums0", [P, NE]), sb("sums1", [P, NE])]

        passed_pool = sem("passed_pool3")
        tab_ok = sem("tab_ok")
        gate_in, up_in, down_in = sem("gate_in"), sem("up_in"), sem("down_in")
        spare_ok = sem("spare_ok")
        moved = sem("moved")
        e_hi, e_lo = sem("e_hi"), sem("e_lo")
        idx_ok, x_rows_in = sem("idx_ok"), sem("x_rows_in")
        x_tr = sem("x_tr")
        ex_hi, ex_lo = sem("ex_hi"), sem("ex_lo")
        g_done, u1_done, sg_ok, hid_ok = (sem(n) for n in ("g_done", "u1_done", "sg_ok", "hid_ok"))
        gu_done = sem("gu_done")
        th_done, hT_hi = sem("th_done"), sem("hT_hi")
        hT_lo = sem("hT_lo")
        y_done = sem("y_done")
        y_read = sem("y_read")
        y_out = sem("y_out")

        def experts(eng, per_expert, per_block, peel=False):
            with eng.Fori(0, NE) as e:
                lo = eng.value_load(blk_tab[0:1, bass.ds(e, 1)], min_val=0, max_val=MAXBLK - 1)
                hi = eng.value_load(blk_tab[0:1, bass.ds(e + NE, 1)], min_val=1, max_val=MAXBLK)
                per_expert(e, lo)
                if peel:
                    per_block(e, lo, lo, True)
                with eng.Fori(lo + 1 if peel else lo, hi) as j:
                    per_block(e, lo, j)

        with nc.Block() as block:

            @block.sync
            def _(sp):

                def load(e, first):
                    which = slice(0, 1) if first else bass.ds(e, 1)
                    view = lambda w: w[0, which, :, :].rearrange("a (k p) f -> p (a k) f", p=P)
                    if not first:
                        sp.wait_ge(e_lo, SPLITS * e + (KD - SPLITS))
                    sp.dma_start(raw_gu[:, 0:KD, :], view(v["w_gate"])).then_inc(gate_in, 16)
                    if not first:
                        sp.wait_ge(e_lo, SPLITS * e + (2 * KD - SPLITS))
                    sp.dma_start(raw_gu[:, KD:2 * KD, :], view(v["w_up"])).then_inc(up_in, 16)
                    if not first:
                        sp.wait_ge(e_lo, SPLITS * e)
                    sp.dma_start(raw_d[:, :, :], view(v["w_down"])).then_inc(down_in, 16)
                load(0, True)
                with sp.Fori(1, NE) as e:
                    load(e, False)

            @block.gpsimd
            def _(pool):
                pool.dma_start(slots[:, :, :], slot_dram.rearrange("(p n) o -> p n o", p=P)).then_inc(y_out, 16)
                nc.gpsimd.memset(spare[:, :], 0.0).then_inc(spare_ok, 1)
                for c in range(2):
                    nc.gpsimd.memset(y[:, c * HALF:(c + 1) * HALF], 0.0).then_inc(y_read, 1)
                for tile in (idx, idx_1):
                    nc.gpsimd.iota(tile[:, 0:1], pattern=[[0, 1]], base=SEQ + SAMPLE, channel_multiplier=1)\
                        .then_inc(spare_ok, 1)
                    nc.gpsimd.memset(tile[:, 1:2], 0).then_inc(spare_ok, 1)
                nc.gpsimd.memset(sg[:, :], 0.0).then_inc(x_tr, 1)
                pool.wait_ge(spare_ok, 5)
                pool.wait_ge(y_out, 16)
                pool.wait_ge(tab_ok, 1)

                def fetch_and_add(col, j):
                    wait_apart(pool, x_tr, j + 1, passed_pool)
                    nc.gpsimd.tensor_copy(idx_2[:, :], idx_1[:, :]).then_inc(moved, 1)
                    wait_apart(pool, moved, 3 * j + 1, passed_pool)
                    nc.gpsimd.tensor_copy(idx_1[:, :], idx[:, :]).then_inc(moved, 1)
                    wait_apart(pool, moved, 3 * j + 2, passed_pool)
                    if col is not None:
                        nc.gpsimd.tensor_copy(idx[:, :], slots[:, col, :].rearrange("p n o -> p (n o)"))\
                            .then_inc(idx_ok, 1)
                        wait_apart(pool, idx_ok, j + 1, passed_pool)
                        nc.gpsimd.indirect_dma_start(out=x[:, :], out_offset=None, in_=hn_dram,
                                                     in_offset=bass.IndirectOffsetOnAxis(ap=idx[:, 0:1], axis=0))\
                            .then_inc(x_rows_in, 16)
                    wait_apart(pool, y_out, 16 * j + 16, passed_pool)
                    nc.gpsimd.tensor_copy(idx_out[:, :], idx_2[:, :]).then_inc(moved, 1)
                    wait_apart(pool, moved, 3 * j + 3, passed_pool)
                    wait_apart(pool, y_read, 2 * j + 2, passed_pool)
                    nc.gpsimd.indirect_dma_start(out=h_dram, in_=y[:, :], in_offset=None, compute_op=ALU.add,
                                                 out_offset=bass.IndirectOffsetOnAxis(ap=idx_out[:, 0:1], axis=0))\
                        .then_inc(y_out, 16)

                def per_block(e, lo, j):
                    col = nc.s_assert_within(pool.snap(e * BPE + j - lo), 0, NSLOT - 1,
                                              skip_runtime_bounds_check_because="an expert has at most BPE blocks")
                    fetch_and_add(bass.ds(col, 1), j)
                experts(pool, lambda e, lo: None, per_block)
                total = pool.value_load(blk_tab[0:1, 2 * NE - 1:2 * NE], min_val=1, max_val=MAXBLK)
                fetch_and_add(slice(0, 1), total)
                fetch_and_add(None, total + 1)
                wait_apart(pool, y_out, 16 * total + 48, passed_pool)

            @block.scalar
            def _(act):
                act.wait_ge(spare_ok, 5)
                act.wait_ge(tab_ok, 1)

                def use_sigmoid_table(c):
                    nc.scalar.activation(spare[:, c:c + 1], spare[:, c:c + 1], ACT.Sigmoid)

                def rows_high(count, j2):
                    act.wait_ge(x_tr, count)
                    for c in range(2):
                        nc.scalar.activation(xT[0][:, 4 * c:4 * c + 4, :],
                                             bankX[c][:, :].rearrange("p (k i) -> p k i", k=4), ACT.Copy)\
                            .then_inc(ex_hi, 1)
                rows_high(2, None)

                def weigh(j):
                    act.wait_ge(y_done, j + 1)
                    act.wait_ge(moved, 3 * j + 6)
                    for c in range(2):
                        nc.scalar.activation(y[:, c * HALF:(c + 1) * HALF], bankY[c][:, :], ACT.Copy,
                                             scale=idx_out[:, 1:2].bitcast(F32)).then_inc(y_read, 1)

                def split(e, lo):
                    use_sigmoid_table(1)
                    act.wait_ge(gu_done, lo + 1)
                    act.wait_ge(gate_in, 16 * e + 16)
                    for k in range(2 * KD):
                        if k == KD:
                            act.wait_ge(up_in, 16 * e + 16)
                        if k == KD + 4:
                            weigh(lo)
                        nc.scalar.activation(gu[0][:, k, :], raw_gu[:, k, :], ACT.Copy).then_inc(e_hi, 1)

                def per_block(e, lo, j, first=False):
                    def down(k):
                        if not first:
                            return
                        if k == 0:
                            act.wait_ge(down_in, 16 * e + 16)
                        nc.scalar.activation(dn[0][:, k, :], raw_d[:, k, :], ACT.Copy).then_inc(e_hi, 1)

                    if not first:
                        use_sigmoid_table(0)
                        weigh(j)
                    act.wait_ge(g_done, j + 1)
                    nc.scalar.activation(sg[:, :], bankG[:, :], ACT.Sigmoid).then_inc(sg_ok, 1)
                    down(0)
                    act.wait_ge(th_done, 2 * j + 1)
                    nc.scalar.activation(hT[0][:, 0:2, :], bankH[0][:, 0:2 * P].rearrange("p (k i) -> p k i", k=2),
                                         ACT.Copy).then_inc(hT_hi, 1)
                    down(1)
                    rows_high(j + 3, j)
                    down(2)
                    act.wait_ge(th_done, 2 * j + 2)
                    nc.scalar.activation(hT[0][:, 2:4, :], bankH[1][:, 0:2 * P].rearrange("p (k i) -> p k i", k=2),
                                         ACT.Copy).then_inc(hT_hi, 1)
                    down(3)
                experts(act, split, per_block, peel=True)
                total = act.value_load(blk_tab[0:1, 2 * NE - 1:2 * NE], min_val=1, max_val=MAXBLK)
                weigh(total)

            @block.vector
            def _(dve):
                tt, ts, stt = nc.vector.tensor_tensor, nc.vector.tensor_scalar, nc.vector.scalar_tensor_tensor
                copy = nc.vector.tensor_copy
                lo_half = lambda out, a, hi: tt(out, a, hi.bitcast(F32), ALU.subtract)

                for b in bankY:
                    last = nc.vector.memset(b[:, :], 0.0)
                last.then_inc(y_done, 1)
                ts(blk_i[:, :], running[:, :], float(P - 1), None, ALU.add)
                dve.drain()
                ts(blk_i[:, :], blk_i[:, :], 7, None, ALU.logical_shift_right)
                dve.drain()
                ts(blk_f[:, :], blk_i[:, :], 1.0, None, ALU.max)
                dve.drain()
                src = blk_f
                for n, step in enumerate((1, 2, 4, 8)):
                    dst = sums[n % 2]
                    tt(dst[:, step:], src[:, step:], src[:, :NE - step], ALU.add)
                    copy(dst[:, :step], src[:, :step])
                    dve.drain()
                    src = dst
                copy(blk_tab[:, NE:2 * NE], src[:, :])
                tt(blk_f[:, :], src[:, :], blk_f[:, :], ALU.subtract)
                dve.drain()
                copy(blk_tab[:, 0:NE], blk_f[:, :]).then_inc(tab_ok, 1)
                nc.vector.memset(sums[0][:, 0:1], 0.0).then_inc(hT_lo, 1)
                nc.vector.memset(sums[0][:, 1:2], 0.0).then_inc(gu_done, 1)

                def rows_low(count):
                    for c in range(2):
                        dve.wait_ge(ex_hi, count + c)
                        lo_half(xT[1][:, 4 * c:4 * c + 4, :], bankX[c][:, :].rearrange("p (k i) -> p k i", k=4),
                                xT[0][:, 4 * c:4 * c + 4, :]).then_inc(ex_lo, 1)
                rows_low(1)

                def split(e, lo):
                    for k in range(2 * KD):
                        dve.wait_ge(e_hi, SPLITS * e + k + 1)
                        lo_half(gu[1][:, k, :], raw_gu[:, k, :], gu[0][:, k, :]).then_inc(e_lo, 1)

                def hidden_low(c):
                    lo_half(hT[1][:, 2 * c:2 * c + 2, :], bankH[c][:, 0:2 * P].rearrange("p (k i) -> p k i", k=2),
                            hT[0][:, 2 * c:2 * c + 2, :]).then_inc(hT_lo, 1)

                def per_block(e, lo, j, first=False):
                    def down(k):
                        if first:
                            dve.wait_ge(e_hi, SPLITS * e + 2 * KD + k + 1)
                            lo_half(dn[1][:, k, :], raw_d[:, k, :], dn[0][:, k, :]).then_inc(e_lo, 1)

                    dve.wait_ge(sg_ok, j + 1)
                    tt(sg[:, :], bankG[:, :], sg[:, :], ALU.mult)
                    dve.drain()
                    dve.wait_ge(u1_done, j + 1)
                    tt(hid[:, 0:256], bankU[0][:, 0:256], sg[:, 0:256], ALU.mult).then_inc(hid_ok, 1)
                    down(0)
                    dve.wait_ge(hT_hi, 2 * j + 1)
                    hidden_low(0)
                    dve.wait_ge(gu_done, j + 2)
                    tt(hid[:, 256:512], bankU[1][:, 0:256], sg[:, 256:512], ALU.mult).then_inc(hid_ok, 1)
                    down(1)
                    rows_low(2 * j + 3)
                    down(2)
                    dve.wait_ge(hT_hi, 2 * j + 2)
                    hidden_low(1)
                    down(3)
                experts(dve, split, per_block, peel=True)

            @block.tensor
            def _(pe):
                def rows_of_x(count):
                    pe.wait_ge(x_rows_in, count)
                    for c in range(2):
                        for k in range(4):
                            last = nc.tensor.transpose(bankX[c][:, k * P:(k + 1) * P],
                                                       x[:, (4 * c + k) * P:(4 * c + k + 1) * P], ident[:, :])
                    last.then_inc(x_tr, 1)

                pe.wait_ge(tab_ok, 1)
                rows_of_x(16)

                def accumulate(out, a, ka, w, kw, cols, n, total):
                    nc.tensor.matmul(out, a[0][:, ka, :], w[0][:, kw, cols], start=(n == 0), stop=False)
                    nc.tensor.matmul(out, a[0][:, ka, :], w[1][:, kw, cols], start=False, stop=False)
                    return nc.tensor.matmul(out, a[1][:, ka, :], w[0][:, kw, cols], start=False, stop=(n == total - 1))

                def hidden_transposed(c):
                    for k in range(2):
                        last = nc.tensor.transpose(bankH[c][:, k * P:(k + 1) * P],
                                                   hid[:, (2 * c + k) * P:(2 * c + k + 1) * P], ident[:, :])
                    last.then_inc(th_done, 1)

                def per_block(e, lo, j):
                    pe.wait_ge(ex_lo, 2 * j + 2)
                    pe.wait_ge(hT_lo, 2 * j + 1)
                    for k in range(KD):
                        pe.wait_ge(e_lo, SPLITS * e + k + 1)
                        last = accumulate(bankG[:, :], xT, k, gu, k, slice(0, HALF), k, KD)
                    last.then_inc(g_done, 1)
                    for k in range(KD):
                        pe.wait_ge(e_lo, SPLITS * e + KD + k + 1)
                        last = accumulate(bankU[0][:, 0:256], xT, k, gu, KD + k, slice(0, 256), k, KD)
                    last.then_inc(u1_done, 1)
                    for k in range(KD):
                        last = accumulate(bankU[1][:, 0:256], xT, k, gu, KD + k, slice(256, 512), k, KD)
                        if k == 4:
                            pe.wait_ge(hid_ok, 2 * j + 1)
                            hidden_transposed(0)
                    last.then_inc(gu_done, 1)
                    rows_of_x(16 * j + 32)
                    pe.wait_ge(y_read, 2 * j + 4)
                    pe.wait_ge(hT_lo, 2 * j + 2)
                    for k in range(KH):
                        pe.wait_ge(e_lo, SPLITS * e + 2 * KD + k + 1)
                        if k == 2:
                            pe.wait_ge(hT_lo, 2 * j + 3)
                        for half in range(2):
                            last = accumulate(bankY[half][:, :], hT, k, dn, k, slice(half * HALF, (half + 1) * HALF),
                                              k, KH)
                        if k == 0:
                            pe.wait_ge(hid_ok, 2 * j + 2)
                            hidden_transposed(1)
                    last.then_inc(y_done, 1)
                experts(pe, lambda e, lo: None, per_block)


def phase_four(nc, v):
    sem, h_dram = v["sem"], v["h_dram"]
    GROUPS = [(i * TPG * P, P, TPG) for i in range(NPROMPT)] + [(SEQ, SAMPLE, 1)]
    LAST = NPROMPT
    stack = ExitStack()
    with stack:
        sb = v["tiles"](stack)
        gf = sb("gf", [P, D])
        rows = [sb(f"final{i}", [P, tiles, D]) for i, (_, _, tiles) in enumerate(GROUPS)]
        out = sb("out", [P, NT, D])
        sq = sb("sq", [P, 2, D], BF16)
        ss = sb("ss4", [P, NT])
        ms = sb("ms4", [P, NT])
        rs = sb("rs4", [P, NT])
        half_neg = sb("half_neg4", [P, 1])
        gf_in, ss_ok, ms_ok, root_ok, out_ok, half_ok = (
            sem(n) for n in ("gf_in", "ss_ok", "ms_ok", "root_ok", "out_ok", "half_ok"))
        h_in = [sem(f"h_in{i}") for i in range((NT + 1) // 2)]
        stored = sem("stored")
        tiles_of = [(i, first, r, t) for i, (first, r, tiles) in enumerate(GROUPS) for t in range(tiles)]

        def rows_view(a, first, r, tiles):
            return a[first:first + tiles * r, :].rearrange("(t p) d -> p t d", p=r)

        with nc.Block() as block:
            @block.sync
            def _(sp):
                for i, (first, r, tiles) in enumerate(GROUPS):
                    for t0 in range(0, tiles, 2):
                        n = min(2, tiles - t0)
                        sp.dma_start(rows[i][0:r, t0:t0 + n, :], rows_view(h_dram, first + t0 * r, r, n))\
                            .then_inc(h_in[(i * TPG + t0) // 2], 16)
                    if i == 0:
                        sp.dma_start(gf[:, :], v["g_final"].rearrange("(a n) -> a n", a=1).broadcast_to([P, D]))\
                            .then_inc(gf_in, 16)

            @block.gpsimd
            def _(pool):
                nc.gpsimd.memset(half_neg[:, :], -0.5).then_inc(half_ok, 1)
                pool.wait_ge(half_ok, 1)
                for n, (i, first, r, t) in enumerate(tiles_of):
                    pool.wait_ge(ms_ok, n + 1)
                    nc.gpsimd.tensor_tensor(rs[0:r, n:n + 1], ms[0:r, n:n + 1], half_neg[0:r, :], ALU.pow)\
                        .then_inc(root_ok, 1)

            def store(act, n):
                i, first, r, t = tiles_of[n]
                act.wait_ge(out_ok, n + 1)
                to = v["y_prompt"][0, first + t * P:first + (t + 1) * P, :] if i < LAST else v["y_sample"][0, :, :]
                act.dma_start(to, out[0:r, n, :]).then_inc(stored, 16)

            @block.scalar
            def _(act):
                for n, (i, first, r, t) in enumerate(tiles_of):
                    act.wait_ge(h_in[n // 2], 16)
                    if n >= 2:
                        act.wait_ge(ss_ok, n - 1)
                    nc.scalar.activation(sq[0:r, n % 2, :], rows[i][0:r, t, :], ACT.Square,
                                         accum_out=ss[0:r, n:n + 1]).then_inc(ss_ok, 1)
                    if n >= 2:
                        store(act, n - 2)
                store(act, NT - 2)
                store(act, NT - 1)
                act.wait_ge(stored, 16 * NT)

            @block.vector
            def _(dve):
                def scale(n):
                    i, first, r, t = tiles_of[n]
                    dve.wait_ge(root_ok, n + 1)
                    nc.vector.scalar_tensor_tensor(out[0:r, n, :], rows[i][0:r, t, :], rs[0:r, n:n + 1],
                                                   gf[0:r, :], ALU.mult, ALU.mult).then_inc(out_ok, 1)
                dve.wait_ge(gf_in, 16)
                for n, (i, first, r, t) in enumerate(tiles_of):
                    dve.wait_ge(ss_ok, n + 1)
                    nc.vector.tensor_scalar(ms[0:r, n:n + 1], ss[0:r, n:n + 1], 1.0 / D, EPS, ALU.mult, ALU.add)\
                        .then_inc(ms_ok, 1)
                    if n:
                        scale(n - 1)
                scale(NT - 1)


_INS = ["x_prompt", "x_sample", "state_pool", "g_mix", "w_in", "w_pool", "pool_scale", "g_v", "w_spatial",
        "b_spatial", "w_up_pool", "w_up_gmlp", "w_out", "g_ffn", "w_group", "b_group", "w_router", "b_router",
        "w_gate", "w_up", "w_down", "g_final"]
_OUTS = [(1, SEQ, D), (1, SAMPLE, D), (1, 1, HIST, HALF), (1, 1, HIST, HALF), (1, 1, SAMPLE, HALF)]


def kernel(**inputs):
    import numpy as np
    import concourse.bacc as bacc
    from concourse.bass_utils import run_bass_kernel_spmd

    nc = bacc.Bacc("TRN2", target_bir_lowering=False, num_devices=1)
    arrays, args = {}, []
    for name in _INS:
        a = np.ascontiguousarray(inputs[name])
        arrays[f"in_{name}"] = a
        args.append(nc.dram_tensor(f"in_{name}", a.shape, mybir.dt.from_np(a.dtype), kind="ExternalInput").ap())
    for i, shape in enumerate(_OUTS):
        args.append(nc.dram_tensor(f"out_{i}", shape, F32, kind="ExternalOutput").ap())
    build(nc, *args)
    r = run_bass_kernel_spmd(nc, [arrays], core_ids=[0])
    return tuple(r.results[0][f"out_{i}"] for i in range(len(_OUTS)))
```

```python
from contextlib import ExitStack

import concourse.bass as bass
from concourse import mybir

F32 = mybir.dt.float32
F32R = mybir.dt.float32r
BF16 = mybir.dt.bfloat16
I32 = mybir.dt.int32
U32 = mybir.dt.uint32
ALU = mybir.AluOpType
ACT = mybir.ActivationFunctionType
AX = mybir.AxisListType.X

P = 128
D = 1024
KD = D // P
SEQ = 2048
SAMPLE = 32
HALF = 512
KH = HALF // P
IN_COLS = 3 * HALF + 2 * D
HIST = 15
GROUP = 512
TPG = GROUP // P
NPROMPT = SEQ // GROUP
NT = SEQ // P + 1
NG, EPG = 4, 4
NE = NG * EPG
BPE = (SEQ + SAMPLE + P - 1) // P
NSLOT = NE * BPE
MINBLK = 2
MAXBLK = (2 * (SEQ + SAMPLE)) // P + MINBLK * NE
EPS = 1e-6
NEG = -3.0e38

NPAN = 22
PRE = 4
SPLITS = 20
SPLITS_ACT = SPLITS - 1


def products(nc, out, pairs):
    n = len(pairs)
    last = None
    for i, ((lh, ll), (rh, rl)) in enumerate(pairs):
        nc.tensor.matmul(out, lh, rh, start=(i == 0), stop=False)
        nc.tensor.matmul(out, lh, rl, start=False, stop=False)
        last = nc.tensor.matmul(out, ll, rh, start=False, stop=(i == n - 1))
    return last


def bank_uses(nt, nt_next, first):
    seq = []
    if not first:
        seq += [("u", m) for m in range(4)]
        for i in range(4):
            seq += [("ga", 2 * i), ("ga", 2 * i + 1), ("gb", 2 * i), ("gb", 2 * i + 1)]
            seq += [("P", 2 * i), ("Q", 2 * i), ("P", 2 * i + 1), ("Q", 2 * i + 1)]
    seq += [("x", t, c) for t in range(nt_next) for c in range(2)]
    if not first:
        seq += [("hn", t, c) for t in range(nt) for c in range(2)]
    if nt_next:
        seq += [("a", 0), ("a", 1), ("a", 2)]
        seq += [("pm", 0), ("a", 3)] if nt_next > 1 else [("a", 3), ("pm", 0)]
        seq += [("pm", 1), ("pm", 2), ("pm", 3)]
    return {key: i for i, key in enumerate(seq)}, len(seq)


PRO_USES, N_PRO = bank_uses(0, TPG, True)
MID_USES, N_MID = bank_uses(TPG, TPG, False)
LAST_P_USES, N_LAST_P = bank_uses(TPG, 1, False)
SAM_USES, N_SAM = bank_uses(1, 0, False)
assert N_PRO % 2 == N_MID % 2 == 0
N_USES = N_PRO + (NPROMPT - 1) * N_MID + N_LAST_P + N_SAM


def wait_apart(eng, s, value, passed):
    eng.wait_ge(s, value)
    eng.sem_inc(passed, 1)


class PhaseOne:

    def __init__(self, g):
        self.g = g
        static = isinstance(g, int)
        self.pro = static and g < 0
        self.nt = 0 if self.pro else (1 if static and g == NPROMPT else TPG)
        self.n = SAMPLE if static and g == NPROMPT else GROUP
        self.rows = SAMPLE if static and g == NPROMPT else P
        self.next = not (static and g == NPROMPT)
        self.nt2 = 0 if not self.next else (1 if static and g == NPROMPT - 1 else TPG)
        self.n2 = SAMPLE if static and g == NPROMPT - 1 else GROUP
        self.rows2 = SAMPLE if static and g == NPROMPT - 1 else P
        before_last = N_PRO + (NPROMPT - 1) * N_MID
        if self.pro:
            self.uses, self.start = PRO_USES, 0
        elif static and g == NPROMPT:
            self.uses, self.start = SAM_USES, before_last + N_LAST_P
        elif static and g == NPROMPT - 1:
            self.uses, self.start = LAST_P_USES, before_last
        else:
            self.uses, self.start = MID_USES, (N_PRO + g * N_MID if static else None)
        self.before = None if self.pro else (
            (LAST_P_USES, N_LAST_P) if static and g == NPROMPT else (MID_USES, N_MID))

    @property
    def prev(self):
        return None if isinstance(self.g, int) and (self.g < 1 or self.g == NPROMPT) else PhaseOne(self.g - 1)

    @property
    def places_itself(self):
        return isinstance(self.g, int) and self.g >= NPROMPT - 1

    def use(self, *key):
        return self._place(self.uses[key])

    def use_before(self, *key):
        table, n = self.before
        return self._place(table[key] - n)

    def _place(self, i):
        if self.start is None:
            return i % 2, self.g * (N_MID // 2) + (N_PRO + i) // 2
        return (self.start + i) % 2, (self.start + i) // 2

    def panel(self, i):
        if self.pro:
            return i % 2, i
        return i % 2, self.g * NPAN + PRE + i


def build(nc, x_prompt, x_sample, state_pool, g_mix, w_in, w_pool, pool_scale, g_v, w_spatial, b_spatial,
          w_up_pool, w_up_gmlp, w_out, g_ffn, w_group, b_group, w_router, b_router, w_gate, w_up, w_down,
          g_final, y_prompt, y_sample, new_pool_prompt, new_pool_sample, new_v):
    outer = ExitStack()

    def sem(name):
        return outer.enter_context(nc.semaphore(name))

    def tiles(stack):
        def sb(name, shape, dt=F32):
            return stack.enter_context(nc.sbuf_tensor(name, shape, dt))
        return sb

    h_dram = nc.dram_tensor("h_rows", [SEQ + SAMPLE + P, D], F32).ap()
    hn_dram = nc.dram_tensor("hn_rows", [SEQ + SAMPLE + P, D], F32).ap()
    slot_dram = nc.dram_tensor("slot_table", [P * NSLOT, 2], I32).ap()

    with outer:
        keep = tiles(outer)
        ident = keep("ident", [P, P])
        running = keep("running", [P, NE])
        iota16 = keep("iota16", [P, NE])
        blk_tab = keep("blk_tab", [P, 2 * NE], I32)
        gate_in, up_in, gf_in = sem("gate_in"), sem("up_in"), sem("gf_in")
        psum = [outer.enter_context(nc.psum_tensor(f"bank{b}", [P, 512], F32)) for b in range(8)]

        with ExitStack() as early:
            raw_gu = tiles(early)("raw_gate_up", [P, 2 * KD, HALF])
            gf = tiles(early)("gf", [P, D])

        shared = dict(locals())
        phase_one(nc, shared)
        phase_three(nc, shared)
        phase_four(nc, shared)


def phase_one(nc, v):
    sem, psum, ident, running, iota16 = (v[k] for k in ("sem", "psum", "ident", "running", "iota16"))
    x_prompt, x_sample = v["x_prompt"], v["x_sample"]
    w_in, w_out = v["w_in"], v["w_out"]
    h_dram, hn_dram, slot_dram = v["h_dram"], v["hn_dram"], v["slot_dram"]
    bankA = [psum[5], psum[6]]
    bankR, bankC = psum[4], psum[7]
    bankV = psum[0:4]

    stack = ExitStack()
    with stack:
        sb = v["tiles"](stack)
        xT = [sb("xT_hi", [P, KD, GROUP], F32R), sb("xT_lo", [P, KD, GROUP], F32R)]
        mg = [sb("mg_hi", [P, KD, GROUP], F32R), sb("mg_lo", [P, KD, GROUP], F32R)]
        with ExitStack() as shared:
            s1 = v["tiles"](shared)
            pa = [s1("pa_hi", [P, KH, GROUP], F32R), s1("pa_lo", [P, KH, GROUP], F32R)]
            pb = [s1("pb_hi", [P, KH, GROUP], F32R), s1("pb_lo", [P, KH, GROUP], F32R)]
        assert TPG * D + 3 * D + KD * P == 4 * KH * GROUP
        h = sb("h", [P, TPG, D])
        hn = sb("hn", [P, 3, D])
        hnT = sb("hnT", [P, KD, P])
        raw = [sb("raw0", [P, 8, 256]), sb("raw1", [P, 8, 256])]
        wh = [sb("wh0", [P, 8, 256], F32R), sb("wh1", [P, 8, 256], F32R)]
        wl = [sb("wl0", [P, 8, 256], F32R), sb("wl1", [P, 8, 256], F32R)]
        xb = sb("xb", [P, TPG, D])
        S = sb("S", [P, 4, GROUP])
        vf = sb("vf", [P, HALF])
        vn = [m[:, 4:8, :] for m in mg]
        exts = [sb("ext0", [P, GROUP + 16]), sb("ext1", [P, GROUP + 16])]
        win = [sb("win0", [P, GROUP + 16]), sb("win1", [P, GROUP + 16])]
        dd = [m[:, 0:2, :] for m in mg]
        junk = sb("junk", [P, D], BF16)
        tm = junk[:, :].bitcast(F32).rearrange("p (a n) -> p a n", a=2)
        hist = [sb("hist_prompt", [P, 4, 16]), sb("hist_sample", [P, 4, 16])]
        state = exts[1][0:16, 0:HALF]
        corr = sb("corr", [P, 4, 16])
        wp_raw = win[0][:, 0:HALF].rearrange("p (g d) -> p g d", g=4)
        wsp_raw = win[1][:, 0:HALF].rearrange("p (g d) -> p g d", g=4)
        wp = [sb("wp_hi", [P, 4, P], F32R), sb("wp_lo", [P, 4, P], F32R)]
        ws = [sb("ws_hi", [P, 4, P], F32R), sb("ws_lo", [P, 4, P], F32R)]
        bsp = sb("bsp", [P, 4, P])
        gv = sb("gv", [P, HALF])
        gmix = sb("gmix", [P, D])
        gffn = sb("gffn", [P, D])
        pscale = sb("pscale", [P, 4])
        wr = sb("wr", [P, KD, 20])
        br = sb("br", [P, 20])
        upper = sb("upper", [P, P])
        ones = sb("ones", [P, P])
        half_neg = sb("half_neg", [P, 1])
        ss = sb("ss", [P, 12])
        ms = sb("ms", [P, 12])
        rs = sb("rs", [P, 12])
        lg = sb("lg", [P, TPG, 24])
        best = sb("best", [P, TPG, 8])
        besti = sb("besti", [P, TPG, 8], U32)
        inside = sb("inside", [P, TPG, NG])
        el = sb("el", [P, TPG, NE])
        gidx = sb("gidx", [P, TPG])
        mask = sb("mask", [P, 2, TPG, NE])
        msum = sb("msum", [P, TPG, NE])
        rank = sb("rank", [P, TPG, NE])
        prod = sb("prod", [P, 2, TPG, NE])
        pen = sb("pen", [P, TPG, NG])
        rec = sb("rec", [P, TPG, 2])
        exps = sb("exps", [P, TPG, NG + 1])
        parts = sb("parts", [P, 2, TPG])
        pay = sb("pay", [P, 2, TPG, 2], I32)
        dest_f = sb("dest_f", [P, 2, TPG])
        dest = sb("dest", [P, 2, TPG], I32)
        tok_all = sb("tok_all", [P, NT], I32)
        empty = S[:, 2:4, :].rearrange("p a n -> p (a n)")[:, 0:2 * NSLOT].rearrange("p (n o) -> p n o", o=2).bitcast(I32)
        zero_rows = S[:, 0:2, :].rearrange("p a n -> p (a n)")
        histT = xb[0:16, 0:2, 0:HALF]
        low7 = sb("low7", [P, 2, TPG], I32)
        high7 = sb("high7", [P, 2, TPG], I32)

        const_in, const_tr, const_ok, setup, dve_setup = (sem(s) for s in (
            "const_in", "const_tr", "const_ok", "setup", "dve_setup"))
        gmix_in, gv_in, tri_ok = sem("gmix_in"), sem("gv_in"), sem("tri_ok")
        x_first = [sem(f"x_first{t}") for t in range(TPG)]
        passed_pool, passed_dve = sem("passed_pool"), sem("passed_dve")
        raw_in = [sem("raw_in0"), sem("raw_in1")]
        w_hi, w_lo, half_used = sem("w_hi"), sem("w_lo"), sem("half_used")
        a_full = [sem("a0_full"), sem("a1_full")]
        a_free = [sem("a0_free"), sem("a1_free")]
        x_in = sem("x_in")
        ext_ok = sem("ext_ok")
        tm_full, tm_ok = sem("tm_full"), sem("tm_ok")
        sp_full, sp_read = sem("sp_full"), sem("sp_read")
        x_ss, x_ms, x_rs, x_scaled, xT_hi = (sem(s) for s in ("x_ss", "x_ms", "x_rs", "x_scaled", "xT_hi"))
        v_full, v_ss, v_ms, v_rs, vf_ok, vn_hi, vn_ok, v_out = (sem(s) for s in (
            "v_full", "v_ss", "v_ms", "v_rs", "vf_ok", "vn_hi", "vn_ok", "v_out"))
        d_ok, d_hi, d_lo, pa_hi = sem("d_ok"), sem("d_hi"), sem("d_lo"), sem("pa_hi")
        pb_hi, pb_ok = sem("pb_hi"), sem("pb_ok")
        mix_ok, mg_hi, mg_ok = sem("mix_ok"), sem("mg_hi"), sem("mg_ok")
        res_in, o_full, h_part, h_ss, h_ms, h_rs, hn_ok, h_out = (sem(s) for s in (
            "res_in", "o_full", "h_part", "h_ss", "h_ms", "h_rs", "hn_ok", "h_out"))
        hn_out = [sem("hn_out0"), sem("hn_out1")]
        exps_in, exps_ok, spare_out = sem("exps_in"), sem("exps_ok"), sem("spare_out")
        lg_full, lg_ok, mask_ok, cum_full, dest_ok, scattered = (sem(s) for s in (
            "lg_full", "lg_ok", "mask_ok", "cum_full", "dest_ok", "scattered"))
        hist_full, hist_ok, hist_out = sem("hist_full"), sem("hist_ok"), sem("hist_out")

        def win_view(c0, k0, nk, width):
            return w_in[0, k0 * P:(k0 + nk) * P, c0:c0 + width].rearrange("(k p) n -> p k n", p=P)

        def panel_sources(i, pro):
            whole = lambda r: r[:, :, :]
            wide = lambda r: r[:, :, :].rearrange("p (k a) n -> p k (a n)", a=2)
            if pro:
                i += NPAN - PRE
            if i < 2:
                return [(whole, win_view(HALF + i * 256, 0, 8, 256))]
            if i < 14:
                j, kind = (i - 2) // 3, (i - 2) % 3
                if kind < 2:
                    return [(whole, win_view(3 * HALF + kind * D + j * 256, 0, 8, 256))]
                view = lambda w: w[0, :, j * 256:(j + 1) * 256].rearrange("(k p) n -> p k n", p=P)
                return [(lambda r: r[:, 0:4, :], view(v["w_up_pool"])),
                        (lambda r: r[:, 4:8, :], view(v["w_up_gmlp"]))]
            if i < 18:
                half, kh = (i - 14) // 2, (i - 14) % 2
                return [(wide, w_out[0, kh * 512:(kh + 1) * 512, half * 512:(half + 1) * 512]
                         .rearrange("(k p) n -> p k n", p=P))]
            if i < 20:
                return [(wide, win_view(2 * HALF, 4 * (i - 18), 4, 512))]
            return [(whole, win_view((i - 20) * 256, 0, 8, 256))]

        def part(w, q):
            return w[:, 2 * q:2 * q + 2, :]

        def x_rows(ph, t):
            g = ph.g
            if isinstance(g, int) and g == NPROMPT:
                return x_sample[0, :, :]
            return x_prompt[0, bass.ds(g * GROUP + t * P, P), :]

        def passes(eng, body):
            body(PhaseOne(-1))
            body(PhaseOne(0))
            with eng.Fori(1, NPROMPT - 1) as g:
                body(PhaseOne(g))
            body(PhaseOne(NPROMPT - 1))
            body(PhaseOne(NPROMPT))

        def wait(eng, s, value):
            if not (isinstance(value, int) and value <= 0):
                eng.wait_ge(s, value)

        def tm_number(i, s):
            if i >= 20:
                return i - 20
            return 2 + i if i < 2 else 4 + 4 * ((i - 2) // 3) + (i - 2) % 3 + s

        def tm_bank(i, s):
            q = tm_number(i, s)
            return bankV[q % 2 + (2 if i >= 20 else 0)]

        def full(eng, ph, *key):
            b, q = ph.use(*key)
            eng.wait_ge(a_full[b], q + 1)
            return b

        def freed(eng, ph, *key):
            b, q = ph.use(*key)
            eng.wait_ge(a_free[b], q + 1)

        def panel_done(eng, ph, i):
            if ph.pro:
                i += 18
            if i < 0:
                b, q = ph.use_before("a", 5 + 2 * i)
            elif i < 2:
                b, q = ph.use("u", 2 * i + 1)
            elif i < 14:
                b, q = ph.use(("ga", "gb", "Q")[(i - 2) % 3], 2 * ((i - 2) // 3) + 1)
            elif i in (14, 16, 18):
                eng.wait_ge(half_used, 3 * ph.g + 2 + (i - 14) // 2)
                return
            elif i in (15, 17):
                eng.wait_ge(o_full, ph.g * 2 * TPG + (1 if i == 15 else 2) * ph.nt)
                return
            elif i == 19:
                eng.wait_ge(v_full, (ph.g + 1) * TPG + ph.nt2)
                return
            else:
                b, q = ph.use("a", 2 * (i - 20) + 1)
            eng.wait_ge(a_full[b], q + 1)

        N_CONST = 10

        block_stack = ExitStack()
        block = block_stack.enter_context(nc.Block())

        @block.sync
        def _(sp):
            consts = [
                (wp_raw, v["w_pool"][0].rearrange("g c d -> c g d")),
                (wsp_raw, v["w_spatial"][0].rearrange("h i j -> i h j")),
                (bsp[:, :, :].rearrange("p h i -> p (h i)"),
                 v["b_spatial"].rearrange("a h i -> a (h i)").broadcast_to([P, HALF])),
                (gffn[:, :], v["g_ffn"].broadcast_to([P, D])),
                (pscale[:, :], v["pool_scale"][0].rearrange("(k p) -> p k", p=P)),
                (wr[:, :, 0:4], v["w_group"][0].rearrange("(k p) n -> p k n", p=P)),
                (wr[:, :, 4:20], v["w_router"][0].rearrange("(k p) n -> p k n", p=P)),
                (br[:, 0:4], v["b_group"].broadcast_to([P, NG])),
                (br[:, 4:20], v["b_router"].broadcast_to([P, NE])),
            ]
            assert N_CONST == len(consts) + 1

            def early_loads(i):
                if i == 0:
                    for t in range(TPG):
                        sp.dma_start(xb[:, t, :], x_prompt[0, t * P:(t + 1) * P, :]).then_inc(x_first[t], 16)
                        if t == 0:
                            sp.dma_start(gmix[:, :], v["g_mix"].broadcast_to([P, D])).then_inc(gmix_in, 16)
                    load_panel(PhaseOne(-1), 0)
                else:
                    load_panel(PhaseOne(-1), 1)
                    sp.dma_start(gv[:, :], v["g_v"].broadcast_to([P, HALF])).then_inc(gv_in, 16)
                    sp.wait_ge(setup, 1)
                    sp.dma_start(state[1:16, :], v["state_pool"][0, 0, :, :]).then_inc(const_in, 16)
                    with nc.allow_non_contiguous_dma(reason="short columns of constants"):
                        for dst, src in consts:
                            sp.dma_start(dst, src).then_inc(const_in, 16)

            def load_panel(ph, i):
                par, n = ph.panel(i)
                if not (ph.pro and i < 2):
                    sp.wait_ge(w_lo, n - 1)
                for view, src in panel_sources(i, ph.pro):
                    sp.dma_start(view(raw[par]), src).then_inc(raw_in[par], 16)

            def store_h(ph, tiles):
                for t in tiles:
                    sp.wait_ge(hn_ok, ph.g * TPG + t + 1)
                    rows = bass.ds(ph.g * GROUP + t * P, ph.rows)
                    sp.dma_start(h_dram[rows, :], h[0:ph.rows, t, :]).then_inc(h_out, 16)
                    sp.dma_start(hn_dram[rows, :], hn[0:ph.rows, t % 3, :]).then_inc(hn_out[min(t, 1)], 16)

            def body(ph):
                count = PRE if ph.pro else (NPAN if ph.next else NPAN - PRE)
                for i in range(count):
                    if ph.pro and i < 2:
                        early_loads(i)
                    else:
                        load_panel(ph, i)
                    if not ph.pro and i == 15:
                        panel_done(sp, ph, 13)
                        for t in range(ph.nt):
                            sp.dma_start(h[0:ph.rows, t, :], x_rows(ph, t)).then_inc(res_in, 16)
                    if not ph.pro and i == 19:
                        store_h(ph, range(0, ph.nt - 2))
                    if not ph.pro and i == 20:
                        store_h(ph, range(ph.nt - 2, ph.nt))
                if not ph.next:
                    panel_done(sp, ph, 12)
                    for k0, w, landed in ((0, v["w_gate"], v["gate_in"]), (KD, v["w_up"], v["up_in"])):
                        sp.dma_start(v["raw_gu"][:, k0:k0 + KD, :], w[0, 0].rearrange("(k p) f -> p k f", p=P))\
                            .then_inc(landed, 16)
                    store_h(ph, range(ph.nt))
                if isinstance(ph.g, int) and ph.g == NPROMPT - 1:
                    sp.wait_ge(vf_ok, NT)
                    sp.dma_start(v["new_v"][0, 0, :, :], vf[0:SAMPLE, :]).then_inc(v_out, 16)
            passes(sp, body)
            sp.wait_ge(v_out, 16)
            sp.wait_ge(h_out, 16 * NT)
            sp.wait_ge(hn_out[0], 16 + 16 * (NPROMPT + 1))
            sp.wait_ge(hn_out[1], 16 + 16 * (TPG - 1) * NPROMPT)
            for c, out in ((0, v["new_pool_prompt"]), (1, v["new_pool_sample"])):
                sp.wait_ge(hist_ok, c + 1)
                sp.dma_start(out[0, 0, :, :], histT[1:16, c, :]).then_inc(hist_out, 16)
            sp.wait_ge(hist_out, 32)

        @block.gpsimd
        def _(pool):
            nc.gpsimd.memset(state, 0.0).then_inc(setup, 1)
            nc.gpsimd.memset(half_neg[:, :], -0.5).then_inc(setup, 1)
            nc.gpsimd.memset(ones[:, :], 1.0).then_inc(setup, 1)
            nc.gpsimd.memset(zero_rows, 0.0).then_inc(setup, 1)
            nc.gpsimd.memset(empty[:, :, 1:2], 0).then_inc(setup, 1)
            nc.gpsimd.iota(empty[:, :, 0:1], pattern=[[0, NSLOT], [0, 1]], base=SEQ + SAMPLE, channel_multiplier=1)\
                .then_inc(setup, 1)
            nc.gpsimd.iota(iota16[:, :], pattern=[[1, NE]], base=0, channel_multiplier=0,
                           allow_small_or_imprecise_dtypes=True).then_inc(setup, 1)
            nc.gpsimd.iota(tok_all[:, :], pattern=[[P, NT]], base=0, channel_multiplier=1).then_inc(setup, 1)
            nc.gpsimd.memset(lg[:, :, 4:8], NEG).then_inc(hn_out[0], 16)
            nc.gpsimd.memset(running[:, :], 0.0).then_inc(hn_out[1], 16)
            nc.gpsimd.memset(msum[:, :, :], 0.0).then_inc(setup, 1)
            pool.wait_ge(setup, 9)
            nc.gpsimd.affine_select(out=ident[:, :], in_=ones[:, :], compare_op=ALU.is_equal, fill=0.0, base=0,
                                    pattern=[[-1, P]], channel_multiplier=1).then_inc(setup, 1)
            nc.gpsimd.affine_select(out=upper[:, :], in_=ones[:, :], compare_op=ALU.is_gt, fill=0.0, base=0,
                                    pattern=[[1, P]], channel_multiplier=-1).then_inc(setup, 1)
            pool.dma_start(slot_dram.rearrange("(p n) o -> p n o", p=P), empty).then_inc(scattered, 16)
            for rows in (h_dram, hn_dram):
                pool.dma_start(rows[SEQ + SAMPLE:SEQ + SAMPLE + P, :], zero_rows).then_inc(spare_out, 16)

            def rsqrt(ms_sem, value, rows, col, done):
                pool.wait_ge(ms_sem, value)
                nc.gpsimd.tensor_tensor(rs[0:rows, col:col + 1], ms[0:rows, col:col + 1], half_neg[0:rows, :],
                                        ALU.pow).then_inc(done, 1)

            def scatter(ph):
                pool.wait_ge(dest_ok, ph.g + 1)
                wait_apart(pool, scattered, 16 + 32 * TPG * ph.g, passed_pool)
                for t in range(ph.nt):
                    for c in range(2):
                        nc.gpsimd.indirect_dma_start(
                            out=slot_dram,
                            out_offset=bass.IndirectOffsetOnAxis(ap=dest[0:ph.rows, c, t:t + 1], axis=0),
                            in_=pay[0:ph.rows, c, t, :], in_offset=None).then_inc(scattered, 16)

            def body(ph):
                first = (ph.g + 1) * TPG
                if ph.nt2 and not ph.pro:
                    pool.wait_ge(xT_hi, 2 * first)
                    if ph.n2 == GROUP:
                        src = x_prompt[0, bass.ds((ph.g + 1) * GROUP, GROUP), :].rearrange("(t p) d -> p t d", p=P)
                        pool.dma_start(xb[:, :, :], src).then_inc(x_in, 16)
                    else:
                        pool.dma_start(xb[0:SAMPLE, 0, :], x_sample[0, :, :]).then_inc(x_in, 16)
                for t in range(min(2, ph.nt2)):
                    rsqrt(x_ms, first + t + 1, ph.rows2, t, x_rs)
                if ph.prev:
                    scatter(ph.prev)
                for t in range(2, ph.nt2):
                    rsqrt(x_ms, first + t + 1, ph.rows2, t, x_rs)
                if ph.pro:
                    pool.wait_ge(const_in, 16 * N_CONST)
                    nc.gpsimd.affine_select(out=wsp_raw, in_=wsp_raw, compare_op=ALU.is_ge, fill=0.0, base=0,
                                            pattern=[[0, 4], [-1, P]], channel_multiplier=1).then_inc(tri_ok, 1)
                for t in range(min(3, ph.nt)):
                    rsqrt(h_ms, ph.g * TPG + t + 1, ph.rows, 8 + t, h_rs)
                for t in range(max(ph.nt, ph.nt2)):
                    if t < ph.nt2:
                        rsqrt(v_ms, first + t + 1, ph.rows2, 4 + t, v_rs)
                    if t == 0 and ph.nt > 3:
                        rsqrt(h_ms, ph.g * TPG + 4, ph.rows, 11, h_rs)
                if ph.places_itself:
                    scatter(ph)
            passes(pool, body)
            pool.wait_ge(scattered, 16 + 32 * NT)

        @block.scalar
        def _(act):
            def split(ph, i):
                par, n = ph.panel(i)
                loads = sum(len(panel_sources(q, ph.pro)) for q in range(par, i + 1, 2))
                act.wait_ge(raw_in[par], 16 * (loads if ph.pro else 2 + 13 * ph.g + loads))
                if not (ph.pro and i < 2):
                    panel_done(act, ph, i - 2)
                for q in range(4):
                    nc.scalar.activation(part(wh[par], q), part(raw[par], q), ACT.Copy).then_inc(w_hi, 1)

            def constants():
                act.wait_ge(const_in, 16 * N_CONST)
                nc.scalar.activation(wp[0][:, :, :], wp_raw, ACT.Copy).then_inc(const_ok, 1)
                act.wait_ge(const_tr, 1)
                nc.scalar.activation(ws[0][:, :, :], bankC[:, :].rearrange("p (h i) -> p h i", h=4),
                                     ACT.Copy).then_inc(const_ok, 1)

            def softmaxes(ph):
                act.wait_ge(exps_in, ph.g + 1)
                nc.scalar.activation(exps[0:ph.rows, 0:ph.nt, :], exps[0:ph.rows, 0:ph.nt, :], ACT.Exp)\
                    .then_inc(exps_ok, 1)

            def to_rows(ph, i, count=1):
                if ph.next and i < 20:
                    return
                for s in range(count):
                    q = tm_number(i, s)
                    act.wait_ge(tm_full, q + 1)
                    nc.scalar.activation(tm[0:SAMPLE, q % 2, :], tm_bank(i, s)[0:SAMPLE, 0:256], ACT.Copy)\
                        .then_inc(tm_ok, 1)

            def squares_of_x(ph, tiles):
                if ph.nt2 and not ph.pro:
                    act.wait_ge(x_in, 16 * (ph.g + 1))
                for t in tiles:
                    if ph.pro:
                        act.wait_ge(x_first[t], 16)
                    r, num = ph.rows2, (ph.g + 1) * TPG + t
                    if t:
                        act.wait_ge(x_ss, num)
                    nc.scalar.activation(junk[0:r, :], xb[0:r, t, :], ACT.Square,
                                         accum_out=ss[0:r, t:t + 1]).then_inc(x_ss, 1)

            def body(ph):
                n, n2, g = ph.n, ph.n2, ph.g
                first = (g + 1) * TPG
                o = 0 if ph.pro else 18
                if ph.pro:
                    squares_of_x(ph, range(2))
                else:
                    for i in range(2):
                        split(ph, i + 1)
                        to_rows(ph, i)
                        for m in (2 * i, 2 * i + 1):
                            freed(act, ph, "u", m)
                            if m == 0:
                                act.wait_ge(hn_out[0], 16 * g + 16)
                                act.wait_ge(hn_out[1], 16 * (TPG - 1) * g + 16)
                            nc.scalar.activation(pb[0][:, m, 0:n], win[m % 2][:, 0:n], ACT.Copy).then_inc(pb_hi, 1)
                    for i in range(4):
                        for kind, name in enumerate(("ga", "gb")):
                            split(ph, 3 + 3 * i + kind)
                            to_rows(ph, 2 + 3 * i + kind)
                            for c in range(2):
                                b = full(act, ph, name, 2 * i + c)
                                if kind == 0 and c == 0:
                                    if i:
                                        act.wait_ge(mg_ok, g * 8 + 2 * i)
                                    else:
                                        act.wait_ge(pb_ok, g * 4 + 4)
                                nc.scalar.activation(S[:, 2 * kind + c, 0:n], bankA[b][:, 0:n], ACT.Sigmoid)\
                                    .then_inc(a_free[b], 1)
                            if kind == 0 and i == 0:
                                squares_of_x(ph, range(min(2, ph.nt2)))
                            if kind == 0 and i == 3:
                                squares_of_x(ph, range(2, ph.nt2))
                        split(ph, 5 + 3 * i)
                        to_rows(ph, 4 + 3 * i, 2)
                        for m in (2 * i, 2 * i + 1):
                            act.wait_ge(mix_ok, g * 8 + m + 1)
                            nc.scalar.activation(mg[0][:, m, 0:n], win[m % 2][:, 0:n], ACT.Copy).then_inc(mg_hi, 1)
                        if ph.prev and i == 1:
                            softmaxes(ph.prev)
                    split(ph, 15)
                for t in range(ph.nt2):
                    r = ph.rows2
                    for c in range(2):
                        b = full(act, ph, "x", t, c)
                        nc.scalar.activation(xT[0][:, 4 * c:4 * c + 4, t * P:t * P + r],
                                             bankA[b][:, :].rearrange("p (k i) -> p k i", k=4)[:, :, 0:r],
                                             ACT.Copy).then_inc(xT_hi, 1)
                    if ph.pro and t < 2:
                        squares_of_x(ph, [t + 2])
                    if ph.pro and t == 2:
                        split(ph, 0)
                    if t == (3 if ph.pro else min(1, ph.nt2 - 1)):
                        split(ph, 1 if ph.pro else 16)
                if not ph.pro:
                    if not ph.next:
                        split(ph, 16)
                    split(ph, 17)
                    if ph.next:
                        split(ph, 18)
                    for t in range(ph.nt):
                        act.wait_ge(h_part, g * 2 * TPG + ph.nt + t + 1)
                        if t:
                            act.wait_ge(h_ss, g * TPG + t)
                        nc.scalar.activation(junk[0:ph.rows, :], h[0:ph.rows, t, :], ACT.Square,
                                             accum_out=ss[0:ph.rows, 8 + t:9 + t]).then_inc(h_ss, 1)
                    if ph.next:
                        split(ph, 19)
                if ph.pro:
                    constants()
                if ph.next:
                    split(ph, o + 2)
                for t in range(max(ph.nt, ph.nt2)):
                    r = ph.rows2
                    if t < ph.nt2:
                        act.wait_ge(v_full, first + t + 1)
                        nc.scalar.activation(junk[0:r, 0:HALF], bankV[t][0:r, :], ACT.Square,
                                             accum_out=ss[0:r, 4 + t:5 + t]).then_inc(v_ss, 1)
                    if t < ph.nt:
                        if t:
                            act.wait_ge(lg_full, TPG * g + t)
                        for c in range(2):
                            b = full(act, ph, "hn", t, c)
                            nc.scalar.activation(hnT[:, 4 * c:4 * c + 4, 0:ph.rows],
                                                 bankA[b][:, :].rearrange("p (k i) -> p k i", k=4)[:, :, 0:ph.rows],
                                                 ACT.Copy).then_inc(a_free[b], 1)
                    if t < ph.nt2:
                        act.wait_ge(vf_ok, first + t + 1)
                        nc.scalar.activation(vn[0][0:r, t, :], vf[0:r, :], ACT.Copy).then_inc(vn_hi, 1)
                if not ph.next:
                    softmaxes(ph)
                    return
                split(ph, o + 3)

                def take_a(m):
                    if m >= 2:
                        act.wait_ge(d_ok, (g + 1) * 4 + m - 1)
                    elif not ph.pro:
                        act.wait_ge(d_ok, g * 4 + m + 3)
                    hs = hist[1] if n2 == SAMPLE else hist[0]
                    nc.scalar.activation(exts[m % 2][:, 0:16], hs[:, m, :], ACT.Copy).then_inc(ext_ok, 1)
                    b = full(act, ph, "a", m)
                    nc.scalar.activation(exts[m % 2][:, 16:16 + n2], bankA[b][:, 0:n2], ACT.Copy)\
                        .then_inc(a_free[b], 1)

                def d_high(m):
                    act.wait_ge(d_ok, (g + 1) * 4 + m + 1)
                    if m >= 2:
                        full(act, ph, "pm", m - 2)
                    nc.scalar.activation(dd[0][:, m % 2, 0:n2], win[(m + 1) % 2][:, 0:n2], ACT.Copy).then_inc(d_hi, 1)

                def pa_high(m):
                    b = full(act, ph, "pm", m)
                    if m == 0 and not ph.pro:
                        act.wait_ge(h_out, 16 * (TPG * g + ph.nt))
                    nc.scalar.activation(pa[0][:, m, 0:n2], bankA[b][:, 0:n2], ACT.Copy,
                                         scale=pscale[:, m:m + 1]).then_inc(pa_hi, 1)
                if ph.nt2 == 1:
                    to_rows(ph, 20)
                take_a(0)
                take_a(1)
                d_high(0)
                d_high(1)
                split(PhaseOne(g + 1), 0)
                if ph.nt2 == 1:
                    to_rows(ph, 21)
                take_a(2)
                d_high(2)
                pa_high(0)
                take_a(3)
                d_high(3)
                pa_high(1)
                if ph.places_itself:
                    softmaxes(ph)
                pa_high(2)
                pa_high(3)
            passes(act, body)

        @block.vector
        def _(dve):
            tt, ts, stt = nc.vector.tensor_tensor, nc.vector.tensor_scalar, nc.vector.scalar_tensor_tensor
            lo = lambda out, x, hi: tt(out, x, hi.bitcast(F32), ALU.subtract)

            dve.wait_ge(setup, 11)
            for m in range(4):
                ts(corr[:, m, :], iota16[:, :], 1.0, float(2 << m), ALU.add, ALU.min)
            nc.vector.memset(hist[0][:, :, :], 0.0)
            dve.drain()
            nc.vector.reciprocal(corr[:, :, :], corr[:, :, :])
            dve.drain()
            for m in range(4):
                ts(corr[:, m, :], corr[:, m, :], float(2 << m), None, ALU.mult)
            def split(ph, i):
                par, n = ph.panel(i)
                for q in range(4):
                    dve.wait_ge(w_hi, 4 * n + q + 1)
                    last = lo(part(wl[par], q), part(raw[par], q), part(wh[par], q))
                last.then_inc(w_lo, 1)

            def constants():
                dve.wait_ge(const_in, 16 * N_CONST)
                dve.wait_ge(scattered, 16)
                dve.wait_ge(spare_out, 32)
                dve.wait_ge(const_ok, 1)
                lo(wp[1][:, :, :], wp_raw, wp[0][:, :, :])
                dve.wait_ge(const_ok, 2)
                lo(ws[1][:, :, :], bankC[:, :].rearrange("p (h i) -> p h i", h=4), ws[0][:, :, :])
                nc.vector.tensor_copy(hist[1][:, :, :], bankR[:, 0:64].rearrange("p (g i) -> p g i", g=4))\
                    .then_inc(dve_setup, 1)

            def mean(ss_sem, value, rows, col, width, done):
                dve.wait_ge(ss_sem, value)
                ts(ms[0:rows, col:col + 1], ss[0:rows, col:col + 1], 1.0 / width, EPS, ALU.mult, ALU.add)\
                    .then_inc(done, 1)

            def norm_x(ph, tiles):
                r, first = ph.rows2, (ph.g + 1) * TPG
                for t in tiles:
                    mean(x_ss, first + t + 1, r, t, D, x_ms)
                if ph.pro:
                    dve.wait_ge(gmix_in, 16)
                for t in tiles:
                    dve.wait_ge(x_rs, first + t + 1)
                    stt(xb[0:r, t, :], xb[0:r, t, :], rs[0:r, t:t + 1], gmix[0:r, :], ALU.mult, ALU.mult)\
                        .then_inc(x_scaled, 1)

            def rows_of_x(ph, t):
                r, num = ph.rows2, (ph.g + 1) * TPG + t
                for c in range(2):
                    b = full(dve, ph, "x", t, c)
                    dve.wait_ge(xT_hi, 2 * num + c + 1)
                    lo(xT[1][:, 4 * c:4 * c + 4, t * P:t * P + r],
                       bankA[b][:, :].rearrange("p (k i) -> p k i", k=4)[:, :, 0:r],
                       xT[0][:, 4 * c:4 * c + 4, t * P:t * P + r]).then_inc(a_free[b], 1)

            def add_residual(ph, half):
                r = ph.rows
                for t in range(ph.nt):
                    dve.wait_ge(res_in, 16 * (ph.g * TPG + ph.nt))
                    dve.wait_ge(o_full, ph.g * 2 * TPG + half * ph.nt + t + 1)
                    part = h[0:r, t, half * HALF:(half + 1) * HALF]
                    tt(part, bankV[t][0:r, :], part, ALU.add).then_inc(h_part, 1)

            def norm_h(ph, t):
                r, num = ph.rows, ph.g * TPG + t
                mean(h_ss, num + 1, r, 8 + t, D, h_ms)
                dve.wait_ge(h_rs, num + 1)
                if t == 3:
                    dve.wait_ge(hn_out[0], 16 + 16 * ph.g + 16)
                    full(dve, ph, "hn", 0, 1)
                stt(hn[0:r, t % 3, :], h[0:r, t, :], rs[0:r, 8 + t:9 + t], gffn[0:r, :], ALU.mult, ALU.mult)\
                    .then_inc(hn_ok, 1)

            def norm_v(ph, t):
                r, num = ph.rows2, (ph.g + 1) * TPG + t
                mean(v_ss, num + 1, r, 4 + t, HALF, v_ms)
                dve.wait_ge(v_rs, num + 1)
                stt(vf[0:r, :], bankV[t][0:r, :], rs[0:r, 4 + t:5 + t], gv[0:r, :], ALU.mult, ALU.mult)\
                    .then_inc(vf_ok, 1)
                dve.wait_ge(vn_hi, num + 1)
                lo(vn[1][0:r, t, :], vf[0:r, :], vn[0][0:r, t, :]).then_inc(vn_ok, 1)

            def logits(ph, t):
                r = ph.rows
                dve.wait_ge(lg_full, ph.g * TPG + t + 1)
                tt(lg[0:r, t, 0:4], bankR[0:r, 0:4], br[0:r, 0:4], ALU.add)
                tt(lg[0:r, t, 8:24], bankR[0:r, 4:20], br[0:r, 4:20], ALU.add).then_inc(lg_ok, 1)

            def pooled(ph, m):
                hs, n2, ext = (hist[1] if ph.n2 == SAMPLE else hist[0]), ph.n2, exts[m % 2]
                end, src = n2 + 16, ext
                dve.drain()
                dve.wait_ge(ext_ok, (ph.g + 1) * 4 + m + 1)
                freed(dve, ph, "a", m)
                for level in range(m + 1):
                    s, dst = 1 << level, win[level % 2]
                    if level:
                        dve.drain()
                    tt(dst[:, 2 * s:end], src[:, 2 * s:end], src[:, s:end - s], ALU.add)
                    src = dst
                nc.vector.tensor_copy(hs[:, m, :], ext[:, n2:end])
                dve.drain()
                if ph.pro:
                    tt(src[:, 16:32], src[:, 16:32], corr[:, m, :], ALU.mult)
                    dve.drain()
                d = win[(m + 1) % 2][:, 0:n2]
                stt(d, src[:, 16:end], 1.0 / (2 << m), ext[:, 16:end], ALU.mult, ALU.subtract).then_inc(d_ok, 1)
                dve.wait_ge(d_hi, (ph.g + 1) * 4 + m + 1)
                lo(dd[1][:, m % 2, 0:n2], d, dd[0][:, m % 2, 0:n2]).then_inc(d_lo, 1)

            def pa_low(ph, m):
                b = full(dve, ph, "pm", m)
                dve.wait_ge(pa_hi, (ph.g + 1) * 4 + m + 1)
                stt(pa[1][:, m, 0:ph.n2], bankA[b][:, 0:ph.n2], pscale[:, m:m + 1], pa[0][:, m, 0:ph.n2].bitcast(F32),
                    ALU.mult, ALU.subtract).then_inc(a_free[b], 1)

            def spatial(ph, t):
                r = ph.rows2
                dve.wait_ge(sp_full, (ph.g + 1) * TPG + t + 1)
                tt(S[:, :, t * P:t * P + r], bankV[t][:, :].rearrange("p (h i) -> p h i", h=4)[:, :, 0:r],
                   bsp[:, :, 0:r], ALU.add).then_inc(sp_read, 1)

            def choose(ph):
                r, ts_ = ph.rows, range(ph.nt)
                dve.drain()
                for t in ts_:
                    nc.vector.max(best[0:r, t, :], lg[0:r, t, 0:8])
                dve.drain()
                for t in ts_:
                    nc.vector.max_index(besti[0:r, t, :], best[0:r, t, :], lg[0:r, t, 0:8])
                dve.drain()
                for t in ts_:
                    nc.vector.tensor_copy(gidx[0:r, t:t + 1], besti[0:r, t, 0:1])
                tt(exps[0:r, 0:ph.nt, 0:NG], lg[0:r, 0:ph.nt, 0:NG],
                   best[0:r, 0:ph.nt, 0:1].broadcast_to([r, ph.nt, NG]), ALU.subtract)
                dve.drain()
                for t in ts_:
                    ts(inside[0:r, t, :], iota16[0:r, 0:NG], gidx[0:r, t:t + 1], None, ALU.is_equal)
                dve.drain()
                ts(pen[0:r, :, :], inside[0:r, :, :], -NEG, NEG, ALU.mult, ALU.add)
                for t in ts_:
                    wide = inside[0:r, t, :].unsqueeze(2).broadcast_to([r, NG, EPG])
                    tt(el[0:r, t, :].rearrange("p (a b) -> p a b", a=NG),
                       lg[0:r, t, 8:24].rearrange("p (a b) -> p a b", a=NG), wide, ALU.mult)
                dve.drain()
                for t in ts_:
                    wide = pen[0:r, t, :].unsqueeze(2).broadcast_to([r, NG, EPG])
                    part = el[0:r, t, :].rearrange("p (a b) -> p a b", a=NG)
                    tt(part, part, wide, ALU.add)
                dve.drain()
                for t in ts_:
                    nc.vector.max(best[0:r, t, :], el[0:r, t, :])
                dve.drain()
                for t in ts_:
                    nc.vector.max_index(besti[0:r, t, :], best[0:r, t, :], el[0:r, t, :])
                dve.drain()
                nt = ph.nt
                nc.vector.tensor_copy(rec[0:r, 0:nt, :], besti[0:r, 0:nt, 0:2])
                tt(exps[0:r, 0:nt, NG:NG + 1], best[0:r, 0:nt, 1:2], best[0:r, 0:nt, 0:1], ALU.subtract)\
                    .then_inc(exps_in, 1)
                dve.drain()
                for t in ts_:
                    for c in range(2):
                        ts(mask[0:r, c, t, :], iota16[0:r, :], rec[0:r, t, c:c + 1], None, ALU.is_equal)
                dve.drain()
                tt(msum[0:r, 0:nt, :], mask[0:r, 0, 0:nt, :], mask[0:r, 1, 0:nt, :], ALU.add).then_inc(mask_ok, 1)

            def place(ph):
                r, nt, g = ph.rows, ph.nt, ph.g
                dve.wait_ge(cum_full, g + 1)
                for t in range(nt):
                    tt(rank[0:r, t, :], bankC[0:r, t * NE:(t + 1) * NE], running[0:r, :], ALU.add)
                    dve.drain()
                    tt(running[:, :], bankC[:, 64 + t * NE:64 + (t + 1) * NE], running[:, :], ALU.add)
                    dve.drain()
                for c in range(2):
                    tt(prod[0:r, c, 0:nt, :], mask[0:r, c, 0:nt, :], rank[0:r, 0:nt, :], ALU.mult)
                dve.drain()
                for c in range(2):
                    nc.vector.reduce_sum(dest_f[0:r, c, 0:nt], prod[0:r, c, 0:nt, :], axis=AX)
                dve.drain()
                nc.vector.tensor_copy(low7[0:r, :, 0:nt], dest_f[0:r, :, 0:nt])
                dve.wait_ge(exps_ok, g + 1)
                second = exps[0:r, 0:nt, NG:NG + 1].rearrange("p t o -> p (t o)")
                nc.vector.reduce_sum(parts[0:r, 0, 0:nt], exps[0:r, 0:nt, 0:NG], axis=AX)
                ts(parts[0:r, 1, 0:nt], second, 1.0, None, ALU.add)
                dve.drain()
                ts(high7[0:r, :, 0:nt], low7[0:r, :, 0:nt], 7, None, ALU.logical_shift_right)
                dve.drain()
                ts(low7[0:r, :, 0:nt], low7[0:r, :, 0:nt], P - 1, None, ALU.bitwise_and)
                tt(parts[0:r, 0, 0:nt], parts[0:r, 0, 0:nt], parts[0:r, 1, 0:nt], ALU.mult)
                dve.drain()
                stt(dest_f[0:r, :, 0:nt], low7[0:r, :, 0:nt], float(NSLOT), high7[0:r, :, 0:nt], ALU.mult, ALU.add)
                nc.vector.reciprocal(parts[0:r, 0, 0:nt], parts[0:r, 0, 0:nt])
                wait_apart(dve, scattered, 16 + 32 * TPG * g, passed_dve)
                dve.drain()
                which = slice(g * TPG, g * TPG + nt) if isinstance(g, int) else bass.ds(g * TPG, TPG)
                weight = pay[0:r, :, 0:nt, 1:2].rearrange("p c t o -> p c (t o)").bitcast(F32)
                for c in range(2):
                    nc.vector.tensor_copy(pay[:, c, 0:nt, 0:1].rearrange("p t o -> p (t o)"), tok_all[:, which])
                nc.vector.tensor_copy(weight[:, 0, :], parts[0:r, 0, 0:nt])
                tt(weight[:, 1, :], parts[0:r, 0, 0:nt], second, ALU.mult)
                for c in range(2):
                    last = stt(dest[0:r, c, 0:nt], rec[0:r, 0:nt, c], float(BPE), dest_f[0:r, c, 0:nt],
                               ALU.mult, ALU.add)
                last.then_inc(dest_ok, 1)

            def body(ph):
                g, n = ph.g, ph.n
                o = 0 if ph.pro else 18
                if ph.pro:
                    norm_x(ph, [0])
                    norm_x(ph, [1])
                else:
                    for i in range(2):
                        split(ph, i + 1)
                        for m in (2 * i, 2 * i + 1):
                            b = full(dve, ph, "u", m)
                            t1 = win[m % 2][:, 0:n]
                            if m == 0:
                                dve.wait_ge(sp_read, g * TPG + ph.nt)
                            tt(t1, bankA[b][:, 0:n], S[:, m, 0:n], ALU.mult).then_inc(a_free[b], 1)
                            dve.wait_ge(pb_hi, g * 4 + m + 1)
                            lo(pb[1][:, m, 0:n], t1, pb[0][:, m, 0:n]).then_inc(pb_ok, 1)
                    for i in range(4):
                        split(ph, 3 + 3 * i)
                        if ph.prev and i == 1:
                            choose(ph.prev)
                        if ph.prev and i == 2:
                            place(ph.prev)
                        if i == 0:
                            norm_x(ph, range(min(2, ph.nt2)))
                        if i == 3:
                            norm_x(ph, range(2, ph.nt2))
                        split(ph, 4 + 3 * i)
                        split(ph, 5 + 3 * i)
                        for c in range(2):
                            m = 2 * i + c
                            for kind, (gate, name) in enumerate((("ga", "P"), ("gb", "Q"))):
                                freed(dve, ph, gate, m)
                                b = full(dve, ph, name, m)
                                part = S[:, 2 * kind + c, 0:n]
                                tt(part, bankA[b][:, 0:n], part, ALU.mult).then_inc(a_free[b], 1)
                            dve.drain()
                            t1 = win[m % 2][:, 0:n]
                            tt(t1, S[:, c, 0:n], S[:, 2 + c, 0:n], ALU.add).then_inc(mix_ok, 1)
                            dve.wait_ge(mg_hi, g * 8 + m + 1)
                            lo(mg[1][:, m, 0:n], t1, mg[0][:, m, 0:n]).then_inc(mg_ok, 1)
                    split(ph, 15)
                for t in range(ph.nt2):
                    rows_of_x(ph, t)
                    if ph.pro and t < 2:
                        norm_x(ph, [t + 2])
                    if ph.pro and t == 2:
                        split(ph, 0)
                    if t == (3 if ph.pro else min(1, ph.nt2 - 1)):
                        split(ph, 1 if ph.pro else 16)
                if not ph.pro:
                    if not ph.next:
                        split(ph, 16)
                    add_residual(ph, 0)
                    split(ph, 17)
                    if ph.next:
                        split(ph, 18)
                    add_residual(ph, 1)
                    for t in range(min(3, ph.nt)):
                        if t == min(2, ph.nt) and ph.next:
                            split(ph, 19)
                        norm_h(ph, t)
                if ph.pro:
                    constants()
                    dve.wait_ge(gv_in, 16)
                if ph.next:
                    split(ph, o + 2)
                for t in range(max(ph.nt, ph.nt2)):
                    if t < ph.nt2:
                        norm_v(ph, t)
                    if t == 0 and ph.nt > 3:
                        norm_h(ph, 3)
                    if t < ph.nt and (t < ph.nt - 1 or not ph.next):
                        logits(ph, t)
                if not ph.next:
                    choose(ph)
                    place(ph)
                    return
                split(ph, o + 3)
                if ph.nt:
                    logits(ph, ph.nt - 1)
                pooled(ph, 0)
                pooled(ph, 1)
                if ph.places_itself:
                    choose(ph)
                split(PhaseOne(g + 1), 0)
                pooled(ph, 2)
                pa_low(ph, 0)
                pooled(ph, 3)
                pa_low(ph, 1)
                if ph.places_itself:
                    place(ph)
                pa_low(ph, 2)
                for t in range(ph.nt2):
                    spatial(ph, t)
                pa_low(ph, 3)
            passes(dve, body)
            for c in range(2):
                dve.wait_ge(hist_full, c + 1)
                nc.vector.tensor_copy(histT[:, c, :], (bankA[0], bankA[1])[c][0:16, :]).then_inc(hist_ok, 1)

        @block.tensor
        def _(pe):
            pe.wait_ge(setup, 11)

            def constants():
                pe.wait_ge(tri_ok, 1)
                for m in range(4):
                    nc.tensor.transpose(bankR[:, 16 * m:16 * m + 16], state[:, m * P:(m + 1) * P], ident[0:16, 0:16])
                for hd in range(4):
                    last = nc.tensor.transpose(bankC[:, hd * P:(hd + 1) * P], wsp_raw[:, hd, :], ident[:, :])
                last.then_inc(const_tr, 1)

            def take(ph, *key):
                b, q = ph.use(*key)
                wait(pe, a_free[b], q)
                return b

            def rows_of_x(ph, t):
                r, num = ph.rows2, (ph.g + 1) * TPG + t
                pe.wait_ge(x_scaled, num + 1)
                for c in range(2):
                    b = take(ph, "x", t, c)
                    for k in range(4):
                        last = nc.tensor.transpose(bankA[b][:, k * P:k * P + r],
                                                   xb[0:r, t, (4 * c + k) * P:(4 * c + k + 1) * P],
                                                   ident[0:r, 0:r])
                    last.then_inc(a_full[b], 1)

            def start_panel(ph, i):
                par, n = ph.panel(i)
                pe.wait_ge(w_lo, n + 1)
                return wh[par], wl[par]

            def chunk(ph, i, c, name, m, src, ks, n):
                wh_, wl_ = start_panel(ph, i)
                b = take(ph, name, m)
                cols = slice(c * P, (c + 1) * P)
                return products(nc, bankA[b][:, 0:n],
                                [((wh_[:, kw, cols], wl_[:, kw, cols]), (src[0][:, ka, 0:n], src[1][:, ka, 0:n]))
                                 for kw, ka in ks]).then_inc(a_full[b], 1)

            def sample_panel(ph, i, jobs):
                wh_, wl_ = start_panel(ph, i)
                n = SAMPLE
                if i >= 20:
                    pe.wait_ge(h_part, 2 * TPG * (ph.g + 1))
                for s, (name, m0, src, ks) in enumerate(jobs):
                    products(nc, tm_bank(i, s)[0:n, 0:256],
                             [((src[0][:, ka, 0:n], src[1][:, ka, 0:n]), (wh_[:, kw, :], wl_[:, kw, :]))
                              for kw, ka in ks]).then_inc(tm_full, 1)
                for c in range(2):
                    for s, (name, m0, src, ks) in enumerate(jobs):
                        q = tm_number(i, s)
                        pe.wait_ge(tm_ok, q + 1)
                        b = take(ph, name, m0 + c)
                        nc.tensor.transpose(bankA[b][:, 0:n], tm[0:n, q % 2, c * P:(c + 1) * P], ident[0:n, 0:n])\
                            .then_inc(a_full[b], 1)

            def token_major(ph, i, t, src, k0, rows, n_acc):
                wh_, wl_ = start_panel(ph, i)
                view = lambda w: w[:, :, :].rearrange("p (k a) n -> p k (a n)", a=2)
                cols = slice(t * P, t * P + rows)
                last = None
                for k in range(4):
                    ah, al = src[0][:, k0 + k, cols], src[1][:, k0 + k, cols]
                    wh4, wl4 = view(wh_)[:, k, :], view(wl_)[:, k, :]
                    out = bankV[t][0:rows, :]
                    nc.tensor.matmul(out, ah, wh4, start=(n_acc == 0 and k == 0), stop=False)
                    nc.tensor.matmul(out, ah, wl4, start=False, stop=False)
                    last = nc.tensor.matmul(out, al, wh4, start=False, stop=(n_acc == 1 and k == 3))
                return last

            def transpose_hn(ph, t):
                r = ph.rows
                pe.wait_ge(hn_ok, ph.g * TPG + t + 1)
                for c in range(2):
                    b = take(ph, "hn", t, c)
                    for k in range(4):
                        last = nc.tensor.transpose(bankA[b][:, k * P:k * P + r],
                                                   hn[0:r, t % 3, (4 * c + k) * P:(4 * c + k + 1) * P],
                                                   ident[0:r, 0:r])
                    last.then_inc(a_full[b], 1)

            def router(ph, t):
                r = ph.rows
                freed(pe, ph, "hn", t, 0)
                freed(pe, ph, "hn", t, 1)
                if t:
                    pe.wait_ge(lg_ok, ph.g * TPG + t)
                for k in range(KD):
                    last = nc.tensor.matmul(bankR[0:r, 0:20], hnT[:, k, 0:r], wr[:, k, :], start=(k == 0),
                                            stop=(k == KD - 1))
                last.then_inc(lg_full, 1)

            def count(ph):
                r, w = ph.rows, ph.nt * NE
                pe.wait_ge(mask_ok, ph.g + 1)
                flat = msum[0:r, 0:ph.nt, :].rearrange("p t e -> p (t e)")
                nc.tensor.matmul(bankC[0:r, 0:w], upper[0:r, 0:r], flat, start=True, stop=True)
                nc.tensor.matmul(bankC[:, 64:64 + w], ones[0:r, :], flat, start=True, stop=True).then_inc(cum_full, 1)

            def pool_products(ph, m):
                pe.wait_ge(d_lo, (ph.g + 1) * 4 + m + 1)
                b = take(ph, "pm", m)
                products(nc, bankA[b][:, 0:ph.n2],
                         [((wp[0][:, m, :], wp[1][:, m, :]), (dd[0][:, m % 2, 0:ph.n2], dd[1][:, m % 2, 0:ph.n2]))])\
                    .then_inc(a_full[b], 1)

            def spatial(ph, t):
                r = ph.rows2
                pe.wait_ge(vn_ok, (ph.g + 1) * TPG + t + 1)
                for hd in range(4):
                    cols = slice(hd * P, (hd + 1) * P)
                    last = products(nc, bankV[t][:, hd * P:hd * P + r],
                                    [((vn[0][0:r, t, cols], vn[1][0:r, t, cols]),
                                      (ws[0][0:r, hd, 0:r], ws[1][0:r, hd, 0:r]))])
                last.then_inc(sp_full, 1)

            def body(ph):
                g, n, n2 = ph.g, ph.n, ph.n2
                o = 0 if ph.pro else 18
                every = [(k, k) for k in range(KD)]
                if not ph.pro and not ph.next:
                    pe.wait_ge(sp_read, g * TPG + ph.nt)
                    for i in range(2):
                        sample_panel(ph, i, [("u", 2 * i, xT, every)])
                    for i in range(4):
                        sample_panel(ph, 2 + 3 * i, [("ga", 2 * i, xT, every)])
                        sample_panel(ph, 3 + 3 * i, [("gb", 2 * i, xT, every)])
                        pe.wait_ge(pb_ok, g * 4 + 4)
                        sample_panel(ph, 4 + 3 * i, [("P", 2 * i, pa, [(k, k) for k in range(4)]),
                                                     ("Q", 2 * i, pb, [(4 + k, k) for k in range(4)])])
                elif not ph.pro:
                    for i in range(2):
                        for c in range(2):
                            chunk(ph, i, c, "u", 2 * i + c, xT, every, n)
                    for i in range(4):
                        for kind, name in enumerate(("ga", "gb")):
                            for c in range(2):
                                chunk(ph, 2 + 3 * i + kind, c, name, 2 * i + c, xT, every, n)
                        pe.wait_ge(pb_ok, g * 4 + 4)
                        for c in range(2):
                            chunk(ph, 4 + 3 * i, c, "P", 2 * i + c, pa, [(k, k) for k in range(4)], n)
                            chunk(ph, 4 + 3 * i, c, "Q", 2 * i + c, pb, [(4 + k, k) for k in range(4)], n)
                        if ph.prev and i == 1:
                            count(ph.prev)
                if not ph.pro:
                    pe.wait_ge(mg_ok, g * 8 + 4)
                    pe.wait_ge(sp_read, g * TPG + ph.nt)
                    for t in range(ph.nt):
                        last = token_major(ph, 14, t, mg, 0, ph.rows, 0)
                    last.then_inc(half_used, 1)
                    pe.wait_ge(mg_ok, g * 8 + 8)
                    for t in range(max(ph.nt, ph.nt2)):
                        if t < ph.nt2:
                            rows_of_x(ph, t)
                        if t < ph.nt:
                            token_major(ph, 15, t, mg, 4, ph.rows, 1).then_inc(o_full, 1)
                    for t in range(ph.nt):
                        pe.wait_ge(h_part, g * 2 * TPG + t + 1)
                        last = token_major(ph, 16, t, mg, 0, ph.rows, 0)
                    last.then_inc(half_used, 1)
                    for t in range(ph.nt):
                        token_major(ph, 17, t, mg, 4, ph.rows, 1).then_inc(o_full, 1)
                else:
                    for t in range(ph.nt2):
                        rows_of_x(ph, t)
                if ph.next:
                    freed(pe, ph, "x", ph.nt2 - 1, 0)
                    freed(pe, ph, "x", ph.nt2 - 1, 1)
                    for t in range(ph.nt2):
                        if not ph.pro:
                            pe.wait_ge(h_part, g * 2 * TPG + TPG + t + 1)
                        last = token_major(ph, o, t, xT, 0, ph.rows2, 0)
                    last.then_inc(half_used, 1)
                if ph.pro:
                    constants()
                for t in range(max(ph.nt, ph.nt2)):
                    if t < ph.nt2:
                        token_major(ph, o + 1, t, xT, 4, ph.rows2, 1).then_inc(v_full, 1)
                    if 0 < t < ph.nt:
                        router(ph, t - 1)
                    if t < ph.nt:
                        transpose_hn(ph, t)
                if not ph.next:
                    router(ph, 0)
                    count(ph)
                    return
                if ph.nt2 == 1:
                    sample_panel(ph, 20, [("a", 0, xT, every)])
                    router(ph, ph.nt - 1)
                    sample_panel(ph, 21, [("a", 2, xT, every)])
                    pool_products(ph, 0)
                    pool_products(ph, 1)
                    count(ph)
                else:
                    chunk(ph, o + 2, 0, "a", 0, xT, every, n2)
                    if ph.pro:
                        pe.wait_ge(dve_setup, 1)
                    if ph.nt:
                        router(ph, ph.nt - 1)
                    chunk(ph, o + 2, 1, "a", 1, xT, every, n2)
                    chunk(ph, o + 3, 0, "a", 2, xT, every, n2)
                    pool_products(ph, 0)
                    chunk(ph, o + 3, 1, "a", 3, xT, every, n2)
                    pool_products(ph, 1)
                for t in range(ph.nt2):
                    spatial(ph, t)
                    if t == min(1, ph.nt2 - 1):
                        pool_products(ph, 2)
                pool_products(ph, 3)
            passes(pe, body)
            for c in range(2):
                pe.wait_ge(a_free[c], (N_USES + 1 - c) // 2)
                for m in range(4):
                    last = nc.tensor.transpose((bankA[0], bankA[1])[c][0:16, m * P:(m + 1) * P], hist[c][:, m, :],
                                               ident[:, :])
                last.then_inc(hist_full, 1)

        block_stack.close()


def phase_three(nc, v):
    sem, psum, ident, running, iota16 = (v[k] for k in ("sem", "psum", "ident", "running", "iota16"))
    blk_tab, hn_dram, slot_dram, h_dram = v["blk_tab"], v["hn_dram"], v["slot_dram"], v["h_dram"]
    raw_gu, gate_in, up_in = v["raw_gu"], v["gate_in"], v["up_in"]
    bankG, bankU, bankY = psum[0], psum[1:3], psum[3:5]
    bankX, bankH = psum[5:7], [psum[7], psum[0]]

    stack = ExitStack()
    with stack:
        sb = v["tiles"](stack)
        sb("place_of_raw_gate_up_and_gf", [P, 2 * KD * HALF + D])
        raw_d = sb("raw_d", [P, KH, D])
        gu = [sb("gu_hi", [P, 2 * KD, HALF], F32R), sb("gu_lo", [P, 2 * KD, HALF], F32R)]
        dn = [sb("dn_hi", [P, KH, D], F32R), sb("dn_lo", [P, KH, D], F32R)]
        x = sb("x_rows", [P, D])
        xT = [sb("ex_hi", [P, KD, P], F32R), sb("ex_lo", [P, KD, P], F32R)]
        sg = sb("sg", [P, HALF])
        hid = sb("hid", [P, HALF])
        hT = [sb("hT_hi", [P, KH, P], F32R), sb("hT_lo", [P, KH, P], F32R)]
        y = sb("y_rows", [P, D])
        slots = sb("slots", [P, NSLOT, 2], I32)
        idx = sb("idx", [P, 2], I32)
        idx_1 = sb("idx_1", [P, 2], I32)
        idx_2 = sb("idx_2", [P, 2], I32)
        idx_out = sb("idx_out", [P, 2], I32)
        spare = sb("spare", [P, 2])
        blk_f = sb("blk_f", [P, NE])
        blk_i = sb("blk_i", [P, NE], I32)
        sums = [sb("sums0", [P, NE]), sb("sums1", [P, NE])]

        passed_pool = sem("passed_pool3")
        tab_ok = sem("tab_ok")
        down_in = sem("down_in")
        spare_ok = sem("spare_ok")
        moved = sem("moved")
        e_hi, e_lo = sem("e_hi"), sem("e_lo")
        idx_ok, x_rows_in = sem("idx_ok"), sem("x_rows_in")
        x_tr = sem("x_tr")
        ex_hi, ex_lo = sem("ex_hi"), sem("ex_lo")
        g_done, u1_done, sg_ok, hid_ok = (sem(n) for n in ("g_done", "u1_done", "sg_ok", "hid_ok"))
        gu_done = sem("gu_done")
        th_done, hT_hi = sem("th_done"), sem("hT_hi")
        hT_lo = sem("hT_lo")
        y_done = sem("y_done")
        y_read = sem("y_read")
        y_out = sem("y_out")

        def experts(eng, per_expert, per_block, peel=False):
            with eng.Fori(0, NE) as e:
                lo = eng.value_load(blk_tab[0:1, bass.ds(e, 1)], min_val=0, max_val=MAXBLK - 1)
                hi = eng.value_load(blk_tab[0:1, bass.ds(e + NE, 1)], min_val=1, max_val=MAXBLK)
                per_expert(e, lo)
                if peel:
                    per_block(e, lo, lo, True)
                with eng.Fori(lo + 1 if peel else lo, hi) as j:
                    per_block(e, lo, j)

        with nc.Block() as block:

            @block.sync
            def _(sp):

                def load(e):
                    view = lambda w: w[0, bass.ds(e, 1), :, :].rearrange("a (k p) f -> p (a k) f", p=P)
                    sp.wait_ge(e_lo, SPLITS * e + (KD - SPLITS))
                    sp.dma_start(raw_gu[:, 0:KD, :], view(v["w_gate"])).then_inc(gate_in, 16)
                    sp.wait_ge(e_lo, SPLITS * e + (2 * KD - SPLITS))
                    sp.dma_start(raw_gu[:, KD:2 * KD, :], view(v["w_up"])).then_inc(up_in, 16)
                    sp.wait_ge(e_lo, SPLITS * e)
                    sp.dma_start(raw_d[:, :, :], view(v["w_down"])).then_inc(down_in, 16)
                sp.dma_start(v["gf"][:, :], v["g_final"].rearrange("(a n) -> a n", a=1).broadcast_to([P, D]))\
                    .then_inc(v["gf_in"], 16)
                sp.wait_ge(x_rows_in, 16)
                sp.dma_start(raw_d[:, :, :], v["w_down"][0, 0].rearrange("(k p) f -> p k f", p=P)).then_inc(down_in, 16)
                with sp.Fori(1, NE) as e:
                    load(e)

            @block.gpsimd
            def _(pool):
                pool.dma_start(slots[:, :, :], slot_dram.rearrange("(p n) o -> p n o", p=P)).then_inc(y_out, 16)
                nc.gpsimd.memset(spare[:, :], 0.0).then_inc(spare_ok, 1)
                for c in range(2):
                    nc.gpsimd.memset(y[:, c * HALF:(c + 1) * HALF], 0.0).then_inc(y_read, 1)
                for tile in (idx, idx_1):
                    nc.gpsimd.iota(tile[:, 0:1], pattern=[[0, 1]], base=SEQ + SAMPLE, channel_multiplier=1)\
                        .then_inc(spare_ok, 1)
                    nc.gpsimd.memset(tile[:, 1:2], 0).then_inc(spare_ok, 1)
                nc.gpsimd.memset(sg[:, :], 0.0).then_inc(x_tr, 1)
                pool.wait_ge(spare_ok, 5)
                pool.wait_ge(y_out, 16)
                pool.wait_ge(tab_ok, 1)

                def fetch_and_add(col, j):
                    wait_apart(pool, x_tr, j + 1, passed_pool)
                    nc.gpsimd.tensor_copy(idx_2[:, :], idx_1[:, :]).then_inc(moved, 1)
                    wait_apart(pool, moved, 3 * j + 1, passed_pool)
                    nc.gpsimd.tensor_copy(idx_1[:, :], idx[:, :]).then_inc(moved, 1)
                    wait_apart(pool, moved, 3 * j + 2, passed_pool)
                    if col is not None:
                        nc.gpsimd.tensor_copy(idx[:, :], slots[:, col, :].rearrange("p n o -> p (n o)"))\
                            .then_inc(idx_ok, 1)
                        wait_apart(pool, idx_ok, j + 1, passed_pool)
                        nc.gpsimd.indirect_dma_start(out=x[:, :], out_offset=None, in_=hn_dram,
                                                     in_offset=bass.IndirectOffsetOnAxis(ap=idx[:, 0:1], axis=0))\
                            .then_inc(x_rows_in, 16)
                    wait_apart(pool, y_out, 16 * j + 16, passed_pool)
                    nc.gpsimd.tensor_copy(idx_out[:, :], idx_2[:, :]).then_inc(moved, 1)
                    wait_apart(pool, moved, 3 * j + 3, passed_pool)
                    wait_apart(pool, y_read, 2 * j + 2, passed_pool)
                    nc.gpsimd.indirect_dma_start(out=h_dram, in_=y[:, :], in_offset=None, compute_op=ALU.add,
                                                 out_offset=bass.IndirectOffsetOnAxis(ap=idx_out[:, 0:1], axis=0))\
                        .then_inc(y_out, 16)

                def per_block(e, lo, j):
                    col = nc.s_assert_within(pool.snap(e * BPE + j - lo), 0, NSLOT - 1,
                                              skip_runtime_bounds_check_because="an expert has at most BPE blocks")
                    fetch_and_add(bass.ds(col, 1), j)
                experts(pool, lambda e, lo: None, per_block)
                total = pool.value_load(blk_tab[0:1, 2 * NE - 1:2 * NE], min_val=1, max_val=MAXBLK)
                fetch_and_add(slice(0, 1), total)
                fetch_and_add(None, total + 1)
                wait_apart(pool, y_out, 16 * total + 48, passed_pool)

            @block.scalar
            def _(act):
                act.wait_ge(spare_ok, 5)
                act.wait_ge(tab_ok, 1)

                def use_sigmoid_table(c):
                    nc.scalar.activation(spare[:, c:c + 1], spare[:, c:c + 1], ACT.Sigmoid)

                def rows_high(count, j2):
                    act.wait_ge(x_tr, count)
                    for c in range(2):
                        nc.scalar.activation(xT[0][:, 4 * c:4 * c + 4, :],
                                             bankX[c][:, :].rearrange("p (k i) -> p k i", k=4), ACT.Copy)\
                            .then_inc(ex_hi, 1)
                rows_high(2, None)

                def weigh(j):
                    act.wait_ge(y_done, j + 1)
                    act.wait_ge(moved, 3 * j + 6)
                    for c in range(2):
                        nc.scalar.activation(y[:, c * HALF:(c + 1) * HALF], bankY[c][:, :], ACT.Copy,
                                             scale=idx_out[:, 1:2].bitcast(F32)).then_inc(y_read, 1)

                def split(e, lo):
                    use_sigmoid_table(1)
                    act.wait_ge(gu_done, lo + 1)
                    act.wait_ge(gate_in, 16 * e + 16)
                    for k in range(1, 2 * KD):
                        if k == KD:
                            act.wait_ge(up_in, 16 * e + 16)
                        if k == KD + 6:
                            weigh(lo)
                        nc.scalar.activation(gu[0][:, k, :], raw_gu[:, k, :], ACT.Copy).then_inc(e_hi, 1)

                def per_block(e, lo, j, first=False):
                    def down(k):
                        if not first:
                            return
                        if k == 0:
                            act.wait_ge(down_in, 16 * e + 16)
                        nc.scalar.activation(dn[0][:, k, :], raw_d[:, k, :], ACT.Copy).then_inc(e_hi, 1)

                    if not first:
                        use_sigmoid_table(0)
                        weigh(j)
                    act.wait_ge(g_done, j + 1)
                    nc.scalar.activation(sg[:, :], bankG[:, :], ACT.Sigmoid).then_inc(sg_ok, 1)
                    down(0)
                    act.wait_ge(th_done, 2 * j + 1)
                    nc.scalar.activation(hT[0][:, 0:2, :], bankH[0][:, 0:2 * P].rearrange("p (k i) -> p k i", k=2),
                                         ACT.Copy).then_inc(hT_hi, 1)
                    down(1)
                    down(2)
                    if not first:
                        rows_high(j + 3, j)
                    act.wait_ge(th_done, 2 * j + 2)
                    nc.scalar.activation(hT[0][:, 2:4, :], bankH[1][:, 0:2 * P].rearrange("p (k i) -> p k i", k=2),
                                         ACT.Copy).then_inc(hT_hi, 1)
                    down(3)
                    if first:
                        rows_high(j + 3, j)
                experts(act, split, per_block, peel=True)
                total = act.value_load(blk_tab[0:1, 2 * NE - 1:2 * NE], min_val=1, max_val=MAXBLK)
                weigh(total)

            @block.vector
            def _(dve):
                tt, ts, stt = nc.vector.tensor_tensor, nc.vector.tensor_scalar, nc.vector.scalar_tensor_tensor
                copy = nc.vector.tensor_copy
                lo_half = lambda out, a, hi: tt(out, a, hi.bitcast(F32), ALU.subtract)

                for b in bankY:
                    last = nc.vector.memset(b[:, :], 0.0)
                last.then_inc(y_done, 1)
                ts(blk_i[:, :], running[:, :], float(P - 1), None, ALU.add)
                dve.drain()
                ts(blk_i[:, :], blk_i[:, :], 7, None, ALU.logical_shift_right)
                dve.drain()
                ts(blk_f[:, :], blk_i[:, :], float(MINBLK), None, ALU.max)
                dve.drain()
                src = blk_f
                for n, step in enumerate((1, 2, 4, 8)):
                    dst = sums[n % 2]
                    tt(dst[:, step:], src[:, step:], src[:, :NE - step], ALU.add)
                    copy(dst[:, :step], src[:, :step])
                    dve.drain()
                    src = dst
                copy(blk_tab[:, NE:2 * NE], src[:, :])
                tt(blk_f[:, :], src[:, :], blk_f[:, :], ALU.subtract)
                dve.drain()
                copy(blk_tab[:, 0:NE], blk_f[:, :]).then_inc(tab_ok, 1)
                nc.vector.memset(sums[0][:, 0:1], 0.0).then_inc(hT_lo, 1)
                nc.vector.memset(sums[0][:, 1:2], 0.0).then_inc(gu_done, 1)

                def rows_low(count):
                    for c in range(2):
                        dve.wait_ge(ex_hi, count + c)
                        lo_half(xT[1][:, 4 * c:4 * c + 4, :], bankX[c][:, :].rearrange("p (k i) -> p k i", k=4),
                                xT[0][:, 4 * c:4 * c + 4, :]).then_inc(ex_lo, 1)
                rows_low(1)

                def split(e, lo):
                    dve.wait_ge(gate_in, 16 * e + 16)
                    dve.wait_ge(gu_done, lo + 1)
                    copy(gu[0][:, 0, :], raw_gu[:, 0, :])
                    dve.drain()
                    for k in range(2 * KD):
                        if k:
                            dve.wait_ge(e_hi, SPLITS_ACT * e + k)
                        lo_half(gu[1][:, k, :], raw_gu[:, k, :], gu[0][:, k, :]).then_inc(e_lo, 1)

                def hidden_low(c):
                    lo_half(hT[1][:, 2 * c:2 * c + 2, :], bankH[c][:, 0:2 * P].rearrange("p (k i) -> p k i", k=2),
                            hT[0][:, 2 * c:2 * c + 2, :]).then_inc(hT_lo, 1)

                def per_block(e, lo, j, first=False):
                    def down(k):
                        if first:
                            dve.wait_ge(e_hi, SPLITS_ACT * e + 2 * KD + k)
                            lo_half(dn[1][:, k, :], raw_d[:, k, :], dn[0][:, k, :]).then_inc(e_lo, 1)

                    dve.wait_ge(sg_ok, j + 1)
                    tt(sg[:, :], bankG[:, :], sg[:, :], ALU.mult)
                    dve.drain()
                    dve.wait_ge(u1_done, j + 1)
                    tt(hid[:, 0:256], bankU[0][:, 0:256], sg[:, 0:256], ALU.mult).then_inc(hid_ok, 1)
                    down(0)
                    dve.wait_ge(hT_hi, 2 * j + 1)
                    hidden_low(0)
                    dve.wait_ge(gu_done, j + 2)
                    tt(hid[:, 256:512], bankU[1][:, 0:256], sg[:, 256:512], ALU.mult).then_inc(hid_ok, 1)
                    down(1)
                    down(2)
                    if not first:
                        rows_low(2 * j + 3)
                    dve.wait_ge(hT_hi, 2 * j + 2)
                    hidden_low(1)
                    down(3)
                    if first:
                        rows_low(2 * j + 3)
                experts(dve, split, per_block, peel=True)

            @block.tensor
            def _(pe):
                def rows_of_x(count):
                    pe.wait_ge(x_rows_in, count)
                    for c in range(2):
                        for k in range(4):
                            last = nc.tensor.transpose(bankX[c][:, k * P:(k + 1) * P],
                                                       x[:, (4 * c + k) * P:(4 * c + k + 1) * P], ident[:, :])
                    last.then_inc(x_tr, 1)

                pe.wait_ge(tab_ok, 1)
                rows_of_x(16)

                def accumulate(out, a, ka, w, kw, cols, n, total):
                    nc.tensor.matmul(out, a[0][:, ka, :], w[0][:, kw, cols], start=(n == 0), stop=False)
                    nc.tensor.matmul(out, a[0][:, ka, :], w[1][:, kw, cols], start=False, stop=False)
                    return nc.tensor.matmul(out, a[1][:, ka, :], w[0][:, kw, cols], start=False, stop=(n == total - 1))

                def hidden_transposed(c):
                    for k in range(2):
                        last = nc.tensor.transpose(bankH[c][:, k * P:(k + 1) * P],
                                                   hid[:, (2 * c + k) * P:(2 * c + k + 1) * P], ident[:, :])
                    last.then_inc(th_done, 1)

                def per_block(e, lo, j, first=False):
                    early = 5 if first else 0
                    up = lambda c, k: accumulate(bankU[c][:, 0:256], xT, k, gu, KD + k,
                                                 slice(c * 256, (c + 1) * 256), k, KD)
                    pe.wait_ge(ex_lo, 2 * j + 2)
                    pe.wait_ge(hT_lo, 2 * j + 1)
                    for k in range(KD):
                        pe.wait_ge(e_lo, SPLITS * e + k + 1)
                        last = accumulate(bankG[:, :], xT, k, gu, k, slice(0, HALF), k, KD)
                    last.then_inc(g_done, 1)
                    for k in range(KD):
                        pe.wait_ge(e_lo, SPLITS * e + KD + k + 1)
                        last = up(0, k)
                        if k < early:
                            up(1, k)
                    last.then_inc(u1_done, 1)
                    for k in range(early, KD):
                        last = up(1, k)
                        if k == (6 if first else 4):
                            pe.wait_ge(hid_ok, 2 * j + 1)
                            hidden_transposed(0)
                    last.then_inc(gu_done, 1)
                    rows_of_x(16 * j + 32)
                    pe.wait_ge(y_read, 2 * j + 4)
                    pe.wait_ge(hT_lo, 2 * j + 2)
                    for k in range(KH):
                        pe.wait_ge(e_lo, SPLITS * e + 2 * KD + k + 1)
                        if k == 2:
                            pe.wait_ge(hT_lo, 2 * j + 3)
                        for half in range(2):
                            last = accumulate(bankY[half][:, :], hT, k, dn, k, slice(half * HALF, (half + 1) * HALF),
                                              k, KH)
                        if k == 0:
                            pe.wait_ge(hid_ok, 2 * j + 2)
                            hidden_transposed(1)
                    last.then_inc(y_done, 1)
                experts(pe, lambda e, lo: None, per_block, peel=True)


def phase_four(nc, v):
    sem, h_dram, gf, gf_in = v["sem"], v["h_dram"], v["gf"], v["gf_in"]
    GROUPS = [(i * TPG * P, P, TPG) for i in range(NPROMPT)] + [(SEQ, SAMPLE, 1)]
    LAST = NPROMPT
    stack = ExitStack()
    with stack:
        sb = v["tiles"](stack)
        sb("place_of_gf", [P, 2 * KD * HALF + D])
        rows = [sb(f"final{i}", [P, tiles, D]) for i, (_, _, tiles) in enumerate(GROUPS)]
        out = sb("out", [P, NT, D])
        sq = sb("sq", [P, 2, D], BF16)
        ss = sb("ss4", [P, NT])
        ms = sb("ms4", [P, NT])
        rs = sb("rs4", [P, NT])
        half_neg = sb("half_neg4", [P, 1])
        ss_ok, ms_ok, root_ok, out_ok, half_ok = (
            sem(n) for n in ("ss_ok", "ms_ok", "root_ok", "out_ok", "half_ok"))
        h_in = [sem(f"h_in{i}") for i in range((NT + 1) // 2)]
        stored = sem("stored")
        tiles_of = [(i, first, r, t) for i, (first, r, tiles) in enumerate(GROUPS) for t in range(tiles)]

        def rows_view(a, first, r, tiles):
            return a[first:first + tiles * r, :].rearrange("(t p) d -> p t d", p=r)

        with nc.Block() as block:
            @block.sync
            def _(sp):
                for i, (first, r, tiles) in enumerate(GROUPS):
                    for t0 in range(0, tiles, 2):
                        n = min(2, tiles - t0)
                        sp.dma_start(rows[i][0:r, t0:t0 + n, :], rows_view(h_dram, first + t0 * r, r, n))\
                            .then_inc(h_in[(i * TPG + t0) // 2], 16)

            @block.gpsimd
            def _(pool):
                nc.gpsimd.memset(half_neg[:, :], -0.5).then_inc(half_ok, 1)
                pool.wait_ge(half_ok, 1)
                for n, (i, first, r, t) in enumerate(tiles_of):
                    pool.wait_ge(ms_ok, n + 1)
                    nc.gpsimd.tensor_tensor(rs[0:r, n:n + 1], ms[0:r, n:n + 1], half_neg[0:r, :], ALU.pow)\
                        .then_inc(root_ok, 1)

            def store(act, n):
                i, first, r, t = tiles_of[n]
                act.wait_ge(out_ok, n + 1)
                to = v["y_prompt"][0, first + t * P:first + (t + 1) * P, :] if i < LAST else v["y_sample"][0, :, :]
                act.dma_start(to, out[0:r, n, :]).then_inc(stored, 16)

            @block.scalar
            def _(act):
                for n, (i, first, r, t) in enumerate(tiles_of):
                    act.wait_ge(h_in[n // 2], 16)
                    if n >= 2:
                        act.wait_ge(ss_ok, n - 1)
                    nc.scalar.activation(sq[0:r, n % 2, :], rows[i][0:r, t, :], ACT.Square,
                                         accum_out=ss[0:r, n:n + 1]).then_inc(ss_ok, 1)
                    if n >= 2:
                        store(act, n - 2)
                store(act, NT - 2)
                store(act, NT - 1)
                act.wait_ge(stored, 16 * NT)

            @block.vector
            def _(dve):
                def scale(n):
                    i, first, r, t = tiles_of[n]
                    dve.wait_ge(root_ok, n + 1)
                    nc.vector.scalar_tensor_tensor(out[0:r, n, :], rows[i][0:r, t, :], rs[0:r, n:n + 1],
                                                   gf[0:r, :], ALU.mult, ALU.mult).then_inc(out_ok, 1)
                dve.wait_ge(gf_in, 16)
                for n, (i, first, r, t) in enumerate(tiles_of):
                    dve.wait_ge(ss_ok, n + 1)
                    nc.vector.tensor_scalar(ms[0:r, n:n + 1], ss[0:r, n:n + 1], 1.0 / D, EPS, ALU.mult, ALU.add)\
                        .then_inc(ms_ok, 1)
                    if n:
                        scale(n - 1)
                scale(NT - 1)


_INS = ["x_prompt", "x_sample", "state_pool", "g_mix", "w_in", "w_pool", "pool_scale", "g_v", "w_spatial",
        "b_spatial", "w_up_pool", "w_up_gmlp", "w_out", "g_ffn", "w_group", "b_group", "w_router", "b_router",
        "w_gate", "w_up", "w_down", "g_final"]
_OUTS = [(1, SEQ, D), (1, SAMPLE, D), (1, 1, HIST, HALF), (1, 1, HIST, HALF), (1, 1, SAMPLE, HALF)]


def kernel(**inputs):
    import numpy as np
    import concourse.bacc as bacc
    from concourse.bass_utils import run_bass_kernel_spmd

    nc = bacc.Bacc("TRN2", target_bir_lowering=False, num_devices=1)
    arrays, args = {}, []
    for name in _INS:
        a = np.ascontiguousarray(inputs[name])
        arrays[f"in_{name}"] = a
        args.append(nc.dram_tensor(f"in_{name}", a.shape, mybir.dt.from_np(a.dtype), kind="ExternalInput").ap())
    for i, shape in enumerate(_OUTS):
        args.append(nc.dram_tensor(f"out_{i}", shape, F32, kind="ExternalOutput").ap())
    build(nc, *args)
    r = run_bass_kernel_spmd(nc, [arrays], core_ids=[0])
    return tuple(r.results[0][f"out_{i}"] for i in range(len(_OUTS)))
```
